# Optimizing a Trainium2 kernel written in Bass

```python
import math
import jax
import jax.numpy as jnp
from jax import lax
import numpy as np
import jax, jax.numpy as jnp

D_MODEL = 1024
BATCH = 1
SEQ = 512
DEPTH = 2

N_MIXERS = 4
F32 = jnp.float32
ROPE_THETA = 10000.0
DEEPNORM_ALPHA = (2.0 * DEPTH) ** 0.25
DEEPNORM_BETA = (8.0 * DEPTH) ** -0.25
LN_EPS = 1e-5
NEG_INF = -1e30
D_FF = ((8 * D_MODEL + 3 * 256 - 1) // (3 * 256)) * 256

RWKV_HEAD_DIM = 64
RWKV_HEADS = D_MODEL // RWKV_HEAD_DIM
RWKV_LORA_DECAY = 64
RWKV_LORA_ICLR = 64
RWKV_LORA_GATE = 128
RWKV_GN_EPS = 64e-5
GDN_HEAD_DIM = 128
GDN_HEADS = D_MODEL // GDN_HEAD_DIM
GDN_CONV = 4
GDN_CHUNK = 64
GDN_QKV = 3 * GDN_HEADS * GDN_HEAD_DIM
GDN_PROJ = 4 * GDN_HEADS * GDN_HEAD_DIM + 2 * GDN_HEADS
DIFF_HEADS = 8
DIFF_HEAD_DIM = D_MODEL // (2 * DIFF_HEADS)
ATTN_Q_BLOCK = 128
SWA_HEAD_DIM = 64
SWA_Q_HEADS = D_MODEL // SWA_HEAD_DIM
SWA_KV_HEADS = SWA_Q_HEADS // 8
SWA_WINDOW = 128
SWA_QKV = (SWA_Q_HEADS + 2 * SWA_KV_HEADS) * SWA_HEAD_DIM


def _layer_norm(x, g, b):
    xf = x.astype(F32)
    mu = jnp.mean(xf, -1, keepdims=True)
    var = jnp.mean(jnp.square(xf - mu), -1, keepdims=True)
    return ((xf - mu) * lax.rsqrt(var + LN_EPS) * g + b).astype(x.dtype)

def _rms_norm(x, g, eps):
    xf = x.astype(F32)
    return xf * lax.rsqrt(jnp.mean(xf * xf, -1, keepdims=True) + eps) * g

def _l2norm(x, eps=1e-6):
    xf = x.astype(F32)
    return (xf * lax.rsqrt(jnp.sum(xf * xf, -1, keepdims=True) + eps)).astype(x.dtype)

def _rope(x, pos):
    d = x.shape[-1]
    inv = ROPE_THETA ** (-jnp.arange(0, d, 2, dtype=F32) / d)
    ang = pos.astype(F32)[:, None] * inv[None, :]
    cos = jnp.cos(ang)[None, :, None, :]
    sin = jnp.sin(ang)[None, :, None, :]
    x1, x2 = jnp.split(x.astype(F32), 2, axis=-1)
    return jnp.concatenate([x1 * cos - x2 * sin, x2 * cos + x1 * sin], -1).astype(x.dtype)

def _token_shift(x):
    return jnp.pad(x, ((0, 0), (1, 0), (0, 0)))[:, :-1]

def _causal_depthwise_conv(x, w):
    K, C = w.shape
    return lax.conv_general_dilated(x, w[:, None, :].astype(x.dtype), window_strides=(1,),
                                    padding=[(K - 1, 0)], dimension_numbers=('NWC', 'WIO', 'NWC'),
                                    feature_group_count=C)

def _rwkv7_mixer(u, mu, w_rkv, w0, w1, w2, a0, a1, a2, g1, g2, k_k, k_a, r_k, gn_g, gn_b, w_out):
    B, T, D = u.shape
    H, N = RWKV_HEADS, RWKV_HEAD_DIM
    xx = _token_shift(u) - u
    lerp = lambda i: u + xx * mu[i]
    r = lerp(0) @ w_rkv[0]
    k = lerp(1) @ w_rkv[1]
    v = lerp(2) @ w_rkv[2]
    w_log = -jax.nn.softplus(-(w0 + jnp.tanh(lerp(3) @ w1) @ w2)) - 0.5
    a = jax.nn.sigmoid(a0 + (lerp(4) @ a1) @ a2)
    g = jax.nn.sigmoid(lerp(5) @ g1) @ g2
    heads = lambda t: t.reshape(B, T, H, N)
    kk = _l2norm(heads(k * k_k))
    k = k * (1 + (a - 1) * k_a)
    r, k, v, a = heads(r), heads(k), heads(v), heads(a)
    decay = jnp.exp(-jnp.exp(heads(w_log).astype(F32)))
    tm = lambda t: jnp.moveaxis(t.astype(F32), 1, 0)

    def step(S, inp):
        r_t, k_t, v_t, w_t, a_t, b_t = inp
        sa = jnp.einsum('bhvk,bhk->bhv', S, a_t)
        S = S * w_t[:, :, None, :] + sa[..., None] * b_t[:, :, None, :] + v_t[..., None] * k_t[:, :, None, :]
        return S, jnp.einsum('bhvk,bhk->bhv', S, r_t)

    S0 = jnp.zeros((B, H, N, N), F32)
    _, y = lax.scan(step, S0, (tm(r), tm(k), tm(v), jnp.moveaxis(decay, 1, 0), tm(-kk), tm(kk * a)))
    y = jnp.moveaxis(y, 0, 1)
    mean = jnp.mean(y, -1, keepdims=True)
    var = jnp.mean(jnp.square(y - mean), -1, keepdims=True)
    y = ((y - mean) * lax.rsqrt(var + RWKV_GN_EPS)).reshape(B, T, D) * gn_g + gn_b
    bonus = jnp.sum((r * k * r_k).astype(F32), -1, keepdims=True) * v.astype(F32)
    y = (y + bonus.reshape(B, T, D)).astype(u.dtype)
    return (y * g) @ w_out

def _chunk_gated_delta_rule(q, k, v, g, beta):
    B, T, H, dk = q.shape
    dv = v.shape[-1]
    C = GDN_CHUNK
    n = T // C
    chunks = lambda t: jnp.moveaxis(t.astype(F32).reshape(B, n, C, H, -1), 3, 1)
    q, k, v = chunks(q), chunks(k), chunks(v)
    beta = chunks(beta[..., None])
    gc = jnp.cumsum(chunks(g[..., None])[..., 0], axis=-1)
    k_beta, v_beta = k * beta, v * beta
    idx = jnp.arange(C)
    causal = idx[:, None] >= idx[None, :]
    strict = idx[:, None] > idx[None, :]
    decay = jnp.exp(jnp.where(causal, gc[..., :, None] - gc[..., None, :], -jnp.inf))
    L = jnp.where(strict, jnp.einsum('bhnid,bhnjd->bhnij', k_beta, k) * decay, 0.0)
    eye = jnp.eye(C, dtype=F32)
    tinv = lax.linalg.triangular_solve(eye + L, jnp.broadcast_to(eye, L.shape), left_side=True, lower=True)
    u_c = tinv @ v_beta
    w_c = tinv @ (k_beta * jnp.exp(gc)[..., None])
    a_intra = jnp.where(causal, jnp.einsum('bhnid,bhnjd->bhnij', q, k) * decay, 0.0)
    q_dec = q * jnp.exp(gc)[..., None]
    k_dec = k * jnp.exp(gc[..., -1:] - gc)[..., None]
    g_last = jnp.exp(gc[..., -1])

    def step(S, inp):
        q_i, k_i, u_i, w_i, a_i, gl = inp
        v_new = u_i - w_i @ S
        o = q_i @ S + a_i @ v_new
        S = S * gl[..., None, None] + jnp.einsum('bhck,bhcv->bhkv', k_i, v_new)
        return S, o

    xs = tuple(jnp.moveaxis(t, 2, 0) for t in (q_dec, k_dec, u_c, w_c, a_intra, g_last))
    _, o = lax.scan(step, jnp.zeros((B, H, dk, dv), F32), xs)
    return jnp.transpose(o, (1, 0, 3, 2, 4)).reshape(B, T, H, dv)

def _gated_deltanet_mixer(u, w_in, conv_w, a_log, dt_bias, norm_g, w_out):
    B, T, _ = u.shape
    H, d = GDN_HEADS, GDN_HEAD_DIM
    hd = H * d
    proj = u @ w_in
    qkv = jax.nn.silu(_causal_depthwise_conv(proj[..., :3 * hd], conv_w))
    z = proj[..., 3 * hd:4 * hd].reshape(B, T, H, d)
    b_in = proj[..., 4 * hd:4 * hd + H]
    a_in = proj[..., 4 * hd + H:]
    q = _l2norm(qkv[..., :hd].reshape(B, T, H, d)) * d ** -0.5
    k = _l2norm(qkv[..., hd:2 * hd].reshape(B, T, H, d))
    v = qkv[..., 2 * hd:].reshape(B, T, H, d)
    beta = jax.nn.sigmoid(b_in.astype(F32))
    g = -jnp.exp(a_log.astype(F32)) * jax.nn.softplus(a_in.astype(F32) + dt_bias)
    o = _chunk_gated_delta_rule(q, k, v, g, beta)
    o = _rms_norm(o, norm_g, 1e-6) * jax.nn.silu(z.astype(F32))
    return o.reshape(B, T, hd).astype(u.dtype) @ w_out

def _diff_attention_mixer(u, pos, w_in, lam_p, subln_g, w_out, lam_init):
    B, T, D = u.shape
    H, d, Qb = DIFF_HEADS, DIFF_HEAD_DIM, ATTN_Q_BLOCK
    proj = u @ w_in
    q = _rope(proj[..., :D].reshape(B, T, 2 * H, d), pos) * d ** -0.5
    k = _rope(proj[..., D:2 * D].reshape(B, T, 2 * H, d), pos)
    v = proj[..., 2 * D:].reshape(B, T, H, 2 * d)
    lp = lam_p.astype(F32)
    lam = jnp.exp(jnp.sum(lp[0] * lp[1])) - jnp.exp(jnp.sum(lp[2] * lp[3])) + lam_init
    nb = T // Qb
    qb = jnp.moveaxis(q.reshape(B, nb, Qb, 2 * H, d), 1, 0)
    kf, vf = k.astype(F32), v.astype(F32)
    kpos = jnp.arange(T)

    def block(args):
        q_blk, i = args
        s = jnp.einsum('bqhd,bkhd->bhqk', q_blk.astype(F32), kf)
        qpos = i * Qb + jnp.arange(Qb)
        s = jnp.where(kpos[None, :] <= qpos[:, None], s, NEG_INF)
        p = jax.nn.softmax(s, axis=-1).reshape(B, H, 2, Qb, T)
        attn = p[:, :, 0] - lam * p[:, :, 1]
        return jnp.einsum('bhqk,bkhe->bqhe', attn, vf)

    o = lax.map(block, (qb, jnp.arange(nb)))
    o = jnp.moveaxis(o, 0, 1).reshape(B, T, H, 2 * d)
    o = _rms_norm(o, subln_g, 1e-5) * (1.0 - lam_init)
    return o.reshape(B, T, D).astype(u.dtype) @ w_out

def _swa_sink_mixer(u, pos, w_qkv, b_qkv, sinks, w_out, b_out):
    B, T, _ = u.shape
    Hq, Hkv, d, W = SWA_Q_HEADS, SWA_KV_HEADS, SWA_HEAD_DIM, SWA_WINDOW
    G = Hq // Hkv
    nb = T // W
    proj = u @ w_qkv + b_qkv
    q = _rope(proj[..., :Hq * d].reshape(B, T, Hq, d), pos) * d ** -0.5
    k = _rope(proj[..., Hq * d:(Hq + Hkv) * d].reshape(B, T, Hkv, d), pos)
    v = proj[..., (Hq + Hkv) * d:].reshape(B, T, Hkv, d)
    qb = q.astype(F32).reshape(B, nb, W, Hkv, G, d)

    def band(t):
        tb = t.astype(F32).reshape(B, nb, W, Hkv, d)
        prev = jnp.pad(tb, ((0, 0), (1, 0), (0, 0), (0, 0), (0, 0)))[:, :-1]
        return jnp.concatenate([prev, tb], axis=2)

    kb, vb = band(k), band(v)
    s = jnp.einsum('bnqhgd,bnkhd->bnhgqk', qb, kb)
    qi = jnp.arange(W)[:, None]
    kj = jnp.arange(2 * W)[None, :]
    rel = W + qi - kj
    in_window = (rel >= 0) & (rel < W)
    key_pos = jnp.arange(nb)[:, None] * W + jnp.arange(2 * W)[None, :] - W
    valid = in_window[None, :, :] & (key_pos >= 0)[:, None, :]
    s = jnp.where(valid[None, :, None, None], s, NEG_INF)
    sink = sinks.astype(F32).reshape(Hkv, G)[None, None, :, :, None, None]
    m = jnp.maximum(jnp.max(s, -1, keepdims=True), sink)
    p = jnp.exp(s - m)
    p = p / (jnp.sum(p, -1, keepdims=True) + jnp.exp(sink - m))
    o = jnp.einsum('bnhgqk,bnkhd->bnqhgd', p, vb).reshape(B, T, Hq * d)
    return o.astype(u.dtype) @ w_out + b_out

def _count(m):
    return len(range(m, DEPTH, N_MIXERS))

def first_inputs(seed: int = 0) -> dict:
    key = jax.random.key(seed)
    keys = iter(jax.random.split(key, 48))

    def nrm(shape, std):
        return jax.random.normal(next(keys), shape, F32) * std

    def unif(shape, lo, hi):
        return jax.random.uniform(next(keys), shape, F32, lo, hi)

    D = D_MODEL
    nA, nB, nC, nD = (_count(m) for m in range(N_MIXERS))
    beta = DEEPNORM_BETA
    gdn_hd = GDN_HEADS * GDN_HEAD_DIM
    swa_hd = SWA_Q_HEADS * SWA_HEAD_DIM
    dt = jnp.exp(unif((nB, GDN_HEADS), math.log(1e-3), math.log(1e-1)))
    return {
        'x': nrm((BATCH, SEQ, D), 1.0),
        'c': nrm((BATCH, D), 1.0),
        'ada_w': nrm((DEPTH, D, 6 * D), 0.1 * D ** -0.5),
        'ada_b': nrm((DEPTH, 6 * D), 0.02),
        'ln_g': 1.0 + nrm((DEPTH, 2, D), 0.02),
        'ln_b': nrm((DEPTH, 2, D), 0.02),
        'ffn_w_in': nrm((DEPTH, D, 2 * D_FF), D ** -0.5),
        'ffn_w_out': nrm((DEPTH, D_FF, D), beta * D_FF ** -0.5),
        'rwkv_mu': unif((nA, 6, D), 0.0, 1.0),
        'rwkv_w_rkv': nrm((nA, 3, D, D), D ** -0.5),
        'rwkv_w0': unif((nA, D), -6.0, 1.0),
        'rwkv_w1': nrm((nA, D, RWKV_LORA_DECAY), D ** -0.5),
        'rwkv_w2': nrm((nA, RWKV_LORA_DECAY, D), 0.5 * RWKV_LORA_DECAY ** -0.5),
        'rwkv_a0': nrm((nA, D), 0.1),
        'rwkv_a1': nrm((nA, D, RWKV_LORA_ICLR), D ** -0.5),
        'rwkv_a2': nrm((nA, RWKV_LORA_ICLR, D), 0.5 * RWKV_LORA_ICLR ** -0.5),
        'rwkv_g1': nrm((nA, D, RWKV_LORA_GATE), D ** -0.5),
        'rwkv_g2': nrm((nA, RWKV_LORA_GATE, D), RWKV_LORA_GATE ** -0.5),
        'rwkv_k_k': 1.0 + nrm((nA, D), 0.1),
        'rwkv_k_a': 1.0 + nrm((nA, D), 0.1),
        'rwkv_r_k': nrm((nA, RWKV_HEADS, RWKV_HEAD_DIM), 0.1),
        'rwkv_gn_g': 1.0 + nrm((nA, D), 0.02),
        'rwkv_gn_b': nrm((nA, D), 0.02),
        'rwkv_w_out': nrm((nA, D, D), beta * D ** -0.5),
        'gdn_w_in': nrm((nB, D, GDN_PROJ), D ** -0.5),
        'gdn_conv': nrm((nB, GDN_CONV, GDN_QKV), GDN_CONV ** -0.5),
        'gdn_a_log': jnp.log(unif((nB, GDN_HEADS), 1.0, 16.0)),
        'gdn_dt_bias': dt + jnp.log(-jnp.expm1(-dt)),
        'gdn_norm_g': 1.0 + nrm((nB, GDN_HEAD_DIM), 0.02),
        'gdn_w_out': nrm((nB, gdn_hd, D), beta * gdn_hd ** -0.5),
        'diff_w_in': nrm((nC, D, 3 * D), D ** -0.5),
        'diff_lambda': nrm((nC, 4, DIFF_HEAD_DIM), 0.1),
        'diff_subln_g': 1.0 + nrm((nC, 2 * DIFF_HEAD_DIM), 0.02),
        'diff_w_out': nrm((nC, D, D), beta * D ** -0.5),
        'swa_w_qkv': nrm((nD, D, SWA_QKV), D ** -0.5),
        'swa_b_qkv': nrm((nD, SWA_QKV), 0.02),
        'swa_sinks': nrm((nD, SWA_Q_HEADS), 1.0),
        'swa_w_out': nrm((nD, swa_hd, D), beta * swa_hd ** -0.5),
        'swa_b_out': nrm((nD, D), 0.02),
    }

def first_block(x, c, ada_w, ada_b, ln_g, ln_b, ffn_w_in, ffn_w_out,
              rwkv_mu, rwkv_w_rkv, rwkv_w0, rwkv_w1, rwkv_w2, rwkv_a0, rwkv_a1, rwkv_a2,
              rwkv_g1, rwkv_g2, rwkv_k_k, rwkv_k_a, rwkv_r_k, rwkv_gn_g, rwkv_gn_b, rwkv_w_out,
              gdn_w_in, gdn_conv, gdn_a_log, gdn_dt_bias, gdn_norm_g, gdn_w_out,
              diff_w_in, diff_lambda, diff_subln_g, diff_w_out,
              swa_w_qkv, swa_b_qkv, swa_sinks, swa_w_out, swa_b_out):
    T = x.shape[1]
    pos = jnp.arange(T)
    cond = jax.nn.silu(c)
    for i in range(DEPTH):
        mod = (cond @ ada_w[i] + ada_b[i])[:, None, :]
        sh1, sc1, ga1, sh2, sc2, ga2 = jnp.split(mod, 6, axis=-1)
        u = x * (1 + sc1) + sh1
        m, j = i % N_MIXERS, i // N_MIXERS
        if m == 0:
            y = _rwkv7_mixer(u, rwkv_mu[j], rwkv_w_rkv[j], rwkv_w0[j], rwkv_w1[j], rwkv_w2[j],
                             rwkv_a0[j], rwkv_a1[j], rwkv_a2[j], rwkv_g1[j], rwkv_g2[j],
                             rwkv_k_k[j], rwkv_k_a[j], rwkv_r_k[j], rwkv_gn_g[j], rwkv_gn_b[j],
                             rwkv_w_out[j])
        elif m == 1:
            y = _gated_deltanet_mixer(u, gdn_w_in[j], gdn_conv[j], gdn_a_log[j], gdn_dt_bias[j],
                                      gdn_norm_g[j], gdn_w_out[j])
        elif m == 2:
            lam_init = 0.8 - 0.6 * math.exp(-0.3 * i)
            y = _diff_attention_mixer(u, pos, diff_w_in[j], diff_lambda[j], diff_subln_g[j],
                                      diff_w_out[j], lam_init)
        else:
            y = _swa_sink_mixer(u, pos, swa_w_qkv[j], swa_b_qkv[j], swa_sinks[j], swa_w_out[j],
                                swa_b_out[j])
        x = _layer_norm(DEEPNORM_ALPHA * x + (1 + ga1) * y, ln_g[i, 0], ln_b[i, 0])
        u = x * (1 + sc2) + sh2
        gate, up = jnp.split(u @ ffn_w_in[i], 2, axis=-1)
        y = (jax.nn.silu(gate) * up) @ ffn_w_out[i]
        x = _layer_norm(DEEPNORM_ALPHA * x + (1 + ga2) * y, ln_g[i, 1], ln_b[i, 1])
    return x


D_MIX = D_MODEL
MLA_HEADS = 4
MLA_NOPE = 128
MLA_ROPE = 64
MLA_V = 128
Q_LORA = 384
KV_LORA = 256
ROPE_BASE = 10000.0
Q_BLOCK = 128
MLA_W = MLA_HEADS * MLA_V
POOL_WINDOWS = (2, 4, 8, 16)
POOL_GROUPS = 4
POOL_CH = 64
POOL_W = POOL_GROUPS * POOL_CH
M_HEADS = 4
M_HEAD_DIM = 64
M_W = M_HEADS * M_HEAD_DIM
M_CONV = 4
M_CHUNK = 64
D_FF_2 = 2816
FFN_CONV = 3
RMS_EPS = 1e-6
ALPHA = (2 * DEPTH) ** 0.25
BETA = (8 * DEPTH) ** -0.25

IN_SIZES = (Q_LORA, KV_LORA, MLA_ROPE, POOL_W, M_W, M_W, M_W, M_HEADS, M_HEADS)
D_IN = Q_LORA + KV_LORA + MLA_ROPE + POOL_W + 3 * M_W + 2 * M_HEADS


def _split_points():
    return [int(v) for v in np.cumsum(np.array(IN_SIZES))[:-1]]

def layer_norm(x, g, b):
    xf = x.astype(jnp.float32)
    mu = jnp.mean(xf, axis=-1, keepdims=True)
    var = jnp.mean(jnp.square(xf - mu), axis=-1, keepdims=True)
    y = (xf - mu) * lax.rsqrt(var + LN_EPS) * g + b
    return y.astype(x.dtype)

def rms_norm(x, g):
    xf = x.astype(jnp.float32)
    y = xf * lax.rsqrt(jnp.mean(jnp.square(xf), axis=-1, keepdims=True) + RMS_EPS) * g
    return y.astype(x.dtype)

def rotary_tables(seq, dim):
    inv = 1.0 / (ROPE_BASE ** (jnp.arange(0, dim, 2, dtype=jnp.float32) / dim))
    ang = jnp.arange(seq, dtype=jnp.float32)[:, None] * inv[None, :]
    return jnp.cos(ang), jnp.sin(ang)

def apply_rotary(x, cos, sin):
    xf = x.astype(jnp.float32)
    half = xf.shape[-1] // 2
    x1, x2 = xf[..., :half], xf[..., half:]
    return jnp.concatenate([x1 * cos - x2 * sin, x2 * cos + x1 * sin], axis=-1).astype(x.dtype)

def causal_dwconv(x, w, b):
    k = w.shape[0]
    y = lax.conv_general_dilated(
        x, w[:, None, :], window_strides=(1,), padding=((k - 1, 0),),
        dimension_numbers=("NWC", "WIO", "NWC"), feature_group_count=x.shape[-1])
    return y + b

def mla(cq, ckv, kr, g_qn, w_uq, g_kvn, w_ukv, cos, sin):
    B, S, _ = cq.shape
    H = MLA_HEADS
    q = (rms_norm(cq, g_qn) @ w_uq).reshape(B, S, H, MLA_NOPE + MLA_ROPE)
    q_nope, q_pe = q[..., :MLA_NOPE], q[..., MLA_NOPE:]
    q_pe = apply_rotary(q_pe, cos[:, None, :], sin[:, None, :])
    kv = (rms_norm(ckv, g_kvn) @ w_ukv).reshape(B, S, H, MLA_NOPE + MLA_V)
    k_nope, v = kv[..., :MLA_NOPE], kv[..., MLA_NOPE:]
    k_pe = apply_rotary(kr, cos, sin)
    scale = (MLA_NOPE + MLA_ROPE) ** -0.5
    nb = S // Q_BLOCK
    qn_b = (q_nope * scale).reshape(B, nb, Q_BLOCK, H, MLA_NOPE).transpose(1, 0, 3, 2, 4)
    qp_b = (q_pe * scale).reshape(B, nb, Q_BLOCK, H, MLA_ROPE).transpose(1, 0, 3, 2, 4)
    k_nope_t = k_nope.transpose(0, 2, 1, 3)
    v_t = v.transpose(0, 2, 1, 3)
    key_pos = jnp.arange(S)

    def block(args):
        qn, qp, start = args
        s = (jnp.einsum("bhqd,bhkd->bhqk", qn, k_nope_t)
             + jnp.einsum("bhqd,bkd->bhqk", qp, k_pe)).astype(jnp.float32)
        q_pos = start + jnp.arange(Q_BLOCK)
        s = jnp.where(key_pos[None, :] <= q_pos[:, None], s, -jnp.inf)
        p = jax.nn.softmax(s, axis=-1).astype(v_t.dtype)
        return jnp.einsum("bhqk,bhkd->bhqd", p, v_t)

    o = lax.map(block, (qn_b, qp_b, jnp.arange(nb) * Q_BLOCK))
    return o.transpose(1, 0, 3, 2, 4).reshape(B, S, H * MLA_V).astype(cq.dtype)

def multiscale_pool(p, w_pool, s_pool):
    B, S, _ = p.shape
    G, C = POOL_GROUPS, POOL_CH
    pg = p.reshape(B, S, G, C).astype(jnp.float32)
    cs = jnp.concatenate([jnp.zeros((B, 1, G, C), jnp.float32), jnp.cumsum(pg, axis=1)], axis=1)
    t = jnp.arange(S)
    win = jnp.array(POOL_WINDOWS, dtype=jnp.int32)
    lo = jnp.maximum(t[:, None] + 1 - win[None, :], 0)
    window_sum = cs[:, 1:] - cs[:, lo, jnp.arange(G)[None, :]]
    count = (t[:, None] + 1 - lo).astype(jnp.float32)
    y = (window_sum / count[None, :, :, None] - pg).astype(p.dtype)
    y = jnp.einsum("bsgc,gcd->bsgd", y, w_pool) * s_pool.reshape(G, C)
    return y.reshape(B, S, G * C).astype(p.dtype)

def mlstm(xqk, xv, xo, ipre, fpre, w_mconv, b_mconv, w_mq, w_mk, b_i, b_f, g_mh):
    B, S, _ = xqk.shape
    H, Dh, L = M_HEADS, M_HEAD_DIM, M_CHUNK
    nc = S // L
    c = jax.nn.silu(causal_dwconv(xqk, w_mconv, b_mconv)).reshape(B, S, H, Dh)
    q = jnp.einsum("bshd,hde->bshe", c, w_mq).astype(jnp.float32)
    k = (jnp.einsum("bshd,hde->bshe", c, w_mk) * (Dh ** -0.5)).astype(jnp.float32)
    v = xv.reshape(B, S, H, Dh).astype(jnp.float32)
    log_i = (ipre + b_i).astype(jnp.float32)
    log_f = jax.nn.log_sigmoid((fpre + b_f).astype(jnp.float32))

    def to_chunks4(a):
        return a.reshape(B, nc, L, H, Dh).transpose(1, 0, 3, 2, 4)

    def to_chunks3(a):
        return a.reshape(B, nc, L, H).transpose(1, 0, 3, 2)

    tri = jnp.tril(jnp.ones((L, L), dtype=bool))

    def step(carry, inp):
        Cm, n, m = carry
        qc, kc, vc, li, lf = inp
        b = jnp.cumsum(lf, axis=-1)
        D = jnp.where(tri, b[..., :, None] - b[..., None, :] + li[..., None, :], -jnp.inf)
        inter = b + m[..., None]
        m_t = jnp.maximum(inter, jnp.max(D, axis=-1))
        g = jnp.exp(inter - m_t)
        sc = jnp.einsum("bhtd,bhsd->bhts", qc, kc) * jnp.exp(D - m_t[..., None])
        num = g[..., None] * jnp.einsum("bhtd,bhde->bhte", qc, Cm) + jnp.einsum("bhts,bhse->bhte", sc, vc)
        den = g * jnp.einsum("bhtd,bhd->bht", qc, n) + jnp.sum(sc, axis=-1)
        h = num / jnp.maximum(jnp.abs(den), jnp.exp(-m_t))[..., None]
        bL = b[..., -1]
        w_log = bL[..., None] - b + li
        m_new = jnp.maximum(bL + m, jnp.max(w_log, axis=-1))
        w = jnp.exp(w_log - m_new[..., None])
        decay = jnp.exp(bL + m - m_new)
        C_new = decay[..., None, None] * Cm + jnp.einsum("bhs,bhsd,bhse->bhde", w, kc, vc)
        n_new = decay[..., None] * n + jnp.einsum("bhs,bhsd->bhd", w, kc)
        return (C_new, n_new, m_new), h

    init = (jnp.zeros((B, H, Dh, Dh), jnp.float32), jnp.zeros((B, H, Dh), jnp.float32),
            jnp.zeros((B, H), jnp.float32))
    _, hs = lax.scan(step, init, (to_chunks4(q), to_chunks4(k), to_chunks4(v),
                                  to_chunks3(log_i), to_chunks3(log_f)))
    h = hs.transpose(1, 0, 3, 2, 4).reshape(B, S, H, Dh)
    mu = jnp.mean(h, axis=-1, keepdims=True)
    var = jnp.mean(jnp.square(h - mu), axis=-1, keepdims=True)
    h = (h - mu) * lax.rsqrt(var + LN_EPS) * g_mh.reshape(H, Dh)
    out = jax.nn.sigmoid(xo.astype(jnp.float32)).reshape(B, S, H, Dh) * h
    return out.reshape(B, S, M_W).astype(xqk.dtype)

def conv_glu_ffn(x, w_up, w_fconv, b_fconv, w_down):
    a, g = jnp.split(x @ w_up, 2, axis=-1)
    g = causal_dwconv(g, w_fconv, b_fconv)
    return (jax.nn.silu(g) * a) @ w_down

def second_inputs(seed: int = 0) -> dict:
    key = jax.random.key(seed)
    ks = jax.random.split(key, 32)
    f32 = jnp.float32

    def nrm(k, shape, scale):
        return jax.random.normal(k, shape, f32) * scale

    def gain(k, shape):
        return 1.0 + 0.02 * jax.random.normal(k, shape, f32)

    L = DEPTH
    return {
        "x": nrm(ks[0], (BATCH, SEQ, D_MODEL), 1.0),
        "ln0_g": gain(ks[1], (D_MODEL,)),
        "ln0_b": nrm(ks[2], (D_MODEL,), 0.02),
        "w_in": nrm(ks[3], (L, D_MODEL, D_IN), D_MODEL ** -0.5),
        "g_qn": gain(ks[4], (L, Q_LORA)),
        "w_uq": nrm(ks[5], (L, Q_LORA, MLA_HEADS * (MLA_NOPE + MLA_ROPE)), Q_LORA ** -0.5),
        "g_kvn": gain(ks[6], (L, KV_LORA)),
        "w_ukv": nrm(ks[7], (L, KV_LORA, MLA_HEADS * (MLA_NOPE + MLA_V)), KV_LORA ** -0.5),
        "w_pool": nrm(ks[8], (L, POOL_GROUPS, POOL_CH, POOL_CH), POOL_CH ** -0.5),
        "s_pool": gain(ks[9], (L, POOL_W)),
        "w_mconv": nrm(ks[10], (L, M_CONV, M_W), M_CONV ** -0.5),
        "b_mconv": nrm(ks[11], (L, M_W), 0.02),
        "w_mq": nrm(ks[12], (L, M_HEADS, M_HEAD_DIM, M_HEAD_DIM), M_HEAD_DIM ** -0.5),
        "w_mk": nrm(ks[13], (L, M_HEADS, M_HEAD_DIM, M_HEAD_DIM), M_HEAD_DIM ** -0.5),
        "b_i": nrm(ks[14], (L, M_HEADS), 0.1),
        "b_f": jnp.linspace(3.0, 6.0, M_HEADS, dtype=f32)[None, :] + nrm(ks[15], (L, M_HEADS), 0.1),
        "g_mh": gain(ks[16], (L, M_W)),
        "w_out": nrm(ks[17], (L, D_MIX, D_MODEL), BETA * D_MIX ** -0.5),
        "ln1_g": gain(ks[18], (L, D_MODEL)),
        "ln1_b": nrm(ks[19], (L, D_MODEL), 0.02),
        "w_up": nrm(ks[20], (L, D_MODEL, 2 * D_FF_2), D_MODEL ** -0.5),
        "w_fconv": nrm(ks[21], (L, FFN_CONV, D_FF_2), FFN_CONV ** -0.5),
        "b_fconv": nrm(ks[22], (L, D_FF_2), 0.02),
        "w_down": nrm(ks[23], (L, D_FF_2, D_MODEL), BETA * D_FF_2 ** -0.5),
        "ln2_g": gain(ks[24], (L, D_MODEL)),
        "ln2_b": nrm(ks[25], (L, D_MODEL), 0.02),
    }

def second_block(x, ln0_g, ln0_b, w_in, g_qn, w_uq, g_kvn, w_ukv, w_pool, s_pool, w_mconv,
              b_mconv, w_mq, w_mk, b_i, b_f, g_mh, w_out, ln1_g, ln1_b, w_up, w_fconv,
              b_fconv, w_down, ln2_g, ln2_b):
    S = x.shape[1]
    cos, sin = rotary_tables(S, MLA_ROPE)
    h = layer_norm(x, ln0_g, ln0_b)
    for l in range(DEPTH):
        proj = h @ w_in[l]
        cq, ckv, kr, xp, xqk, xv, xo, ipre, fpre = jnp.split(proj, _split_points(), axis=-1)
        a = mla(cq, ckv, kr, g_qn[l], w_uq[l], g_kvn[l], w_ukv[l], cos, sin)
        p = multiscale_pool(xp, w_pool[l], s_pool[l])
        m = mlstm(xqk, xv, xo, ipre, fpre, w_mconv[l], b_mconv[l], w_mq[l], w_mk[l],
                  b_i[l], b_f[l], g_mh[l])
        mix = jnp.concatenate([a.astype(h.dtype), p.astype(h.dtype), m.astype(h.dtype)], axis=-1) @ w_out[l]
        h = layer_norm(ALPHA * h + mix, ln1_g[l], ln1_b[l])
        f = conv_glu_ffn(h, w_up[l], w_fconv[l], b_fconv[l], w_down[l])
        h = layer_norm(ALPHA * h + f, ln2_g[l], ln2_b[l])
    return h


def setup_inputs(seed=0):
    out = dict(first_inputs(seed))
    for name, value in second_inputs(seed + 1).items():
        if name != "x":
            out[name + "_2"] = value
    return out


def reference(
    x, c, ada_w, ada_b, ln_g, ln_b, ffn_w_in, ffn_w_out, rwkv_mu, rwkv_w_rkv, rwkv_w0, rwkv_w1,
    rwkv_w2, rwkv_a0, rwkv_a1, rwkv_a2, rwkv_g1, rwkv_g2, rwkv_k_k, rwkv_k_a, rwkv_r_k,
    rwkv_gn_g, rwkv_gn_b, rwkv_w_out, gdn_w_in, gdn_conv, gdn_a_log, gdn_dt_bias, gdn_norm_g,
    gdn_w_out, diff_w_in, diff_lambda, diff_subln_g, diff_w_out, swa_w_qkv, swa_b_qkv,
    swa_sinks, swa_w_out, swa_b_out, ln0_g_2, ln0_b_2, w_in_2, g_qn_2, w_uq_2, g_kvn_2, w_ukv_2,
    w_pool_2, s_pool_2, w_mconv_2, b_mconv_2, w_mq_2, w_mk_2, b_i_2, b_f_2, g_mh_2, w_out_2,
    ln1_g_2, ln1_b_2, w_up_2, w_fconv_2, b_fconv_2, w_down_2, ln2_g_2, ln2_b_2,
):
    x = first_block(
        x, c, ada_w, ada_b, ln_g, ln_b, ffn_w_in, ffn_w_out, rwkv_mu, rwkv_w_rkv, rwkv_w0,
        rwkv_w1, rwkv_w2, rwkv_a0, rwkv_a1, rwkv_a2, rwkv_g1, rwkv_g2, rwkv_k_k, rwkv_k_a,
        rwkv_r_k, rwkv_gn_g, rwkv_gn_b, rwkv_w_out, gdn_w_in, gdn_conv, gdn_a_log, gdn_dt_bias,
        gdn_norm_g, gdn_w_out, diff_w_in, diff_lambda, diff_subln_g, diff_w_out, swa_w_qkv,
        swa_b_qkv, swa_sinks, swa_w_out, swa_b_out,
    )
    return second_block(
        x, ln0_g_2, ln0_b_2, w_in_2, g_qn_2, w_uq_2, g_kvn_2, w_ukv_2, w_pool_2, s_pool_2,
        w_mconv_2, b_mconv_2, w_mq_2, w_mk_2, b_i_2, b_f_2, g_mh_2, w_out_2, ln1_g_2, ln1_b_2,
        w_up_2, w_fconv_2, b_fconv_2, w_down_2, ln2_g_2, ln2_b_2,
    )


_drawn_inputs = setup_inputs


def setup_inputs(seed=0):
    import zlib

    import numpy as np

    out = dict(_drawn_inputs(seed))
    spreads = {}
    factors = {'rwkv_w1': 8.0,
     'rwkv_w2': 8.0,
     'rwkv_a0': 6.042,
     'rwkv_k_k': 3.654,
     'rwkv_gn_g': 8.0,
     'rwkv_gn_b': 8.0,
     'gdn_norm_g': 8.0,
     'g_qn_2': 8.0,
     'g_kvn_2': 8.0,
     's_pool_2': 8.0,
     'b_mconv_2': 8.0,
     'b_i_2': 41.834,
     'g_mh_2': 8.0,
     'b_fconv_2': 8.0}
    for name, (base, spread) in spreads.items():
        noise = np.random.default_rng([zlib.crc32(name.encode()), seed]).standard_normal(out[name].shape)
        drawn = base * np.exp(spread * noise) if base else spread * noise
        out[name] = jnp.asarray(drawn.astype(out[name].dtype))
    for name, factor in factors.items():
        out[name] = (out[name] * factor).astype(out[name].dtype)
    return out
```

```python
from contextlib import ExitStack

import concourse.bass as bass
import numpy as np
from concourse import mybir

F32 = mybir.dt.float32
U32 = mybir.dt.uint32
ALU = mybir.AluOpType
ACT = mybir.ActivationFunctionType
AX_X = mybir.AxisListType.X
ds = bass.ds

P = 128
T = 512
D = 1024
KD = D // P
FF = 2816
KF = FF // P
C = 128
NC = T // C
ALPHA = 4.0 ** 0.25
LN_EPS = 1e-5
LEVELS = (2, 4, 8, 16, 32, 64)


def constants():
    i = np.arange(P)[:, None]
    j = np.arange(P)[None, :]
    parts = {
        "ident": np.eye(P),
        "ones": np.ones((P, P)),
        "head64": (i // 64 == j // 64) * 1.0,
        "upper": (i < j) * 1.0,
        "upto": (i <= j) * 1.0,
        "corner1": ((j % 2 == 1) & (i == j - 1)) * 1.0,
    }
    for b in LEVELS:
        parts[f"corner{b}"] = (((i // b) % 2 == 1) & (j // b == i // b - 1)) * 1.0
    parts["heads16"] = np.concatenate(
        [np.stack([(np.arange(P) // 64 + 2 * p == h) for h in range(16)], 1) for p in range(8)], 1) * 1.0
    spread16 = np.zeros((P, 8 * P))
    for p in range(8):
        for m in range(P):
            spread16[2 * p + m // 64, p * P + m] = 1.0
    parts["spread16"] = spread16
    spread8 = np.zeros((P, 8 * P))
    for h in range(8):
        spread8[h, h * P:(h + 1) * P] = 1.0
    parts["spread8"] = spread8
    parts["pick8"] = np.broadcast_to((np.arange(15) == 7) * 1.0, (P, 15))
    parts["carry"] = np.broadcast_to((np.arange(T) % C != 0) * 1.0, (P, T))
    inv = 1.0 / (10000.0 ** (np.arange(0, 64, 2, dtype=np.float32) / np.float32(64)))
    angle = np.arange(T, dtype=np.float32)[:, None] * inv.astype(np.float32)[None, :]
    parts["cos"] = np.tile(np.cos(angle).T, (4, 1))
    parts["sin"] = np.tile(np.sin(angle).T, (4, 1))
    turn = np.zeros((P, P))
    for m in range(P):
        turn[m + 32 if m % 64 < 32 else m - 32, m] = -1.0 if m % 64 < 32 else 1.0
    parts["turn"] = turn
    t = np.arange(T)
    for g in range(2):
        w = np.where(np.arange(P) < 64, 2 ** (2 * g + 1), 2 ** (2 * g + 2))[:, None]
        parts[f"count{g}"] = 1.0 / np.minimum(t[None, :] + 1, w)
    parts["later"] = (j > i) * -1e30
    at, where = 0, {}
    for name, a in parts.items():
        where[name] = (at, a.shape[1])
        at += a.shape[1]
    return np.concatenate([a.astype(np.float32) for a in parts.values()], 1), where


CONST, CONST_AT = constants()


class Core:

    def __init__(self, nc, ctx, const):
        self.nc, self.ctx, self.const_dram = nc, ctx, const
        self.x = self.sb("x", [P, KD, T])
        self.area = self.sb("area", [P, 10, KD * T])
        self.const_sb = self.sb("const", [P, CONST_KEPT])
        self.cols = self.sb("cols", [P, 470])
        self.mod = self.sb("mod", [P, 2, 48])
        self.stats = self.sb("stats", [P, 2, T])
        self.ps = ctx.enter_context(nc.psum_tensor("ps", [P, 8, 512], F32))
        self.col_at = {}
        self.n_cols = 0
        self.used = []
        self.older = []
        self.count = 0

    def sb(self, name, shape, dt=F32):
        return self.ctx.enter_context(self.nc.sbuf_tensor(name, shape, dt))

    def slot(self, n, *dims):
        size = 1
        for d in dims:
            size *= d
        flat = self.area[:].rearrange("p s n -> p (s n)")[:, n * KD * T:n * KD * T + size]
        if len(dims) == 1:
            return flat
        names = "abcd"[:len(dims)]
        return flat.rearrange(f"p ({' '.join(names)}) -> p {' '.join(names)}",
                              **{k: v for k, v in zip(names, dims)})

    def const(self, name, rows=P):
        at, n = CONST_AT[name]
        return self.const_sb[0:rows, at:at + n]

    def col(self, name, k=0, n=1):
        at = self.col_at[name] + k
        return self.cols[:, at:at + n]

    def semaphores(self, *names):
        self.count += 1
        for s in self.older:
            self.nc.release_semaphore(s)
        self.older, self.used = self.used, [self.nc.alloc_semaphore(f"{n}_{self.count}") for n in names]
        return self.used

    def clear_before(self, sp):
        for s in self.older:
            sp.sem_clear(s)

    def clear_all(self):
        self.semaphores()
        with self.nc.Block() as block:
            @block.sync
            def _(sp):
                self.clear_before(sp)


CONST_KEPT = CONST_AT["cos"][0]


def turn_rows(core, loads, groups, extra_loads=(), clear=True):
    nc = core.nc
    rows = core.slot(8, len(groups), P)
    loaded, turned, copied = core.semaphores("rows_loaded", "rows_turned", "columns_copied")
    plan = []
    for g, group in enumerate(groups):
        at = 0
        first = core.n_cols
        for name, view in group:
            n = view.shape[0]
            core.col_at[name] = first + at
            plan.append((g, at, n, view))
            at += n
        core.n_cols += at
        groups[g] = (first, at)
    with nc.Block() as block:
        @block.sync
        def _(sp):
            core.clear_before(sp)
            for dst, src in loads:
                sp.dma_start(dst, src).then_inc(loaded, 16)
            for g, at, n, view in plan:
                sp.dma_start(rows[at:at + n, g, :], view).then_inc(loaded, 16)

        @block.tensor
        def _(pe):
            pe.wait_ge(loaded, 16 * (len(plan) + len(loads)))
            for g, (first, n) in enumerate(groups):
                if g >= 2:
                    pe.wait_ge(copied, g - 1)
                nc.tensor.transpose(core.ps[:, g % 2, 0:n], rows[0:n, g, :],
                                    core.const("ident", n)[:, 0:n]).then_inc(turned, 1)

        @block.vector
        def _(dve):
            for g, (first, n) in enumerate(groups):
                dve.wait_ge(turned, g + 1)
                nc.vector.tensor_copy(core.cols[:, first:first + n], core.ps[:, g % 2, 0:n]).then_inc(copied, 1)


def load_x(core, x_dram):
    nc = core.nc
    rows = core.slot(0, 4, D)
    loaded, turned, copied = core.semaphores("x_loaded", "x_turned", "x_copied")
    with nc.Block() as block:
        @block.sync
        def _(sp):
            core.clear_before(sp)
            sp.dma_start(rows, x_dram.rearrange("o (a p) d -> p (o a) d", p=P)).then_inc(loaded, 16)

        @block.tensor
        def _(pe):
            pe.wait_ge(loaded, 16)
            for k in range(KD):
                if k >= 2:
                    pe.wait_ge(copied, k - 1)
                for a in range(4):
                    last = nc.tensor.transpose(core.ps[:, k % 2, a * P:(a + 1) * P],
                                               rows[:, a, k * P:(k + 1) * P], core.const("ident"))
                last.then_inc(turned, 1)

        @block.vector
        def _(dve):
            for k in range(KD):
                dve.wait_ge(turned, k + 1)
                nc.vector.tensor_copy(core.x[:, k], core.ps[:, k % 2]).then_inc(copied, 1)


def modulation(core, layer, ada_w):
    nc = core.nc
    W = 512
    U = 2
    blocks = 6 * D // W
    ring = core.slot(0, U, KD, W)
    acc = core.slot(4, U, W)
    cond = core.slot(5, KD)
    loaded = core.semaphores("loaded_0", "loaded_1", "weighed", "summed", "cond_ready", "sums_done")
    weighed, summed, cond_ready, sums_done = loaded[2:]
    view = ada_w[layer].rearrange("(k p) n -> p k n", p=P)
    mod = core.mod[:, layer]
    with nc.Block() as block:
        @block.sync
        def _(sp):
            core.clear_before(sp)
            for s in range(U):
                sp.dma_start(ring[:, s], view[:, :, s * W:(s + 1) * W]).then_inc(loaded[s], 16)
            with sp.Fori(1, blocks // U) as i:
                for s in range(U):
                    sp.wait_ge(weighed, (i - 1) * U + s + 1)
                    sp.dma_start(ring[:, s], view[:, :, ds(i * (U * W) + s * W, W)]).then_inc(loaded[s], 16)

        @block.scalar
        def _(act):
            nc.scalar.activation(cond, core.col("c", 0, KD), ACT.Silu).then_inc(cond_ready, 1)

        @block.vector
        def _(dve):
            dve.wait_ge(cond_ready, 1)
            with dve.Fori(0, blocks // U) as i:
                for s in range(U):
                    dve.wait_ge(loaded[s], i * 16 + 16)
                    dve.wait_ge(summed, i * U + s + 1)
                    nc.vector.tensor_scalar(acc[:, s], ring[:, s, 0], cond[:, 0:1], None, ALU.mult)
                    for k in range(1, KD):
                        dve.drain()
                        last = nc.vector.scalar_tensor_tensor(acc[:, s], ring[:, s, k], cond[:, k:k + 1],
                                                              acc[:, s], ALU.mult, ALU.add)
                    last.then_inc(weighed, 1)
            dve.wait_ge(sums_done, 1)
            nc.vector.tensor_tensor(mod, core.ps[:, 0, 0:48], core.col(f"ada_b{layer}", 0, 48), ALU.add)
            dve.drain()
            for part in (1, 2, 4, 5):
                nc.vector.tensor_scalar(mod[:, part * KD:(part + 1) * KD], mod[:, part * KD:(part + 1) * KD],
                                        1.0, None, ALU.add)

        @block.tensor
        def _(pe):
            pe.sem_inc(summed, U)
            with pe.Fori(0, blocks // U) as i:
                for s in range(U):
                    pe.wait_ge(weighed, i * U + s + 1)
                    for m in range(W // P):
                        last = nc.tensor.matmul(core.ps[:, 0, ds(i * (U * W // P) + s * (W // P) + m, 1)],
                                                acc[:, s, m * P:(m + 1) * P], core.const("ones")[:, 0:1],
                                                start=True, stop=True)
                    last.then_inc(summed, 1)
            pe.drain().then_inc(sums_done, 1)


def layer_norm(core, z, gain, bias):
    nc = core.nc
    mean, rstd = core.stats[:, 0], core.stats[:, 1]
    square = core.slot(9, 2, T)
    (mean_summed, mean_ready, centred, squared, square_used, var_summed, root_ready, rstd_ready,
     normed, scaled) = core.semaphores(
        "mean_summed", "mean_ready", "centred", "squared", "square_used", "var_summed", "root_ready",
        "rstd_ready", "normed", "scaled")
    with nc.Block() as block:
        @block.sync
        def _(sp):
            core.clear_before(sp)

        @block.tensor
        def _(pe):
            for k in range(KD):
                last = nc.tensor.matmul(core.ps[:, 0], core.const("ones"), z[:, k], start=k == 0, stop=k == KD - 1)
            last.then_inc(mean_summed, 1)
            for k in range(KD):
                pe.wait_ge(squared, k + 1)
                last = nc.tensor.matmul(core.ps[:, 1], core.const("ones"), square[:, k % 2],
                                        start=k == 0, stop=k == KD - 1)
                last.then_inc(square_used, 1)

        @block.scalar
        def _(act):
            for k in range(KD):
                act.wait_ge(centred, k + 1)
                if k >= 2:
                    act.wait_ge(square_used, k - 1)
                nc.scalar.activation(square[:, k % 2], z[:, k], ACT.Square).then_inc(squared, 1)
            act.wait_ge(var_summed, 1)
            nc.scalar.activation(rstd, rstd, ACT.Sqrt).then_inc(root_ready, 1)
            for k in range(KD):
                act.wait_ge(normed, k + 1)
                nc.scalar.activation(core.x[:, k], z[:, k], ACT.Identity, bias=core.col(bias, k),
                                     scale=core.col(gain, k)).then_inc(scaled, 1)

        @block.vector
        def _(dve):
            dve.wait_ge(mean_summed, 1)
            nc.vector.tensor_scalar(mean, core.ps[:, 0], 1.0 / D, None, ALU.mult)
            dve.drain()
            for k in range(KD):
                nc.vector.tensor_tensor(z[:, k], z[:, k], mean, ALU.subtract).then_inc(centred, 1)
            dve.wait_ge(square_used, KD)
            nc.vector.tensor_scalar(rstd, core.ps[:, 1], 1.0 / D, LN_EPS, ALU.mult, ALU.add).then_inc(var_summed, 1)
            dve.wait_ge(root_ready, 1)
            nc.vector.reciprocal(mean, rstd)
            dve.drain()
            for k in range(KD):
                nc.vector.tensor_tensor(z[:, k], z[:, k], mean, ALU.mult).then_inc(normed, 1)


def modulate(core, layer, half, u, shifted=None):
    nc = core.nc
    sh, sc = (0, 1) if half == 0 else (3, 4)
    done, = core.semaphores("modulated")
    with nc.Block() as block:
        @block.sync
        def _(sp):
            core.clear_before(sp)

        @block.vector
        def _(dve):
            for k in range(KD):
                nc.vector.tensor_scalar(u[:, k], core.x[:, k], core.mod[:, layer, sc * KD + k:sc * KD + k + 1],
                                        core.mod[:, layer, sh * KD + k:sh * KD + k + 1], ALU.mult, ALU.add)
            if shifted is not None:
                dve.drain()
                for k in range(KD):
                    nc.vector.tensor_tensor(shifted[:, k, 1:T], u[:, k, 0:T - 1], u[:, k, 1:T], ALU.subtract)
                nc.vector.tensor_scalar(shifted[:, :, 0:1], u[:, :, 0:1], -1.0, None, ALU.mult)


def linear(core, weight, tiles, kt, rhs, ring, vector=None, scalar=None, U=2, parts=1, width=P):
    nc = core.nc
    names = [f"weights_in_slot{s}" for s in range(U)]
    sems = core.semaphores(*names, "products_done", "banks_freed")
    loaded, done, freed = sems[:U], sems[U], sems[U + 1]
    assert tiles % U == 0
    n = tiles // U

    def drain(eng, each):
        with eng.Fori(0, n) as i:
            for s in range(U):
                eng.wait_ge(done, i * U + (U + s + 1))
                each(eng, i * U + s, [core.ps[:, s * parts + q] for q in range(parts)], s).then_inc(freed, 1)

    with nc.Block() as block:
        @block.sync
        def _(sp):
            core.clear_before(sp)
            with sp.Fori(0, n) as i:
                for s in range(U):
                    sp.wait_ge(done, i * U + (s + 1))
                    for q in range(parts):
                        sp.dma_start(ring[:, s * parts + q], weight(i * U + s, q)).then_inc(loaded[s], 16)

        @block.tensor
        def _(pe):
            pe.sem_inc(done, U)
            pe.sem_inc(freed, U)
            with pe.Fori(0, n) as i:
                for s in range(U):
                    pe.wait_ge(loaded[s], i * (16 * parts) + 16 * parts)
                    pe.wait_ge(freed, i * U + (s + 1))
                    for q in range(parts):
                        for k in range(kt):
                            last = nc.tensor.matmul(core.ps[0:width, s * parts + q], ring[:, s * parts + q, k],
                                                    rhs[:, k], start=k == 0, stop=k == kt - 1)
                    last.then_inc(done, 1)

        if vector is not None:
            @block.vector
            def _(dve):
                drain(dve, vector)
        if scalar is not None:
            @block.scalar
            def _(act):
                drain(act, scalar)


def columns(w, j, n=P):
    return w[:, ds(j * P, n)].rearrange("(k p) m -> p k m", p=P)


def residual(core, layer, half, w, kt, rhs, z, ring):
    nc = core.nc

    def out(dve, j, banks, s):
        gain = 1.0 if layer is None else core.mod[:, layer, ds((2 if half == 0 else 5) * KD + j, 1)]
        nc.vector.tensor_scalar(z[:, ds(j, 1)].rearrange("p o t -> p (o t)"), banks[0], gain, None, ALU.mult)
        dve.drain()
        zj = z[:, ds(j, 1)].rearrange("p o t -> p (o t)")
        return nc.vector.scalar_tensor_tensor(zj, core.x[:, ds(j, 1)].rearrange("p o t -> p (o t)"), ALPHA, zj,
                                              ALU.mult, ALU.add)

    linear(core, lambda j, q: columns(w, j), KD, kt, rhs, ring, vector=out)


def feed_forward(core, layer, u, h, ring, w_in, w_out, z, gate_first=True, conv=None):
    nc = core.nc
    U = 2
    sems = core.semaphores("weights_in_slot0", "weights_in_slot1", "products_done", "banks_freed", "gated", "convolved")
    loaded, done, freed, gated, convolved = sems[:2], sems[2], sems[3], sems[4], sems[5]
    gq = 0 if gate_first else 1
    gate = core.stats
    n = KF // U
    with nc.Block() as block:
        @block.sync
        def _(sp):
            core.clear_before(sp)
            with sp.Fori(0, n) as i:
                for s in range(U):
                    sp.wait_ge(done, i * U + (s + 1))
                    for q in range(2):
                        sp.dma_start(ring[:, s * 2 + q],
                                     w_in[:, ds((i * U + s) * P + q * FF, P)].rearrange("(k p) m -> p k m", p=P)
                                     ).then_inc(loaded[s], 16)

        @block.tensor
        def _(pe):
            pe.sem_inc(done, U)
            pe.sem_inc(freed, U)
            with pe.Fori(0, n) as i:
                for s in range(U):
                    pe.wait_ge(loaded[s], i * 32 + 32)
                    pe.wait_ge(freed, i * U + (s + 1))
                    for q in range(2):
                        for k in range(KD):
                            last = nc.tensor.matmul(core.ps[:, s * 2 + q], ring[:, s * 2 + q, k], u[:, k],
                                                    start=k == 0, stop=k == KD - 1)
                    last.then_inc(done, 1)

        @block.scalar
        def _(act):
            with act.Fori(0, n) as i:
                for s in range(U):
                    if conv is None:
                        act.wait_ge(done, i * U + (U + s + 1))
                        act.wait_ge(freed, i * U + (s + 1))
                        nc.scalar.activation(gate[:, s], core.ps[:, s * 2 + gq], ACT.Silu).then_inc(gated, 1)
                    else:
                        act.wait_ge(convolved, i * U + (s + 1))
                        nc.scalar.activation(gate[:, s], gate[:, s], ACT.Silu,
                                             bias=core.cols[:, ds(i * U + (s + conv[1]), 1)]).then_inc(gated, 1)

        @block.vector
        def _(dve):
            with dve.Fori(0, n) as i:
                for s in range(U):
                    if conv is not None:
                        dve.wait_ge(done, i * U + (U + s + 1))
                        causal_conv(nc, dve, gate[:, s], core.ps[:, s * 2 + gq],
                                    lambda j: core.cols[:, ds(i * U + (s + conv[0] + j * KF), 1)],
                                    conv[2]).then_inc(convolved, 1)
                    dve.wait_ge(gated, i * U + (s + 1))
                    nc.vector.tensor_tensor(h[:, ds(i * U + s, 1)].rearrange("p o t -> p (o t)"), gate[:, s],
                                            core.ps[:, s * 2 + 1 - gq], ALU.mult).then_inc(freed, 1)
    residual(core, layer, 1, w_out, KF, h, z, core.slot(6, 2, KF, P))


HR = 16
DECAY = float(np.exp(-0.5))


def rwkv_projections(core, A):
    nc = core.nc
    u, xx = core.slot(0, KD, T), core.slot(1, KD, T)
    mix = core.slot(2, 3, KD, T)
    rkv = core.slot(5, 3 * KD, T)
    ring = core.slot(8, 4, KD, P)
    lora = core.slot(9, 4096)
    down = {3: lora[:, 0:512].rearrange("p (k m) -> p k m", k=KD), 4: lora[:, 512:1024].rearrange("p (k m) -> p k m", k=KD),
            5: lora[:, 1024:2048].rearrange("p (k m) -> p k m", k=KD)}
    up = {3: lora[0:64, 2048:3072], 4: lora[0:64, 3072:4096]}
    inner = core.lora_inner
    modulate(core, 0, 0, u, xx)

    def lerp(dve, i, k):
        return nc.vector.scalar_tensor_tensor(mix[:, i % 3, k], xx[:, k], core.col("mu", i * KD + k), u[:, k],
                                              ALU.mult, ALU.add)

    loaded, mixed, summed = core.semaphores("lora_loaded", "mixed", "inner_summed")
    rank = {3: 64, 4: 64, 5: 128}
    with nc.Block() as block:
        @block.sync
        def _(sp):
            core.clear_before(sp)
            for i, name in ((3, "rwkv_w1"), (4, "rwkv_a1"), (5, "rwkv_g1")):
                sp.dma_start(down[i], A[name].rearrange("o (k p) m -> p (o k) m", p=P)).then_inc(loaded, 16)
            for i, name in ((3, "rwkv_w2"), (4, "rwkv_a2")):
                sp.dma_start(up[i], A[name].rearrange("o r n -> (o r) n")).then_inc(loaded, 16)

        @block.vector
        def _(dve):
            for i in (3, 4, 5):
                for k in range(KD):
                    lerp(dve, i, k).then_inc(mixed, 1)

        @block.tensor
        def _(pe):
            pe.wait_ge(loaded, 80)
            for i in (3, 4, 5):
                for k in range(KD):
                    pe.wait_ge(mixed, (i - 3) * KD + k + 1)
                    last = nc.tensor.matmul(core.ps[0:rank[i], i], down[i][:, k], mix[:, i % 3, k],
                                            start=k == 0, stop=k == KD - 1)
                last.then_inc(summed, 1)

        @block.scalar
        def _(act):
            for i, f in ((3, ACT.Tanh), (4, ACT.Identity), (5, ACT.Sigmoid)):
                act.wait_ge(summed, i - 2)
                nc.scalar.activation(inner[0:rank[i], i - 3], core.ps[0:rank[i], i], f)

    U = 4
    sems = core.semaphores(*[f"weights_in_slot{s}" for s in range(U)], "products_done", "banks_freed", "mixed")
    loaded, (done, freed, mixed) = sems[:U], sems[U:]
    w = A["rwkv_w_rkv"].rearrange("o i k n -> (o i) k n")
    per = KD // U
    with nc.Block() as block:
        @block.sync
        def _(sp):
            core.clear_before(sp)
            with sp.Fori(0, 3) as m:
                with sp.Fori(0, per) as i:
                    for s in range(U):
                        sp.wait_ge(done, m * KD + i * U + (s + 1))
                        sp.dma_start(ring[:, s], w[ds(m, 1), :, ds(i * (U * P) + s * P, P)].rearrange(
                            "o (k p) m -> p (o k) m", p=P)).then_inc(loaded[s], 16)

        @block.vector
        def _(dve):
            for i in range(3):
                for k in range(KD):
                    lerp(dve, i, k).then_inc(mixed, 1)

        @block.tensor
        def _(pe):
            pe.sem_inc(done, U)
            pe.sem_inc(freed, U)
            with pe.Fori(0, 3) as m:
                with pe.Fori(0, per) as i:
                    for s in range(U):
                        pe.wait_ge(mixed, m * KD + KD)
                        pe.wait_ge(loaded[s], m * (16 * per) + i * 16 + 16)
                        pe.wait_ge(freed, m * KD + i * U + (s + 1))
                        for k in range(KD):
                            last = nc.tensor.matmul(core.ps[:, s], ring[:, s, k],
                                                    mix[:, ds(m, 1), k].rearrange("p o t -> p (o t)"),
                                                    start=k == 0, stop=k == KD - 1)
                        last.then_inc(done, 1)

        @block.scalar
        def _(act):
            with act.Fori(0, 3) as m:
                with act.Fori(0, per) as i:
                    for s in range(U):
                        act.wait_ge(done, m * KD + i * U + (U + s + 1))
                        nc.scalar.copy(rkv[:, ds(m * KD + i * U + s, 1)].rearrange("p o t -> p (o t)"),
                                       core.ps[:, s]).then_inc(freed, 1)

    lw, a = core.slot(0, KD, T), core.slot(1, KD, T)
    summed, taken = core.semaphores("outer_summed", "banks_taken")
    with nc.Block() as block:
        @block.sync
        def _(sp):
            core.clear_before(sp)

        @block.tensor
        def _(pe):
            for n in range(2 * KD):
                which, k = 3 + n // KD, n % KD
                if n >= 4:
                    pe.wait_ge(taken, n - 3)
                nc.tensor.matmul(core.ps[:, n % 4], up[which][:, k * P:(k + 1) * P], inner[0:64, which - 3],
                                 start=True, stop=True).then_inc(summed, 1)

        @block.scalar
        def _(act):
            for n in range(2 * KD):
                k = n % KD
                act.wait_ge(summed, n + 1)
                nc.scalar.activation((lw if n < KD else a)[:, k], core.ps[:, n % 4], ACT.Sigmoid,
                                     bias=core.col("w0" if n < KD else "a0", k)).then_inc(taken, 1)

        @block.vector
        def _(dve):
            dve.wait_ge(taken, KD)
            nc.vector.tensor_scalar(lw, lw, -DECAY, None, ALU.mult)


def rwkv_decays(core):
    nc = core.nc
    lw, a, r, k, kk = (core.slot(n, KD, T) for n in (0, 1, 5, 6, 2))
    t3, t4 = core.slot(3, KD, T), core.slot(4, KD, T)
    mid, first, ends = core.mid, core.first, core.ends
    (k_scaled, squared, head_summed, floored, rooted, kk_done, product, bonus_summed, running, risen,
     fallen, ends_risen) = core.semaphores(
        "k_scaled", "squared", "head_summed", "floored", "rooted", "kk_done", "bonus_product", "bonus_summed",
        "running_sums", "risen", "fallen", "ends_risen")

    def by_chunk(t):
        return t.rearrange("p k (c t) -> p (k c) t", c=NC)

    with nc.Block() as block:
        @block.sync
        def _(sp):
            core.clear_before(sp)

        @block.scalar
        def _(act):
            for i in range(KD):
                act.wait_ge(k_scaled, i + 1)
                nc.scalar.activation(t3[:, i], kk[:, i], ACT.Square).then_inc(squared, 1)
            for i in range(KD):
                act.wait_ge(floored, i + 1)
                nc.scalar.activation(t4[:, i], t4[:, i], ACT.Sqrt).then_inc(rooted, 1)
            act.wait_ge(running, 1)
            act.wait_ge(bonus_summed, 1)
            nc.scalar.activation(t3, lw, ACT.Exp).then_inc(risen, 1)
            nc.scalar.activation(t4, lw, ACT.Exp, scale=-1.0).then_inc(fallen, 1)
            nc.scalar.activation(first[:], mid[:], ACT.Exp, scale=-1.0)
            nc.scalar.activation(ends[:], ends[:], ACT.Exp).then_inc(ends_risen, 1)

        @block.tensor
        def _(pe):
            for i in range(KD):
                pe.wait_ge(squared, i + 1)
                if i >= 4:
                    pe.wait_ge(floored, i - 3)
                nc.tensor.matmul(core.ps[:, i % 4], core.const("head64"), t3[:, i], start=True,
                                 stop=True).then_inc(head_summed, 1)
            for i in range(KD):
                pe.wait_ge(product, i + 1)
                last = nc.tensor.matmul(core.ps[0:HR, 4], core.const("heads16")[:, i * HR:(i + 1) * HR], t3[:, i],
                                        start=i == 0, stop=i == KD - 1)
            last.then_inc(bonus_summed, 1)

        @block.vector
        def _(dve):
            for i in range(KD):
                nc.vector.tensor_scalar(kk[:, i], k[:, i], core.col("k_k", i), None, ALU.mult).then_inc(k_scaled, 1)
            for i in range(KD):
                dve.wait_ge(head_summed, i + 1)
                nc.vector.tensor_scalar(t4[:, i], core.ps[:, i % 4], 1e-6, None, ALU.add).then_inc(floored, 1)
            for i in range(KD):
                dve.wait_ge(rooted, i + 1)
                nc.vector.reciprocal(t4[:, i], t4[:, i])
            dve.drain()
            nc.vector.tensor_tensor(kk, kk, t4, ALU.mult)
            dve.drain()
            for i in range(KD):
                nc.vector.tensor_scalar(t4[:, i], a[:, i], core.col("k_a", i), core.one_less_k_a[:, i:i + 1],
                                        ALU.mult, ALU.add)
            dve.drain()
            nc.vector.tensor_tensor(k, k, t4, ALU.mult)
            nc.vector.tensor_tensor(a, a, kk, ALU.mult)
            dve.drain()
            for i in range(KD):
                nc.vector.scalar_tensor_tensor(t3[:, i], r[:, i], core.col("r_k", i), k[:, i], ALU.mult,
                                               ALU.mult).then_inc(product, 1)
            for i in range(KD):
                nc.vector.tensor_tensor_scan(t4[:, i], core.const("carry"), lw[:, i], 0.0, ALU.mult, ALU.add)
            dve.drain()
            nc.vector.tensor_copy(mid[:].rearrange("p (n o) -> p n o", o=1), by_chunk(t4)[:, :, C // 2 - 1:C // 2])
            dve.drain()
            nc.vector.tensor_tensor(by_chunk(lw), by_chunk(t4), mid[:].unsqueeze(2).to_broadcast([P, KD * NC, C]),
                                    ALU.subtract)
            dve.drain()
            nc.vector.tensor_copy(ends[:].rearrange("p (n o) -> p n o", o=1), by_chunk(lw)[:, :, C - 1:C])
            dve.drain()
            e4, m4 = (t[:].rearrange("p (k c) -> p k c", c=NC) for t in (ends, mid))
            nc.vector.tensor_tensor(e4[:, :, 0:NC - 1], e4[:, :, 0:NC - 1], m4[:, :, 1:NC], ALU.add)
            dve.drain().then_inc(running, 1)
            dve.wait_ge(bonus_summed, 1)
            nc.vector.tensor_copy(core.bonus[:], core.ps[0:HR, 4])
            dve.wait_ge(risen, 1)
            dve.wait_ge(fallen, 1)
            nc.vector.tensor_tensor(r, r, t3, ALU.mult)
            nc.vector.tensor_tensor(k, k, t4, ALU.mult)
            nc.vector.tensor_tensor(a, a, t4, ALU.mult)
            nc.vector.tensor_tensor(by_chunk(kk)[:, :, 1:C], by_chunk(kk)[:, :, 1:C], by_chunk(t3)[:, :, 0:C - 1],
                                    ALU.mult)
            dve.wait_ge(ends_risen, 1)
            nc.vector.tensor_tensor(by_chunk(kk)[:, :, 0:1], by_chunk(kk)[:, :, 0:1], first[:].unsqueeze(2), ALU.mult)
            nc.vector.memset(e4[:, :, NC - 1:NC], 0.0)


def rwkv_chunks(core):
    nc = core.nc
    R, Aa, B, K, V = (core.slot(n, KD, T) for n in (5, 2, 1, 6, 7))
    HT = KD // 2
    H = HR // 2
    ar = core.slot(0, HT, 2, C)
    b_c, k_c, v_c = (core.area[:, 0, 1024 + n * 512:1536 + n * 512].rearrange("p (k t) -> p k t", k=HT) for n in range(3))
    turned = core.area[:, 0, 2560:4096].rearrange("p (w k t) -> p w k t", w=3, k=HT)
    gram = core.slot(3, H, 4, C)
    X, XT = core.slot(4, H, C), core.area[:, 4, 1024:2048].rearrange("p (h t) -> p h t", h=H)
    W = core.area[:, 4, 2048:3072].rearrange("p (h t) -> p h t", h=H)
    Z = core.area[:, 4, 3072:3584].rearrange("p (h v) -> p h v", h=H)
    Uu = core.area[:, 4, 3584:4096].rearrange("p (h v) -> p h v", h=H)
    S = core.slot(8, HT, 64)
    masks = core.area[:, 8, 1024:1536]
    G = 2
    nlev = len(LEVELS)
    (staged, turned_ps, turned_sb, gram_ps, gram_sb, seed_sb, x_ps, x_sb, w_ps, w_sb, xw_ps, x_new, xt_ps, xt_new,
     z_ps, z_sb, u_ps, u_sb, y_ps, s_ps, s_new, y_sb, gram_seen) = core.semaphores(
        "staged", "turned_ps", "turned_sb", "gram_ps", "gram_sb", "seed_sb", "x_ps", "x_sb", "w_ps", "w_sb", "xw_ps",
        "x_new", "xt_ps", "xt_new", "z_ps", "z_sb", "u_ps", "u_sb", "y_ps", "s_ps", "s_new", "y_sb", "gram_seen")
    ident = core.const("ident")

    def each_step(eng, body):
        with eng.Fori(0, 2) as half:
            with eng.Fori(0, NC) as c:
                body(half, c, half * NC + c)

    def part(t, half, c):
        return t[:, ds(half * HT, HT), ds(c * C, C)]

    def head(t, h):
        return t[64 * (h % 2):64 * (h % 2) + 64, h // 2]

    with nc.Block() as block:
        @block.sync
        def _(sp):
            core.clear_before(sp)

        @block.gpsimd
        def _(pool):
            def body(half, c, n):
                pool.wait_ge(y_ps, n * 1 + 1)
                nc.gpsimd.tensor_copy(b_c, part(B, half, c))
                nc.gpsimd.tensor_copy(k_c, part(K, half, c))
                nc.gpsimd.tensor_copy(v_c, part(V, half, c))
                nc.gpsimd.tensor_copy(ar[:, :, 0], part(Aa, half, c))
                nc.gpsimd.tensor_copy(ar[:, :, 1], part(R, half, c)).then_inc(staged, 1)
            each_step(pool, body)

        @block.tensor
        def _(pe):
            pe.sem_inc(y_ps, 1)

            def body(half, c, n):
                pe.wait_ge(staged, n + 1)
                pe.wait_ge(s_new, n + 1)
                for w, src in enumerate((b_c, k_c, v_c)):
                    for p in range(HT):
                        last = nc.tensor.transpose(core.ps[:, w, p * C:(p + 1) * C], src[:, p], ident)
                    last.then_inc(turned_ps, 1)
                for h in range(H):
                    if h >= 4:
                        pe.wait_ge(gram_sb, n * H + (h - 3))
                    bank = core.ps[:, 4 + h % 4]
                    both = head(ar, h).rearrange("p w t -> p (w t)")
                    nc.tensor.matmul(bank[:, 0:2 * C], head(b_c, h), both, start=True, stop=True)
                    nc.tensor.matmul(bank[:, 2 * C:4 * C], head(k_c, h), both, start=True,
                                     stop=True).then_inc(gram_ps, 1)
                invert_products(core, pe, n, G, ident, lambda h: gram[:, h, 0], X, XT, W,
                                (turned_sb, 3), seed_sb, x_ps, x_sb, w_ps, w_sb, xw_ps, x_new, xt_ps, xt_new)
                for h in range(H):
                    out = core.ps[:, 3 * (h % 2), (h // 2) * 64:(h // 2 + 1) * 64]
                    lo = 64 * (h % 2)
                    nc.tensor.matmul(out, ar[lo:lo + 64, h // 2, 0], S[lo:lo + 64, h // 2], start=True, stop=False)
                    last = nc.tensor.matmul(out, gram[:, h, 2], turned[:, 2, h // 2, lo:lo + 64], start=False, stop=True)
                last.then_inc(z_ps, 1)
                pe.wait_ge(z_sb, n + 1)
                for h in range(H):
                    last = nc.tensor.matmul(core.ps[:, 1, h * 64:(h + 1) * 64], XT[:, h], Z[:, (h % 2) * HT + h // 2], start=True, stop=True)
                last.then_inc(u_ps, 1)
                pe.wait_ge(u_sb, n + 1)
                for h in range(H):
                    lo = 64 * (h % 2)
                    out = core.ps[lo:lo + 64, 2, (h // 2) * 64:(h // 2 + 1) * 64]
                    nc.tensor.matmul(out, turned[:, 0, h // 2, lo:lo + 64], Uu[:, h], start=True, stop=False)
                    last = nc.tensor.matmul(out, turned[:, 1, h // 2, lo:lo + 64], turned[:, 2, h // 2, lo:lo + 64],
                                            start=False, stop=True)
                last.then_inc(s_ps, 1)
                for h in range(H):
                    lo = 64 * (h % 2)
                    out = core.ps[lo:lo + 64, 3, (h // 2) * C:(h // 2 + 1) * C]
                    nc.tensor.matmul(out, S[lo:lo + 64, h // 2], ar[lo:lo + 64, h // 2, 1], start=True, stop=False)
                    nc.tensor.matmul(out, Uu[:, h], gram[:, h, 1], start=False, stop=False)
                    last = nc.tensor.matmul(out, turned[:, 2, h // 2, lo:lo + 64], gram[:, h, 3], start=False, stop=True)
                last.then_inc(y_ps, 1)
            each_step(pe, body)

        @block.scalar
        def _(act):
            def body(half, c, n):
                for w in range(3):
                    act.wait_ge(turned_ps, n * 3 + (w + 1))
                    nc.scalar.copy(turned[:, w].rearrange("p k t -> p (k t)"), core.ps[:, w]).then_inc(turned_sb, 1)
                for g in range(G):
                    act.wait_ge(x_ps, n * G + (g + 1))
                    nc.scalar.copy(X[:, 4 * g:4 * g + 4].rearrange("p h t -> p (h t)"), core.ps[:, g]).then_inc(x_sb, 1)
                act.wait_ge(z_ps, n + 1)
                for odd in range(2):
                    last = nc.scalar.copy(Z[:, odd * HT:(odd + 1) * HT].rearrange("p h v -> p (h v)"),
                                          core.ps[:, 3 * odd, 0:HT * 64])
                last.then_inc(z_sb, 1)
                act.wait_ge(u_ps, n + 1)
                nc.scalar.mul(Uu.rearrange("p h v -> p (h v)"), core.ps[:, 1], -1.0).then_inc(u_sb, 1)
                act.wait_ge(y_ps, n + 2)
                nc.scalar.copy(part(R, half, c), core.ps[:, 3].rearrange("p (k t) -> p k t", k=HT)).then_inc(y_sb, 1)
            each_step(act, body)

        @block.vector
        def _(dve):
            nc.vector.memset(gram, 0.0)
            nc.vector.tensor_copy(masks.rearrange("p (a b) -> p a b", a=2)[:, :, 0:C],
                                  core.const("upper").unsqueeze(1).to_broadcast([P, 2, C]))
            nc.vector.tensor_copy(masks.rearrange("p (a b) -> p a b", a=2)[:, :, C:2 * C],
                                  core.const("upto").unsqueeze(1).to_broadcast([P, 2, C]))
            nc.vector.memset(S, 0.0).then_inc(s_new, 1)
            dve.drain()

            def body(half, c, n):
                for h in range(H):
                    dve.wait_ge(gram_ps, n * H + (h + 1))
                    dve.sem_inc(gram_seen, 1)
                    nc.vector.copy_predicated(gram[:, h].rearrange("p w t -> p (w t)"), masks.bitcast(U32),
                                              core.ps[:, 4 + h % 4]).then_inc(gram_sb, 1)
                dve.drain()
                invert_updates(core, dve, n, G, lambda g: gram[:, 4 * g:4 * g + 4, 0], X, XT, W,
                               seed_sb, x_sb, w_ps, w_sb, xw_ps, x_new, xt_ps, xt_new)
                dve.wait_ge(s_ps, n + 1)
                dve.wait_ge(y_ps, n + 2)
                nc.vector.tensor_tensor(S, S, core.ps[:, 2, 0:HT * 64].rearrange("p (k v) -> p k v", k=HT), ALU.add)
                dve.drain()
                ends = core.ends[:].rearrange("p (k c) -> p k c", c=NC)[:, ds(half * HT, HT), ds(c, 1)]
                nc.vector.tensor_tensor(S, S, ends.to_broadcast([P, HT, 64]), ALU.mult).then_inc(s_new, 1)
                dve.wait_ge(y_sb, n + 1)
            each_step(dve, body)


def invert_products(core, pe, n, G, ident, lower_t, X, XT, W, turned_sb, seed_sb, x_ps, x_sb, w_ps, w_sb, xw_ps, x_new,
                    xt_ps, xt_new):
    nc = core.nc
    nl = len(LEVELS)
    pe.wait_ge(turned_sb[0], n * turned_sb[1] + turned_sb[1])
    for g in range(G):
        pe.wait_ge(seed_sb, n * G + (g + 1))
        for h in range(4):
            last = nc.tensor.transpose(core.ps[:, g, h * C:(h + 1) * C], XT[:, 4 * g + h], ident)
        last.then_inc(x_ps, 1)
    for lev in range(nl):
        final = lev == nl - 1
        for g in range(G):
            if lev == 0:
                pe.wait_ge(x_sb, n * G + (g + 1))
            else:
                pe.wait_ge(x_new, n * (G * (nl - 1)) + (lev - 1) * G + g + 1)
            for h in range(4):
                last = nc.tensor.matmul(core.ps[:, g, h * C:(h + 1) * C], lower_t(4 * g + h), X[:, 4 * g + h],
                                        start=True, stop=True)
            last.then_inc(w_ps, 1)
        for g in range(G):
            pe.wait_ge(w_sb, n * (G * nl) + lev * G + g + 1)
            if lev:
                pe.wait_ge(xt_new, n * (G * nl) + (lev - 1) * G + g + 1)
            if not final:
                for h in range(4):
                    last = nc.tensor.matmul(core.ps[:, 2 + g, h * C:(h + 1) * C], XT[:, 4 * g + h], W[:, 4 * g + h],
                                            start=True, stop=True)
                last.then_inc(xw_ps, 1)
            for h in range(4):
                last = nc.tensor.matmul(core.ps[:, 4 + g, h * C:(h + 1) * C], W[:, 4 * g + h], XT[:, 4 * g + h],
                                        start=True, stop=True)
            last.then_inc(xt_ps, 1)
    pe.wait_ge(xt_new, n * (G * nl) + G * nl)


def invert_updates(core, dve, n, G, lower_t, X, XT, W, seed_sb, x_sb, w_ps, w_sb, xw_ps, x_new, xt_ps, xt_new):
    nc = core.nc
    nl = len(LEVELS)

    def four(t, g):
        return t[:, 4 * g:4 * g + 4]

    def mask(name):
        return core.const(name).unsqueeze(1).to_broadcast([P, 4, C])

    def bank(b):
        return core.ps[:, b].rearrange("p (h t) -> p h t", h=4)

    for g in range(G):
        nc.vector.tensor_tensor(four(XT, g), lower_t(g), mask("corner1"), ALU.mult)
    dve.drain()
    for g in range(G):
        nc.vector.tensor_tensor(four(XT, g), mask("ident"), four(XT, g), ALU.subtract).then_inc(seed_sb, 1)
    for lev, b in enumerate(LEVELS):
        final = lev == nl - 1
        for g in range(G):
            dve.wait_ge(w_ps, n * (G * nl) + lev * G + g + 1)
            nc.vector.tensor_tensor(four(W, g), bank(g), mask(f"corner{b}"), ALU.mult).then_inc(w_sb, 1)
        for g in range(G):
            if not final:
                dve.drain()
                dve.wait_ge(xw_ps, n * (G * (nl - 1)) + lev * G + g + 1)
                if lev == 0:
                    dve.wait_ge(x_sb, n * G + (g + 1))
                nc.vector.tensor_tensor(four(X, g), four(X, g), bank(2 + g), ALU.subtract).then_inc(x_new, 1)
            dve.drain()
            dve.wait_ge(xt_ps, n * (G * nl) + lev * G + g + 1)
            nc.vector.tensor_tensor(four(XT, g), four(XT, g), bank(4 + g), ALU.subtract).then_inc(xt_new, 1)


def rwkv_output(core, A):
    nc = core.nc
    y, v = core.slot(5, KD, T), core.slot(7, KD, T)
    g2 = core.slot(3, D)
    sq = core.slot(4, 4, T)
    (loaded, y_summed, centred, squared, var_summed, floored, rooted, bonus_spread, gate_ps, freed) = core.semaphores(
        "gate_loaded", "y_summed", "centred", "squared", "var_summed", "floored", "rooted", "bonus_spread", "gate_ps",
        "banks_freed")
    bonus_at, _ = CONST_AT["spread16"]
    with nc.Block() as block:
        @block.sync
        def _(sp):
            core.clear_before(sp)
            sp.dma_start(g2, A["rwkv_g2"].rearrange("o r n -> (o r) n")).then_inc(loaded, 16)

        @block.tensor
        def _(pe):
            pe.wait_ge(loaded, 16)
            for k in range(KD):
                b = 4 * (k % 2)
                if k >= 2:
                    pe.wait_ge(freed, k - 1)
                nc.tensor.matmul(core.ps[:, b], core.const("head64"), y[:, k], start=True, stop=True).then_inc(y_summed, 1)
                nc.tensor.matmul(core.ps[:, b + 2], core.const("spread16", HR)[:, k * P:(k + 1) * P], core.bonus[:],
                                 start=True, stop=True).then_inc(bonus_spread, 1)
                nc.tensor.matmul(core.ps[:, b + 3], g2[:, k * P:(k + 1) * P], core.lora_inner[:, 2],
                                 start=True, stop=True).then_inc(gate_ps, 1)
                pe.wait_ge(squared, k + 1)
                nc.tensor.matmul(core.ps[:, b + 1], core.const("head64"), sq[:, k % 2], start=True,
                                 stop=True).then_inc(var_summed, 1)

        @block.scalar
        def _(act):
            for k in range(KD):
                act.wait_ge(centred, k + 1)
                nc.scalar.activation(sq[:, k % 2], y[:, k], ACT.Square).then_inc(squared, 1)
                act.wait_ge(floored, k + 1)
                nc.scalar.activation(sq[:, 2 + k % 2], sq[:, 2 + k % 2], ACT.Sqrt).then_inc(rooted, 1)

        @block.vector
        def _(dve):
            for k in range(KD):
                b = 4 * (k % 2)
                root = sq[:, 2 + k % 2]
                dve.wait_ge(y_summed, k + 1)
                nc.vector.scalar_tensor_tensor(y[:, k], core.ps[:, b], -1.0 / 64, y[:, k], ALU.mult,
                                               ALU.add).then_inc(centred, 1)
                dve.wait_ge(bonus_spread, k + 1)
                nc.vector.tensor_tensor(v[:, k], v[:, k], core.ps[:, b + 2], ALU.mult)
                dve.wait_ge(var_summed, k + 1)
                nc.vector.tensor_scalar(root, core.ps[:, b + 1], 1.0 / 64, 64e-5, ALU.mult, ALU.add).then_inc(floored, 1)
                dve.wait_ge(rooted, k + 1)
                nc.vector.reciprocal(root, root)
                dve.drain()
                nc.vector.scalar_tensor_tensor(y[:, k], y[:, k], core.col("gn_g", k), root, ALU.mult, ALU.mult)
                dve.drain()
                nc.vector.scalar_tensor_tensor(y[:, k], y[:, k], core.col("gn_b", k), v[:, k], ALU.add, ALU.add)
                dve.drain()
                dve.wait_ge(gate_ps, k + 1)
                nc.vector.tensor_tensor(y[:, k], y[:, k], core.ps[:, b + 3], ALU.mult).then_inc(freed, 1)
    z = core.slot(2, KD, T)
    residual(core, 0, 0, A["rwkv_w_out"].rearrange("o k n -> (o k) n"), KD, y, z, core.slot(0, 2, KD, P))
    layer_norm(core, z, "ln_g00", "ln_b00")


HG = 8
TAPS = 4


def causal_conv(nc, dve, tmp, ps, tap, taps):
    nc.vector.tensor_scalar(tmp, ps, tap(taps - 1), None, ALU.mult)
    for back in range(1, taps):
        dve.drain()
        last = nc.vector.scalar_tensor_tensor(tmp[:, back:T], ps[:, 0:T - back], tap(taps - 1 - back), tmp[:, back:T],
                                              ALU.mult, ALU.add)
    return last


def gdn_projections(core, A):
    nc = core.nc
    u = core.slot(0, KD, T)
    qkv, z = core.slot(1, 3 * KD, T), core.slot(4, KD, T)
    ring, tmp = core.slot(5, 4, KD, P), core.slot(6, 2, T)
    w = A["gdn_w_in"].rearrange("o k n -> (o k) n")
    modulate(core, 1, 0, u)
    U = 2
    n = 3 * KD // U
    (l0, l1, done, freed, convolved, activated) = core.semaphores(
        "weights_in_slot0", "weights_in_slot1", "products_done", "banks_freed", "convolved", "activated")
    loaded = (l0, l1)
    conv = core.col_at["conv"]
    with nc.Block() as block:
        @block.sync
        def _(sp):
            core.clear_before(sp)
            with sp.Fori(0, n) as i:
                for s in range(U):
                    sp.wait_ge(done, i * U + (s + 1))
                    sp.dma_start(ring[:, s], columns(w, i * U + s)).then_inc(loaded[s], 16)

        @block.tensor
        def _(pe):
            pe.sem_inc(done, U)
            pe.sem_inc(freed, U)
            with pe.Fori(0, n) as i:
                for s in range(U):
                    pe.wait_ge(loaded[s], i * 16 + 16)
                    pe.wait_ge(freed, i * U + (s + 1))
                    for k in range(KD):
                        last = nc.tensor.matmul(core.ps[:, s], ring[:, s, k], u[:, k], start=k == 0, stop=k == KD - 1)
                    last.then_inc(done, 1)

        @block.vector
        def _(dve):
            dve.sem_inc(activated, U)
            with dve.Fori(0, n) as i:
                for s in range(U):
                    dve.wait_ge(done, i * U + (U + s + 1))
                    dve.wait_ge(activated, i * U + (s + 1))
                    causal_conv(nc, dve, tmp[:, s], core.ps[:, s],
                                lambda j: core.cols[:, ds(i * U + (s + conv + j * 3 * KD), 1)], TAPS)
                    dve.drain().then_inc(convolved, 1)
                    dve.sem_inc(freed, 1)

        @block.scalar
        def _(act):
            with act.Fori(0, n) as i:
                for s in range(U):
                    act.wait_ge(convolved, i * U + (s + 1))
                    nc.scalar.activation(qkv[:, ds(i * U + s, 1)].rearrange("p o t -> p (o t)"), tmp[:, s],
                                         ACT.Silu).then_inc(activated, 1)

    linear(core, lambda j, q: w[:, ds(j * P + 3 * D, P)].rearrange("(k p) m -> p k m", p=P), KD, KD, u, ring,
           scalar=lambda act, j, banks, s: nc.scalar.activation(z[:, ds(j, 1)].rearrange("p o t -> p (o t)"), banks[0],
                                                                ACT.Silu))

    wg = core.slot(5, KD, 2 * HG)
    small = core.slot(6, 2, 4)
    alog, dt = small[0:HG, 0, 0:1], small[0:HG, 1, 0:1]
    tmp = core.slot(7, 4, T)
    x, soft, pos, g = (tmp[0:HG, i] for i in range(4))
    beta, gc, rise, fall = (core.gate_rows[:, i] for i in range(4))
    loaded, summed, shifted, softened, powered, cum, gates_done, turned = core.semaphores(
        "gates_loaded", "gates_summed", "shifted", "softened", "powered", "cumulated", "gates_done", "turned")
    with nc.Block() as block:
        @block.sync
        def _(sp):
            core.clear_before(sp)
            sp.dma_start(wg, w[:, 4 * D:4 * D + 2 * HG].rearrange("(k p) m -> p k m", p=P)).then_inc(loaded, 16)
            sp.dma_start(alog, A["gdn_a_log"].rearrange("o h -> h o")).then_inc(loaded, 16)
            sp.dma_start(dt, A["gdn_dt_bias"].rearrange("o h -> h o")).then_inc(loaded, 16)

        @block.tensor
        def _(pe):
            pe.wait_ge(loaded, 48)
            for q in range(2):
                for k in range(KD):
                    last = nc.tensor.matmul(core.ps[0:HG, q], wg[:, k, q * HG:(q + 1) * HG], u[:, k],
                                            start=k == 0, stop=k == KD - 1)
            last.then_inc(summed, 1)
            pe.wait_ge(cum, 1)
            for c in range(NC):
                last = nc.tensor.transpose(core.ps[:, 2, c * HG:(c + 1) * HG], gc[:, c * C:(c + 1) * C],
                                           core.const("ident", HG)[:, 0:HG])
            last.then_inc(turned, 1)

        @block.scalar
        def _(act):
            act.wait_ge(summed, 1)
            nc.scalar.activation(beta, core.ps[0:HG, 0], ACT.Sigmoid)
            act.wait_ge(loaded, 48)
            nc.scalar.activation(alog, alog, ACT.Exp)
            act.wait_ge(shifted, 1)
            nc.scalar.activation(soft, x, ACT.Abs)
            act.drain()
            nc.scalar.activation(soft, soft, ACT.Exp, scale=-1.0)
            act.drain()
            nc.scalar.activation(soft, soft, ACT.Ln, bias=1.0).then_inc(softened, 1)
            act.wait_ge(cum, 2)
            nc.scalar.activation(rise, gc, ACT.Exp)
            nc.scalar.activation(fall, fall, ACT.Exp).then_inc(powered, 1)

        @block.vector
        def _(dve):
            dve.wait_ge(summed, 1)
            dve.wait_ge(loaded, 48)
            nc.vector.tensor_scalar(x, core.ps[0:HG, 1], dt, None, ALU.add).then_inc(shifted, 1)
            dve.drain()
            nc.vector.tensor_scalar(pos, x, 0.0, None, ALU.max)
            dve.wait_ge(softened, 1)
            dve.drain()
            nc.vector.tensor_tensor(g, pos, soft, ALU.add)
            dve.drain()
            nc.vector.tensor_scalar(g, g, alog, -1.0, ALU.mult, ALU.mult)
            dve.drain()
            nc.vector.tensor_tensor_scan(gc, core.const("carry", HG), g, 0.0, ALU.mult, ALU.add).then_inc(cum, 1)
            dve.drain()
            g3, f3 = (t.rearrange("p (c t) -> p c t", c=NC) for t in (gc, fall))
            nc.vector.tensor_tensor(f3, g3[:, :, C - 1:C].to_broadcast([HG, NC, C]), g3, ALU.subtract).then_inc(cum, 1)
            dve.wait_ge(turned, 1)
            nc.vector.tensor_copy(core.gate_cols[:], core.ps[:, 2, 0:NC * HG])


def head_norms(core, pairs, eps, mean):
    nc = core.nc
    sq = core.slot(9, 2, T)
    squared, summed, floored, rooted = core.semaphores("squared", "summed", "floored", "rooted")
    with nc.Block() as block:
        @block.sync
        def _(sp):
            core.clear_before(sp)

        @block.scalar
        def _(act):
            for n, (t, rows) in enumerate(pairs):
                for h in range(HG):
                    at = n * HG + h
                    if at >= 2:
                        act.wait_ge(summed, at - 1)
                    nc.scalar.activation(sq[:, at % 2], t[:, h], ACT.Square).then_inc(squared, 1)
            for n, (t, rows) in enumerate(pairs):
                act.wait_ge(floored, n + 1)
                nc.scalar.activation(rows, rows, ACT.Sqrt).then_inc(rooted, 1)

        @block.tensor
        def _(pe):
            for n in range(len(pairs)):
                for h in range(HG):
                    at = n * HG + h
                    pe.wait_ge(squared, at + 1)
                    nc.tensor.matmul(core.ps[0:HG, n], core.const("pick8")[:, HG - 1 - h:2 * HG - 1 - h], sq[:, at % 2],
                                     start=h == 0, stop=h == HG - 1).then_inc(summed, 1)

        @block.vector
        def _(dve):
            for n, (t, rows) in enumerate(pairs):
                dve.wait_ge(summed, (n + 1) * HG)
                nc.vector.tensor_scalar(rows, core.ps[0:HG, n], mean, eps, ALU.mult, ALU.add).then_inc(floored, 1)
            for n, (t, rows) in enumerate(pairs):
                dve.wait_ge(rooted, n + 1)
                nc.vector.reciprocal(rows, rows)


def spread_rows(core, jobs):
    nc = core.nc
    spread, used = core.semaphores("spread", "used")
    with nc.Block() as block:
        @block.sync
        def _(sp):
            core.clear_before(sp)

        @block.tensor
        def _(pe):
            for n, (rows, use) in enumerate(jobs):
                for h in range(HG):
                    at = n * HG + h
                    if at >= 4:
                        pe.wait_ge(used, at - 3)
                    nc.tensor.matmul(core.ps[:, at % 4], core.const("spread8", HG)[:, h * P:(h + 1) * P], rows,
                                     start=True, stop=True).then_inc(spread, 1)

        @block.vector
        def _(dve):
            for n, (rows, use) in enumerate(jobs):
                for h in range(HG):
                    at = n * HG + h
                    dve.wait_ge(spread, at + 1)
                    use(dve, h, core.ps[:, at % 4]).then_inc(used, 1)


def gdn_chunks(core):
    nc = core.nc
    q, k, v, o = (core.slot(n, KD, T) for n in (1, 2, 3, 0))

    def tile8(slot, quarter):
        return core.area[:, slot, quarter * 1024:(quarter + 1) * 1024].rearrange("p (h t) -> p h t", h=HG)

    kq = core.slot(5, HG, 2, C)
    k_c, q_dec = tile8(5, 2), tile8(5, 3)
    k_old, v_beta, k_left, left_t = (tile8(6, n) for n in range(4))
    strict, upto = tile8(7, 0), tile8(7, 1)
    lower_t, intra = tile8(7, 2), tile8(7, 3)
    X, XT, W, S = (tile8(8, n) for n in range(4))
    Z, Uu = tile8(9, 0), tile8(9, 1)
    total = core.total[:, 0:HG]
    beta, gc, rise, fall = (core.gate_rows[:, i] for i in range(4))
    ident = core.const("ident")
    G = 2
    nlev = len(LEVELS)
    (staged, spread, differ, decayed, ready, gram_ps, gram_sb, left_ps, left_sb, seed_sb, x_ps, x_sb, w_ps, w_sb, xw_ps,
     x_new, xt_ps, xt_new, z_ps, z_sb, u_ps, u_sb, s_ps, s_new, o_ps, o_sb) = core.semaphores(
        "staged", "spread", "differ", "decayed", "ready", "gram_ps", "gram_sb", "left_ps", "left_sb", "seed_sb", "x_ps",
        "x_sb", "w_ps", "w_sb", "xw_ps", "x_new", "xt_ps", "xt_new", "z_ps", "z_sb", "u_ps", "u_sb", "s_ps", "s_new",
        "o_ps", "o_sb")

    def pair(b):
        return core.ps[:, b:b + 2].rearrange("p b (h t) -> p (b h) t", h=4)

    def chunk(t, c):
        return t[:, :, ds(c * C, C)]

    with nc.Block() as block:
        @block.sync
        def _(sp):
            core.clear_before(sp)

        @block.gpsimd
        def _(pool):
            with pool.Fori(0, NC) as c:
                pool.wait_ge(o_ps, c + 1)
                nc.gpsimd.tensor_copy(k_c, chunk(k, c))
                nc.gpsimd.tensor_copy(kq[:, :, 1], chunk(q, c)).then_inc(staged, 1)

        @block.tensor
        def _(pe):
            pe.sem_inc(o_ps, 1)
            with pe.Fori(0, NC) as c:
                pe.wait_ge(s_new, c + 1)
                pe.wait_ge(o_sb, c + 1)
                for n, rows in enumerate((gc, beta, rise, fall)):
                    for h in range(HG):
                        last = nc.tensor.matmul(core.ps[:, 2 * n + h // 4, (h % 4) * C:(h % 4 + 1) * C],
                                                core.const("spread8", HG)[:, h * P:(h + 1) * P], rows[:, ds(c * C, C)],
                                                start=True, stop=True)
                    last.then_inc(spread, 1)
                pe.wait_ge(ready, c + 1)
                pe.wait_ge(staged, c + 1)
                for h in range(HG):
                    bank = core.ps[:, h // 2, (h % 2) * 2 * C:(h % 2 + 1) * 2 * C]
                    last = nc.tensor.matmul(bank, k_c[:, h], kq[:, h].rearrange("p w t -> p (w t)"), start=True, stop=True)
                    if h % 2:
                        last.then_inc(gram_ps, 1)
                for h in range(HG):
                    last = nc.tensor.transpose(core.ps[:, 4 + h // 4, (h % 4) * C:(h % 4 + 1) * C], k_left[:, h], ident)
                last.then_inc(left_ps, 1)
                invert_products(core, pe, c, G, ident, lambda h: lower_t[:, h], X, XT, W, (left_sb, 1), seed_sb,
                                x_ps, x_sb, w_ps, w_sb, xw_ps, x_new, xt_ps, xt_new)
                for h in range(HG):
                    out = core.ps[:, h // 4, (h % 4) * C:(h % 4 + 1) * C]
                    nc.tensor.matmul(out, k_old[:, h], S[:, h], start=True, stop=False)
                    last = nc.tensor.matmul(out, v_beta[:, h], ident, start=False, stop=True)
                last.then_inc(z_ps, 1)
                pe.wait_ge(z_sb, c + 1)
                for h in range(HG):
                    last = nc.tensor.matmul(core.ps[:, 2 + h // 4, (h % 4) * C:(h % 4 + 1) * C], XT[:, h], Z[:, h],
                                            start=True, stop=True)
                last.then_inc(u_ps, 1)
                pe.wait_ge(u_sb, c + 1)
                for h in range(HG):
                    last = nc.tensor.matmul(core.ps[:, 4 + h // 4, (h % 4) * C:(h % 4 + 1) * C], left_t[:, h], Uu[:, h],
                                            start=True, stop=True)
                last.then_inc(s_ps, 1)
                for h in range(HG):
                    out = core.ps[:, 6 + h // 4, (h % 4) * C:(h % 4 + 1) * C]
                    nc.tensor.matmul(out, S[:, h], q_dec[:, h], start=True, stop=False)
                    last = nc.tensor.matmul(out, Uu[:, h], intra[:, h], start=False, stop=True)
                last.then_inc(o_ps, 1)

        @block.scalar
        def _(act):
            act.sem_inc(o_sb, 1)
            with act.Fori(0, NC) as c:
                act.wait_ge(differ, c + 1)
                nc.scalar.activation(upto, upto, ACT.Exp).then_inc(decayed, 1)
                act.wait_ge(left_ps, c + 1)
                nc.scalar.copy(left_t, pair(4)).then_inc(left_sb, 1)
                for g in range(G):
                    act.wait_ge(x_ps, c * G + (g + 1))
                    nc.scalar.copy(X[:, 4 * g:4 * g + 4].rearrange("p h t -> p (h t)"), core.ps[:, g]).then_inc(x_sb, 1)
                act.wait_ge(z_ps, c + 1)
                nc.scalar.copy(Z, pair(0)).then_inc(z_sb, 1)
                act.wait_ge(u_ps, c + 1)
                nc.scalar.copy(Uu, pair(2)).then_inc(u_sb, 1)
                act.wait_ge(o_ps, c + 2)
                nc.scalar.copy(chunk(o, c), pair(6)).then_inc(o_sb, 1)

        @block.vector
        def _(dve):
            nc.vector.memset(S, 0.0).then_inc(s_new, 1)
            with dve.Fori(0, NC) as c:
                dve.wait_ge(spread, c * 4 + 1)
                for h in range(HG):
                    last = nc.vector.tensor_scalar(upto[:, h], pair(0)[:, h], core.gate_cols[:, ds(c * HG + h, 1)], 0.0,
                                                   ALU.subtract, ALU.min)
                last.then_inc(differ, 1)
                dve.wait_ge(spread, c * 4 + 4)
                nc.vector.tensor_tensor(kq[:, :, 0], chunk(k, c), pair(2), ALU.mult)
                nc.vector.tensor_tensor(v_beta, chunk(v, c), pair(2), ALU.mult)
                nc.vector.tensor_tensor(q_dec, chunk(q, c), pair(4), ALU.mult)
                nc.vector.tensor_tensor(k_left, chunk(k, c), pair(6), ALU.mult)
                nc.vector.tensor_copy(total, pair(4)[:, :, C - 1])
                dve.drain()
                for g in range(G):
                    last = nc.vector.scalar_tensor_tensor(k_old[:, 4 * g:4 * g + 4], kq[:, 4 * g:4 * g + 4, 0], -1.0,
                                                          pair(4)[:, 4 * g:4 * g + 4], ALU.mult, ALU.mult)
                last.then_inc(ready, 1)
                dve.wait_ge(decayed, c + 1)
                nc.vector.tensor_tensor(strict, upto, core.const("upper").unsqueeze(1).to_broadcast([P, HG, C]), ALU.mult)
                dve.drain()
                nc.vector.tensor_tensor(upto, upto, core.const("upto").unsqueeze(1).to_broadcast([P, HG, C]), ALU.mult)
                dve.drain()
                for b in range(4):
                    dve.wait_ge(gram_ps, c * 4 + (b + 1))
                    grams = core.ps[:, b].rearrange("p (h w t) -> p h w t", h=2, w=2)
                    nc.vector.tensor_tensor(lower_t[:, 2 * b:2 * b + 2], grams[:, :, 0], strict[:, 2 * b:2 * b + 2], ALU.mult)
                    nc.vector.tensor_tensor(intra[:, 2 * b:2 * b + 2], grams[:, :, 1], upto[:, 2 * b:2 * b + 2],
                                            ALU.mult).then_inc(gram_sb, 1)
                dve.drain()
                invert_updates(core, dve, c, G, lambda g: lower_t[:, 4 * g:4 * g + 4], X, XT, W,
                               seed_sb, x_sb, w_ps, w_sb, xw_ps, x_new, xt_ps, xt_new)
                dve.wait_ge(s_ps, c + 1)
                dve.wait_ge(o_ps, c + 2)
                nc.vector.tensor_tensor(S, S, total.unsqueeze(2).to_broadcast([P, HG, C]), ALU.mult)
                dve.drain()
                nc.vector.tensor_tensor(S, S, pair(4), ALU.add).then_inc(s_new, 1)


def gdn_mixer(core, A):
    nc = core.nc
    gdn_projections(core, A)
    q, k, o, z = (core.slot(n, KD, T) for n in (1, 2, 0, 4))
    head_norms(core, [(q, core.norm_rows[:, 0]), (k, core.norm_rows[:, 1])], 1e-6, 1.0)
    spread_rows(core, [
        (core.norm_rows[:, 0], lambda dve, h, bank: nc.vector.scalar_tensor_tensor(
            q[:, h], q[:, h], float(P) ** -0.5, bank, ALU.mult, ALU.mult)),
        (core.norm_rows[:, 1], lambda dve, h, bank: nc.vector.tensor_tensor(k[:, h], k[:, h], bank, ALU.mult))])
    gdn_chunks(core)
    head_norms(core, [(o, core.norm_rows[:, 0])], 1e-6, 1.0 / P)

    def gate(dve, h, bank):
        nc.vector.scalar_tensor_tensor(o[:, h], o[:, h], core.col("norm_g"), z[:, h], ALU.mult, ALU.mult)
        dve.drain()
        return nc.vector.tensor_tensor(o[:, h], o[:, h], bank, ALU.mult)

    spread_rows(core, [(core.norm_rows[:, 0], gate)])
    y = core.slot(2, KD, T)
    residual(core, 1, 0, A["gdn_w_out"].rearrange("o k n -> (o k) n"), KD, o, y, core.slot(5, 2, KD, P))
    layer_norm(core, y, "ln_g10", "ln_b10")


Q_LORA, KV_LORA, NOPE, ROPE, HM = 384, 256, 128, 64, 4
KQ, KKV = Q_LORA // P, KV_LORA // P
LAT = Q_LORA + KV_LORA
REST = LAT + ROPE
GATES = REST + 4 * 256
RMS_EPS = 1e-6
CQ, CKV, XP, XQK, XV, XO, KR = 0, 3, 5, 7, 9, 11, 13


def normalise_input(core):
    nc = core.nc
    z = core.slot(1, KD, T)
    core.semaphores()
    with nc.Block() as block:
        @block.sync
        def _(sp):
            core.clear_before(sp)

        @block.vector
        def _(dve):
            nc.vector.tensor_copy(z, core.x[:])
    layer_norm(core, z, "ln0_g", "ln0_b")


def layer_projections(core, A, layer):
    nc = core.nc
    x, proj = core.x, core.slot(0, 16, T)
    w = A["w_in_2"][ds(layer, 1)].rearrange("o k n -> (o k) n")

    def keep(first):
        return lambda act, j, banks, s: nc.scalar.copy(proj[:, ds(first + j, 1)].rearrange("p o t -> p (o t)"), banks[0])

    linear(core, lambda j, q: columns(w, j), LAT // P, KD, x, core.slot(4, 5, KD, P), scalar=keep(0), U=5)
    linear(core, lambda j, q: w[:, ds(j * P + REST, P)].rearrange("(k p) m -> p k m", p=P), 8, KD, x,
           core.slot(4, 4, KD, P), scalar=keep(XP), U=4)

    wr, wg = core.slot(4, KD, P), core.slot(5, KD, 2 * HM)
    bias = core.total[0:HM, 0:2]
    li, xf = core.m_rows[:, 0], core.m_rows[:, 1]
    tables = core.slot(3, KD * T)[:, 3 * T:3 * T + CONST.shape[1] - CONST_KEPT]
    loaded, summed = core.semaphores("loaded", "summed")
    with nc.Block() as block:
        @block.sync
        def _(sp):
            core.clear_before(sp)
            for half in range(2):
                sp.dma_start(wr[:, :, half * ROPE:(half + 1) * ROPE],
                             w[:, LAT:REST].rearrange("(k p) m -> p k m", p=P)).then_inc(loaded, 16)
            sp.dma_start(wg, w[:, GATES:GATES + 2 * HM].rearrange("(k p) m -> p k m", p=P)).then_inc(loaded, 16)
            for n, name in enumerate(("b_i_2", "b_f_2")):
                sp.dma_start(bias[:, n:n + 1], A[name][ds(layer, 1)].rearrange("o h -> h o")).then_inc(loaded, 16)
            sp.dma_start(tables, core.const_dram[:, CONST_KEPT:CONST.shape[1]]).then_inc(loaded, 16)
            sp.wait_ge(loaded, 96)

        @block.tensor
        def _(pe):
            pe.wait_ge(loaded, 96)
            for k in range(KD):
                nc.tensor.matmul(core.ps[:, 0], wr[:, k], x[:, k], start=k == 0, stop=k == KD - 1)
            for q in range(2):
                for k in range(KD):
                    last = nc.tensor.matmul(core.ps[0:HM, 1 + q], wg[:, k, q * HM:(q + 1) * HM], x[:, k],
                                            start=k == 0, stop=k == KD - 1)
            last.then_inc(summed, 1)

        @block.scalar
        def _(act):
            act.wait_ge(summed, 1)
            nc.scalar.copy(proj[:, KR], core.ps[:, 0])

        @block.vector
        def _(dve):
            dve.wait_ge(summed, 1)
            nc.vector.tensor_scalar(li, core.ps[0:HM, 1], bias[:, 0:1], None, ALU.add)
            nc.vector.tensor_scalar(xf, core.ps[0:HM, 2], bias[:, 1:2], None, ALU.add)


def table(core, name):
    at, n = CONST_AT[name]
    return core.slot(3, KD * T)[:, 3 * T + at - CONST_KEPT:3 * T + at - CONST_KEPT + n]


def latent_heads(core, A, layer):
    nc = core.nc
    proj = core.slot(0, 16, T)
    wq, wkv = core.slot(4, KQ, HM * (NOPE + ROPE)), core.slot(5, KKV, HM * 2 * NOPE)
    v = core.slot(5, KD * T)[:, 2048:4096].rearrange("p (a n) -> p a n", a=4)
    qn, kn = core.slot(2, HM, T), core.slot(2, KD, T)[:, HM:2 * HM]
    qp, kp = core.slot(3, 2, T), core.slot(3, KD, T)[:, 2]
    sq = core.slot(9, 2, T)
    rstd = core.slot(9, KD, T)[:, 2:4]
    scale = float((NOPE + ROPE) ** -0.5)
    (loaded, squared, square_used, floored, rooted, normed, q_ps, q_out, kv_ps, kv_out, v_ps, v_out, raw, turned,
     turned_used) = core.semaphores(
        "loaded", "squared", "square_used", "floored", "rooted", "normed", "q_ps", "q_out", "kv_ps", "kv_out", "v_ps",
        "v_out", "raw", "turned", "turned_used")
    latents = ((CQ, KQ, "g_qn", 1.0 / Q_LORA), (CKV, KKV, "g_kvn", 1.0 / KV_LORA))
    rotary = (qp[:, 0], qp[:, 1], kp)
    with nc.Block() as block:
        @block.sync
        def _(sp):
            core.clear_before(sp)
            sp.dma_start(wq, A["w_uq_2"][ds(layer, 1)].rearrange("o (k p) n -> p (o k) n", p=P)).then_inc(loaded, 16)
            sp.dma_start(wkv, A["w_ukv_2"][ds(layer, 1)].rearrange("o (k p) n -> p (o k) n", p=P)).then_inc(loaded, 16)

        @block.scalar
        def _(act):
            n = 0
            for first, kt, g, mean in latents:
                for k in range(kt):
                    if n >= 2:
                        act.wait_ge(square_used, n - 1)
                    nc.scalar.activation(sq[:, n % 2], proj[:, first + k], ACT.Square).then_inc(squared, 1)
                    n += 1
            for i in range(2):
                act.wait_ge(floored, i + 1)
                nc.scalar.activation(rstd[:, i], rstd[:, i], ACT.Sqrt).then_inc(rooted, 1)
            for h in range(HM):
                act.wait_ge(q_ps, h + 1)
                nc.scalar.mul(qn[:, h], core.ps[:, 2 + h % 2], scale).then_inc(q_out, 1)
            for j in range(2):
                act.wait_ge(q_ps, HM + j + 1)
                nc.scalar.mul(qp[:, j], core.ps[:, 2 + j], scale).then_inc(q_out, 1)
            for h in range(HM):
                act.wait_ge(kv_ps, h + 1)
                nc.scalar.copy(kn[:, h], core.ps[:, 4 + h % 2]).then_inc(kv_out, 1)
            for a in range(4):
                act.wait_ge(v_ps, a + 1)
                nc.scalar.copy(v[:, a], core.ps[:, 6 + a % 2]).then_inc(v_out, 1)

        @block.tensor
        def _(pe):
            n = 0
            for i, (first, kt, g, mean) in enumerate(latents):
                for k in range(kt):
                    pe.wait_ge(squared, n + 1)
                    nc.tensor.matmul(core.ps[:, i], core.const("ones"), sq[:, n % 2], start=k == 0,
                                     stop=k == kt - 1).then_inc(square_used, 1)
                    n += 1
            pe.wait_ge(loaded, 32)
            pe.wait_ge(normed, KQ)
            for h in range(HM):
                if h >= 2:
                    pe.wait_ge(q_out, h - 1)
                for k in range(KQ):
                    last = nc.tensor.matmul(core.ps[:, 2 + h % 2], wq[:, k, h * (NOPE + ROPE):h * (NOPE + ROPE) + NOPE],
                                            proj[:, CQ + k], start=k == 0, stop=k == KQ - 1)
                last.then_inc(q_ps, 1)
            for j in range(2):
                pe.wait_ge(q_out, HM - 1 + j)
                for half in range(2):
                    at = (2 * j + half) * (NOPE + ROPE) + NOPE
                    for k in range(KQ):
                        last = nc.tensor.matmul(core.ps[half * ROPE:(half + 1) * ROPE, 2 + j], wq[:, k, at:at + ROPE],
                                                proj[:, CQ + k], start=k == 0, stop=k == KQ - 1)
                last.then_inc(q_ps, 1)
            pe.wait_ge(normed, KQ + KKV)
            for h in range(HM):
                if h >= 2:
                    pe.wait_ge(kv_out, h - 1)
                for k in range(KKV):
                    last = nc.tensor.matmul(core.ps[:, 4 + h % 2], wkv[:, k, h * 2 * NOPE:h * 2 * NOPE + NOPE],
                                            proj[:, CKV + k], start=k == 0, stop=k == KKV - 1)
                last.then_inc(kv_ps, 1)
            values = wkv.rearrange("p k (h m) -> p k h m", h=HM)
            for a in range(4):
                if a >= 2:
                    pe.wait_ge(v_out, a - 1)
                for k in range(KKV):
                    last = nc.tensor.matmul(core.ps[:, 6 + a % 2], proj[:, CKV + k, a * P:(a + 1) * P],
                                            values[:, k, :, NOPE:2 * NOPE], start=k == 0, stop=k == KKV - 1)
                last.then_inc(v_ps, 1)
            for i, t in enumerate((qp[:, 0], qp[:, 1], proj[:, KR])):
                if i < 2:
                    pe.wait_ge(q_out, HM + i + 1)
                else:
                    pe.wait_ge(turned_used, 1)
                nc.tensor.matmul(core.ps[:, i % 2], table(core, "turn"), t, start=True, stop=True).then_inc(turned, 1)

        @block.vector
        def _(dve):
            n = 0
            for i, (first, kt, g, mean) in enumerate(latents):
                n += kt
                dve.wait_ge(square_used, n)
                nc.vector.tensor_scalar(rstd[:, i], core.ps[:, i], mean, RMS_EPS, ALU.mult, ALU.add).then_inc(floored, 1)
            for i, (first, kt, g, mean) in enumerate(latents):
                dve.wait_ge(rooted, i + 1)
                nc.vector.reciprocal(rstd[:, i], rstd[:, i])
                dve.drain()
                for k in range(kt):
                    nc.vector.scalar_tensor_tensor(proj[:, first + k], proj[:, first + k], core.col(g, k), rstd[:, i],
                                                   ALU.mult, ALU.mult).then_inc(normed, 1)
            for i, (t, out) in enumerate(((qp[:, 0], qp[:, 0]), (qp[:, 1], qp[:, 1]), (proj[:, KR], kp))):
                dve.wait_ge(turned, i + 1)
                nc.vector.tensor_tensor(proj[:, 14], core.ps[:, i % 2], table(core, "sin"), ALU.mult).then_inc(turned_used, 1)
                nc.vector.tensor_tensor(proj[:, 15], t, table(core, "cos"), ALU.mult)
                dve.drain()
                nc.vector.tensor_tensor(out, proj[:, 14], proj[:, 15], ALU.add)
                dve.drain()


def latent_attention(core):
    nc = core.nc
    v = core.slot(5, KD * T)[:, 2048:4096].rearrange("p (a n) -> p a n", a=4)
    qn, kn = core.slot(2, HM, T), core.slot(2, KD, T)[:, HM:2 * HM]
    qp, kp = core.slot(3, 2, T), core.slot(3, KD, T)[:, 2]
    prob, prob_t = core.slot(6, 2, T), core.slot(6, KD, T)[:, 2:4]
    out = core.slot(7, KD, T)
    small = core.mid[:]
    items = [(h, a) for h in range(HM) for a in range(4)]
    (s_ps, masked, peak, risen, weighed, t_ps, t_out, o_ps, o_out) = core.semaphores(
        "s_ps", "masked", "peak", "risen", "weighed", "t_ps", "t_out", "o_ps", "o_out")
    with nc.Block() as block:
        @block.sync
        def _(sp):
            core.clear_before(sp)

        @block.tensor
        def _(pe):
            def scores(n):
                h, a = items[n]
                lo, end = 64 * (h % 2), (a + 1) * P
                if n >= 2:
                    pe.wait_ge(risen, n - 1)
                bank = core.ps[:, n % 2, 0:end]
                nc.tensor.matmul(bank, qn[:, h, a * P:end], kn[:, h, 0:end], start=True, stop=False)
                nc.tensor.matmul(bank, qp[lo:lo + 64, h // 2, a * P:end], kp[lo:lo + 64, 0:end], start=False,
                                 stop=True).then_inc(s_ps, 1)

            def values(n):
                h, a = items[n]
                pe.wait_ge(weighed, n + 1)
                if n >= 2:
                    pe.wait_ge(t_out, n - 1)
                for b in range(a + 1):
                    last = nc.tensor.transpose(core.ps[:, 2 + n % 2, b * P:(b + 1) * P], prob[:, n % 2, b * P:(b + 1) * P],
                                               core.const("ident"))
                last.then_inc(t_ps, 1)
                pe.wait_ge(t_out, n + 1)
                if n >= 2:
                    pe.wait_ge(o_out, n - 1)
                for b in range(a + 1):
                    last = nc.tensor.matmul(core.ps[:, 4 + n % 2, 0:P], v[:, b, h * NOPE:(h + 1) * NOPE],
                                            prob_t[:, n % 2, b * P:(b + 1) * P], start=b == 0, stop=b == a)
                last.then_inc(o_ps, 1)

            scores(0)
            for n in range(len(items)):
                if n + 1 < len(items):
                    scores(n + 1)
                values(n)

        @block.vector
        def _(dve):
            for n, (h, a) in enumerate(items):
                end = (a + 1) * P
                bank = core.ps[:, n % 2]
                top, total, part = (small[:, 3 * (n % 2) + i:3 * (n % 2) + i + 1] for i in range(3))
                dve.wait_ge(s_ps, n + 1)
                nc.vector.tensor_tensor(bank[:, a * P:end], bank[:, a * P:end], table(core, "later"), ALU.add)
                dve.drain()
                nc.vector.tensor_reduce(top, bank[:, 0:end], AX_X, ALU.max, negate=True).then_inc(peak, 1)
                dve.wait_ge(risen, n + 1)
                nc.vector.reciprocal(part, total)
                dve.drain()
                nc.vector.tensor_scalar(prob[:, n % 2, 0:end], prob[:, n % 2, 0:end], part, None,
                                        ALU.mult).then_inc(weighed, 1)

        @block.scalar
        def _(act):
            for n, (h, a) in enumerate(items):
                end = (a + 1) * P
                top, total = (small[:, 3 * (n % 2) + i:3 * (n % 2) + i + 1] for i in range(2))
                act.wait_ge(peak, n + 1)
                if n >= 2:
                    act.wait_ge(t_ps, n - 1)
                nc.scalar.activation(prob[:, n % 2, 0:end], core.ps[:, n % 2, 0:end], ACT.Exp, bias=top,
                                     accum_out=total).then_inc(risen, 1)
                act.wait_ge(t_ps, n + 1)
                if n >= 2:
                    act.wait_ge(o_ps, n - 1)
                nc.scalar.copy(prob_t[:, n % 2, 0:end], core.ps[:, 2 + n % 2, 0:end]).then_inc(t_out, 1)
                act.wait_ge(o_ps, n + 1)
                nc.scalar.copy(out[:, h, a * P:end], core.ps[:, 4 + n % 2, 0:P]).then_inc(o_out, 1)


def pool_and_prepare(core, A, layer):
    nc = core.nc
    proj, out = core.slot(0, 16, T), core.slot(7, KD, T)
    sums = core.slot(4, 4, T)
    weights = core.slot(5, KD * T)[:, 0:6 * 64].rearrange("p (w k m) -> p w k m", w=3, k=2)
    conv, q, k = core.slot(8, 2, T), core.slot(8, KD, T)[:, 2:4], core.slot(8, KD, T)[:, 4:6]
    v = core.slot(8, KD * T)[:, 6 * T:6 * T + 4 * 256].rearrange("p (a n) -> p a n", a=4)
    li, xf, soft, B, F, M, floor = (core.m_rows[:, i] for i in range(7))
    ones_row = core.slot(6, KD * T)[0:HM, 7 * T:8 * T]
    (loaded, convolved, activated, pooled, p_ps, qk_ps, qk_out, v_ps, soft_done, rows_done, floor_done,
     cols_ps) = core.semaphores(
        "loaded", "convolved", "activated", "pooled", "p_ps", "qk_ps", "qk_out", "v_ps", "soft_done", "rows_done",
        "floor_done", "cols_ps")
    with nc.Block() as block:
        @block.sync
        def _(sp):
            core.clear_before(sp)
            for w, name in enumerate(("w_pool_2", "w_mq_2", "w_mk_2")):
                for lo in range(2):
                    for t in range(2):
                        sp.dma_start(weights[64 * lo:64 * lo + 64, w, t],
                                     A[name][ds(layer, 1), 2 * t + lo].rearrange("o c m -> (o c) m")).then_inc(loaded, 16)

        @block.vector
        def _(dve):
            for t in range(2):
                tap = lambda j: core.col("w_mconv", j * 2 + t)
                causal_conv(nc, dve, conv[:, t], proj[:, XQK + t], tap, TAPS).then_inc(convolved, 1)
            nc.vector.memset(ones_row, 1.0)
            nc.vector.tensor_scalar(F, xf, 0.0, None, ALU.min)
            dve.wait_ge(soft_done, 1)
            dve.drain()
            nc.vector.tensor_tensor(xf, F, soft, ALU.subtract)
            dve.drain()
            nc.vector.tensor_tensor_scan(B, ones_row, xf, 0.0, ALU.mult, ALU.add)
            dve.drain()
            nc.vector.tensor_tensor(F, li, B, ALU.subtract)
            dve.drain()
            nc.vector.tensor_tensor_scan(M, F, F, 0.0, ALU.max, ALU.max)
            dve.drain()
            nc.vector.tensor_tensor(floor, B, M, ALU.add).then_inc(rows_done, 1)
            for t in range(2):
                x = proj[:, XP + t]
                src = x
                at = 0
                for step in range(2 * t + 2):
                    lo = 64 if step == 2 * t + 1 else 0
                    dst, shift = sums[:, at % 4], 1 << step
                    if lo:
                        nc.vector.tensor_copy(dst[0:64], src[0:64])
                    nc.vector.tensor_copy(dst[lo:P, 0:shift], src[lo:P, 0:shift])
                    nc.vector.tensor_tensor(dst[lo:P, shift:T], src[lo:P, shift:T], src[lo:P, 0:T - shift], ALU.add)
                    dve.drain()
                    src = dst
                    at += 1
                nc.vector.tensor_tensor(src, src, table(core, f"count{t}"), ALU.mult)
                dve.drain()
                nc.vector.tensor_tensor(x, src, x, ALU.subtract).then_inc(pooled, 1)
                dve.drain()
            for t in range(2):
                dve.wait_ge(p_ps, t + 1)
                nc.vector.tensor_scalar(out[:, HM + t], core.ps[:, t], core.col("s_pool", t), None, ALU.mult)
            dve.wait_ge(cols_ps, 1)
            nc.vector.tensor_copy(core.first[:, 0:4 * HM], core.ps[:, 6, 0:4 * HM])

        @block.scalar
        def _(act):
            nc.scalar.activation(soft, xf, ACT.Abs)
            act.drain()
            nc.scalar.activation(soft, soft, ACT.Exp, scale=-1.0)
            act.drain()
            nc.scalar.activation(soft, soft, ACT.Ln, bias=1.0).then_inc(soft_done, 1)
            for t in range(2):
                act.wait_ge(convolved, t + 1)
                nc.scalar.activation(conv[:, t], conv[:, t], ACT.Silu, bias=core.col("b_mconv", t)).then_inc(activated, 1)
            for t in range(2):
                act.wait_ge(qk_ps, t + 1)
                nc.scalar.copy(q[:, t], core.ps[:, 2 + t])
                nc.scalar.mul(k[:, t], core.ps[:, 4 + t], 64.0 ** -0.5).then_inc(qk_out, 1)
            for a in range(2):
                act.wait_ge(v_ps, a + 1)
                nc.scalar.copy(v[:, 2 * a:2 * a + 2].rearrange("p a n -> p (a n)"), core.ps[:, 7 - 5 * a])
            act.wait_ge(rows_done, 1)
            nc.scalar.activation(floor, floor, ACT.Exp, scale=-1.0).then_inc(floor_done, 1)

        @block.tensor
        def _(pe):
            pe.wait_ge(loaded, 12 * 16)
            for t in range(2):
                pe.wait_ge(activated, t + 1)
                for w in (1, 2):
                    for lo in (0, 64):
                        last = nc.tensor.matmul(core.ps[lo:lo + 64, 2 * w + t], weights[lo:lo + 64, w, t],
                                                conv[lo:lo + 64, t], start=True, stop=True)
                last.then_inc(qk_ps, 1)
            pe.wait_ge(qk_out, 2)
            for a in range(4):
                for t in range(2):
                    bank = core.ps[:, 7 - 5 * (a // 2)]
                    at = (a % 2) * 256 + t * P
                    last = nc.tensor.transpose(bank[:, at:at + P], proj[:, XV + t, a * P:(a + 1) * P], core.const("ident"))
                if a % 2:
                    last.then_inc(v_ps, 1)
            pe.wait_ge(rows_done, 1)
            for a in range(4):
                last = nc.tensor.transpose(core.ps[:, 6, a * HM:(a + 1) * HM], F[:, a * P:(a + 1) * P],
                                           core.const("ident", HM)[:, 0:HM])
            last.then_inc(cols_ps, 1)
            for t in range(2):
                pe.wait_ge(pooled, t + 1)
                for lo in (0, 64):
                    last = nc.tensor.matmul(core.ps[lo:lo + 64, t], weights[lo:lo + 64, 0, t],
                                            proj[lo:lo + 64, XP + t], start=True, stop=True)
                last.then_inc(p_ps, 1)


def mlstm(core):
    nc = core.nc
    proj, out = core.slot(0, 16, T), core.slot(7, KD, T)
    q, k = core.slot(8, KD, T)[:, 2:4], core.slot(8, KD, T)[:, 4:6]
    v = core.slot(8, KD * T)[:, 6 * T:6 * T + 4 * 256].rearrange("p (a n) -> p a n", a=4)
    M, floor, den = core.m_rows[:, 5], core.m_rows[:, 6], core.m_rows[:, 2]
    weight, gram = core.slot(4, 2, T), core.slot(4, KD, T)[:, 2:4]
    sq, rstd = core.slot(4, KD, T)[:, 4:6], core.slot(4, KD, T)[:, 6:8]
    items = [(h, a) for h in range(HM) for a in range(4)]
    (m_ps, s_ps, differ, risen, weighed, used, den_abs, den_done, den_ps, centred_ps, centred,
     squared, var_ps, floored, rooted, opened) = core.semaphores(
        "m_ps", "s_ps", "differ", "risen", "weighed", "used", "den_abs", "den_done", "den_ps",
        "centred_ps", "centred", "squared", "var_ps", "floored", "rooted", "opened")
    with nc.Block() as block:
        @block.sync
        def _(sp):
            core.clear_before(sp)

        @block.tensor
        def _(pe):
            def scores(n):
                h, a = items[n]
                lo = 64 * (h % 2)
                if a == 0:
                    if h >= 2:
                        pe.wait_ge(differ, 4 * (h - 1))
                    nc.tensor.matmul(core.ps[:, h % 2], core.const("spread8", HM)[:, h * P:(h + 1) * P], M,
                                     start=True, stop=True).then_inc(m_ps, 1)
                if n >= 2:
                    pe.wait_ge(weighed, n - 1)
                nc.tensor.matmul(core.ps[:, 2 + n % 2, a * P:T], k[lo:lo + 64, h // 2, a * P:(a + 1) * P],
                                 q[lo:lo + 64, h // 2, a * P:T], start=True, stop=True).then_inc(s_ps, 1)

            def values(n):
                h, a = items[n]
                lo = 64 * (h % 2)
                pe.wait_ge(weighed, n + 1)
                g = gram[:, n % 2, a * P:T]
                nc.tensor.matmul(core.ps[lo:lo + 64, 4 + h // 2, a * P:T], v[:, a, h * 64:(h + 1) * 64], g,
                                 start=a == 0, stop=a == 3, skip_group_check=True)
                nc.tensor.matmul(core.ps[0:HM, 6, a * P:T], core.const("pick8")[:, HG - 1 - h:HG - 1 - h + HM], g,
                                 start=n == 0, stop=n == len(items) - 1, skip_group_check=True).then_inc(used, 1)

            scores(0)
            for n in range(len(items)):
                if n + 1 < len(items):
                    scores(n + 1)
                values(n)
            pe.wait_ge(den_done, 1)
            for t in range(2):
                nc.tensor.matmul(core.ps[:, t], core.const("spread16", HM)[:, t * P:(t + 1) * P], den, start=True,
                                 stop=True).then_inc(den_ps, 1)
            for t in range(2):
                pe.wait_ge(den_abs, 2 + t)
                nc.tensor.matmul(core.ps[:, 2 + t], core.const("head64"), out[:, 6 + t], start=True,
                                 stop=True).then_inc(centred_ps, 1)
            for t in range(2):
                pe.wait_ge(squared, t + 1)
                nc.tensor.matmul(core.ps[:, 4 + t], core.const("head64"), sq[:, t], start=True,
                                 stop=True).then_inc(var_ps, 1)

        @block.vector
        def _(dve):
            def weigh(n):
                h, a = items[n]
                dve.wait_ge(s_ps, n + 1)
                dve.wait_ge(risen, n + 1)
                if n >= 2:
                    dve.wait_ge(used, n - 1)
                w, g = weight[:, n % 2], gram[:, n % 2]
                nc.vector.tensor_tensor(w[:, a * P:(a + 1) * P], w[:, a * P:(a + 1) * P], core.const("upto"), ALU.mult)
                dve.drain()
                nc.vector.tensor_tensor(g[:, a * P:T], core.ps[:, 2 + n % 2, a * P:T], w[:, a * P:T],
                                        ALU.mult).then_inc(weighed, 1)

            for n, (h, a) in enumerate(items):
                dve.wait_ge(m_ps, h + 1)
                if n >= 2:
                    dve.wait_ge(weighed, n - 1)
                w = weight[:, n % 2, a * P:T]
                nc.vector.tensor_scalar(w, core.ps[:, h % 2, a * P:T], core.first[:, a * HM + h:a * HM + h + 1], 0.0,
                                        ALU.subtract, ALU.max).then_inc(differ, 1)
                if n >= 1:
                    weigh(n - 1)
            weigh(len(items) - 1)
            dve.wait_ge(den_abs, 1)
            nc.vector.tensor_tensor(den, den, floor, ALU.max)
            dve.drain()
            nc.vector.reciprocal(den, den).then_inc(den_done, 1)
            for t in range(2):
                dve.wait_ge(den_ps, t + 1)
                nc.vector.tensor_copy(rstd[:, t], core.ps[:, t])
                dve.drain()
                nc.vector.tensor_tensor(out[:, 6 + t], core.ps[:, 4 + t], rstd[:, t], ALU.mult).then_inc(den_abs, 1)
            for t in range(2):
                dve.wait_ge(centred_ps, t + 1)
                dve.drain()
                nc.vector.scalar_tensor_tensor(out[:, 6 + t], core.ps[:, 2 + t], -1.0 / 64, out[:, 6 + t], ALU.mult,
                                               ALU.add).then_inc(centred, 1)
            for t in range(2):
                dve.wait_ge(var_ps, t + 1)
                nc.vector.tensor_scalar(rstd[:, t], core.ps[:, 4 + t], 1.0 / 64, LN_EPS, ALU.mult,
                                        ALU.add).then_inc(floored, 1)
            for t in range(2):
                dve.wait_ge(rooted, t + 1)
                nc.vector.reciprocal(rstd[:, t], rstd[:, t])
                dve.drain()
                nc.vector.scalar_tensor_tensor(out[:, 6 + t], out[:, 6 + t], core.col("g_mh", t), rstd[:, t], ALU.mult,
                                               ALU.mult)
                dve.drain()
                dve.wait_ge(opened, t + 1)
                nc.vector.tensor_tensor(out[:, 6 + t], out[:, 6 + t], proj[:, XO + t], ALU.mult)

        @block.scalar
        def _(act):
            for n, (h, a) in enumerate(items):
                act.wait_ge(differ, n + 1)
                nc.scalar.activation(weight[:, n % 2, a * P:T], weight[:, n % 2, a * P:T], ACT.Exp,
                                     scale=-1.0).then_inc(risen, 1)
            act.wait_ge(used, len(items))
            nc.scalar.activation(den, core.ps[0:HM, 6], ACT.Abs).then_inc(den_abs, 1)
            for t in range(2):
                act.wait_ge(centred, t + 1)
                nc.scalar.activation(sq[:, t], out[:, 6 + t], ACT.Square).then_inc(squared, 1)
            for t in range(2):
                act.wait_ge(floored, t + 1)
                nc.scalar.activation(rstd[:, t], rstd[:, t], ACT.Sqrt).then_inc(rooted, 1)
            for t in range(2):
                nc.scalar.activation(proj[:, XO + t], proj[:, XO + t], ACT.Sigmoid).then_inc(opened, 1)


def store_output(core, out):
    nc = core.nc
    rows = core.slot(0, 4, D)
    turned, copied, stored = core.semaphores("turned", "copied", "stored")
    with nc.Block() as block:
        @block.sync
        def _(sp):
            core.clear_before(sp)
            for a in range(4):
                sp.wait_ge(copied, 2 * (a + 1))
                sp.dma_start(out[0, a * P:(a + 1) * P, :], rows[:, a]).then_inc(stored, 16)
            sp.wait_ge(stored, 64)

        @block.tensor
        def _(pe):
            for a in range(4):
                for half in range(2):
                    n = 2 * a + half
                    if n >= 4:
                        pe.wait_ge(copied, n - 3)
                    for j in range(4):
                        last = nc.tensor.transpose(core.ps[:, n % 4, j * P:(j + 1) * P],
                                                   core.x[:, 4 * half + j, a * P:(a + 1) * P], core.const("ident"))
                    last.then_inc(turned, 1)

        @block.vector
        def _(dve):
            for n in range(8):
                dve.wait_ge(turned, n + 1)
                nc.vector.tensor_copy(rows[:, n // 2, (n % 2) * 512:(n % 2 + 1) * 512], core.ps[:, n % 4]).then_inc(copied, 1)


def network(nc, A, const, out, stop=None):
    with ExitStack() as ctx:
        core = Core(nc, ctx, const)
        core.lora_inner = core.sb("lora_inner", [P, 3, T])
        core.mid, core.first, core.ends = (core.sb(n, [P, KD * NC]) for n in ("mid", "first", "ends"))
        core.bonus = core.sb("bonus", [HR, T])
        core.gate_rows = core.slot(9, KD, T)[0:HG, 4:8]
        core.gate_cols, core.total = core.first, core.mid
        core.norm_rows = core.lora_inner[0:HG]
        core.one_less_k_a = core.sb("one_less_k_a", [P, KD])

        def rows(ap, pattern, **sizes):
            return ap.rearrange(pattern, **sizes)

        def vec(name, layer=0):
            return A[name][layer:layer + 1].rearrange("o (r p) -> (o r) p", p=P)

        groups = [
            [("ada_b0", vec("ada_b", 0))] +
            [(f"ln_g{i}{j}", A["ln_g"][i, j:j + 1].rearrange("o (r p) -> (o r) p", p=P)) for i in range(2) for j in range(2)] +
            [(f"ln_b{i}{j}", A["ln_b"][i, j:j + 1].rearrange("o (r p) -> (o r) p", p=P)) for i in range(2) for j in range(2)] +
            [("c", vec("c"))],
            [("ada_b1", vec("ada_b", 1)), ("mu", A["rwkv_mu"].rearrange("o i (r p) -> (o i r) p", p=P))] +
            [(n, vec("rwkv_" + n)) for n in ("w0", "a0", "k_k", "k_a")],
            [("r_k", A["rwkv_r_k"].rearrange("o (r a) n -> (o r) (a n)", a=2))] +
            [(n, vec("rwkv_" + n)) for n in ("gn_g", "gn_b")] +
            [("conv", A["gdn_conv"].rearrange("o i (r p) -> (o i r) p", p=P)), ("norm_g", A["gdn_norm_g"])],
            [("ln0_g", A["ln0_g_2"].rearrange("(r p) -> r p", p=P)), ("ln0_b", A["ln0_b_2"].rearrange("(r p) -> r p", p=P))],
        ]
        turn_rows(core, [(core.const_sb[:], const[:, 0:CONST_KEPT])], groups)
        load_x(core, A["x"])
        modulation(core, 0, A["ada_w"])
        one_less(core)
        rwkv_projections(core, A)
        rwkv_decays(core)
        rwkv_chunks(core)
        rwkv_output(core, A)
        u = core.slot(0, KD, T)
        modulate(core, 0, 1, u)
        feed_forward(core, 0, u, core.slot(2, KF, T), core.slot(6, 4, KD, P), A["ffn_w_in"][0], A["ffn_w_out"][0],
                     core.slot(1, KD, T))
        layer_norm(core, core.slot(1, KD, T), "ln_g01", "ln_b01")
        modulation(core, 1, A["ada_w"])
        gdn_mixer(core, A)
        modulate(core, 1, 1, u)
        feed_forward(core, 1, u, core.slot(2, KF, T), core.slot(6, 4, KD, P), A["ffn_w_in"][1], A["ffn_w_out"][1],
                     core.slot(1, KD, T))
        layer_norm(core, core.slot(1, KD, T), "ln_g11", "ln_b11")

        normalise_input(core)
        core.m_rows = core.slot(6, KD, T)[0:HM]
        core.clear_all()
        with nc.Fori(0, 2) as layer:
            core.n_cols = 0

            def of_layer(name, pattern="o (r p) -> (o r) p"):
                return A[name + "_2"][ds(layer, 1)].rearrange(pattern, p=P)

            turn_rows(core, [], [
                [(n, of_layer(n)) for n in ("g_qn", "g_kvn", "s_pool", "b_mconv", "g_mh", "ln1_g", "ln1_b", "ln2_g", "ln2_b")] +
                [("w_mconv", of_layer("w_mconv", "o i (r p) -> (o i r) p"))],
                [("w_fconv", of_layer("w_fconv", "o i (r p) -> (o i r) p")), ("b_fconv", of_layer("b_fconv"))],
            ])
            layer_projections(core, A, layer)
            latent_heads(core, A, layer)
            pool_and_prepare(core, A, layer)
            mlstm(core)
            latent_attention(core)
            z = core.slot(1, KD, T)
            residual(core, None, 0, A["w_out_2"][ds(layer, 1)].rearrange("o k n -> (o k) n"), KD, core.slot(7, KD, T),
                     z, core.slot(4, 2, KD, P))
            layer_norm(core, z, "ln1_g", "ln1_b")
            feed_forward(core, None, core.x, core.slot(2, KF, T), core.slot(6, 4, KD, P),
                         A["w_up_2"][ds(layer, 1)].rearrange("o k n -> (o k) n"),
                         A["w_down_2"][ds(layer, 1)].rearrange("o k n -> (o k) n"), z, gate_first=False,
                         conv=(core.col_at["w_fconv"], core.col_at["b_fconv"], 3))
            layer_norm(core, z, "ln2_g", "ln2_b")
            core.clear_all()
        store_output(core, out)


def one_less(core):
    nc = core.nc
    core.semaphores()
    with nc.Block() as block:
        @block.sync
        def _(sp):
            core.clear_before(sp)

        @block.vector
        def _(dve):
            nc.vector.tensor_scalar(core.one_less_k_a[:], core.col("k_a", 0, KD), -1.0, 1.0, ALU.mult, ALU.add)


_OUTS = [((1, T, D), "float32")]


def kernel(**inputs):
    import concourse.bacc as _bacc
    from concourse.bass_utils import run_bass_kernel_spmd as _run

    nc = _bacc.Bacc("TRN2", target_bir_lowering=False, num_devices=1)
    arrays, A = {}, {}
    for name, value in inputs.items():
        if name.split("_")[0] in ("diff", "swa"):
            continue
        a = np.ascontiguousarray(value)
        arrays[f"in_{name}_dram"] = a
        A[name] = nc.dram_tensor(f"in_{name}_dram", a.shape, mybir.dt.from_np(a.dtype), kind="ExternalInput").ap()
    arrays["const_dram"] = CONST
    const = nc.dram_tensor("const_dram", CONST.shape, F32, kind="ExternalInput").ap()
    shape, dtype = _OUTS[0]
    out = nc.dram_tensor("out_0_dram", shape, mybir.dt.from_np(np.dtype(dtype)), kind="ExternalOutput").ap()
    network(nc, A, const, out)
    r = _run(nc, [arrays], core_ids=[0])
    return r.results[0]["out_0_dram"]
```

```python
from contextlib import ExitStack

import concourse.bass as bass
import numpy as np
from concourse import mybir

F32 = mybir.dt.float32
F32R = mybir.dt.float32r
U32 = mybir.dt.uint32
ALU = mybir.AluOpType
ACT = mybir.ActivationFunctionType
AX_X = mybir.AxisListType.X
ds = bass.ds

P = 128
T = 512
D = 1024
KD = D // P
FF = 2816
KF = FF // P
C = 128
NC = T // C
ALPHA = 4.0 ** 0.25
LN_EPS = 1e-5
LEVELS = (2, 4, 8, 16, 32, 64)


def constants():
    i = np.arange(P)[:, None]
    j = np.arange(P)[None, :]
    parts = {
        "ident": np.eye(P),
        "ones": np.ones((P, P)),
        "head64": (i // 64 == j // 64) * 1.0,
        "upper": (i < j) * 1.0,
        "upto": (i <= j) * 1.0,
        "corner1": ((j % 2 == 1) & (i == j - 1)) * 1.0,
    }
    for b in LEVELS:
        parts[f"corner{b}"] = (((i // b) % 2 == 1) & (j // b == i // b - 1)) * 1.0
    parts["heads16"] = np.concatenate(
        [np.stack([(np.arange(P) // 64 + 2 * p == h) for h in range(16)], 1) for p in range(8)], 1) * 1.0
    spread16 = np.zeros((P, 8 * P))
    for p in range(8):
        for m in range(P):
            spread16[2 * p + m // 64, p * P + m] = 1.0
    parts["spread16"] = spread16
    spread8 = np.zeros((P, 8 * P))
    for h in range(8):
        spread8[h, h * P:(h + 1) * P] = 1.0
    parts["spread8"] = spread8
    parts["pick8"] = np.broadcast_to((np.arange(15) == 7) * 1.0, (P, 15))
    parts["carry"] = np.broadcast_to((np.arange(T) % C != 0) * 1.0, (P, T))
    inv = 1.0 / (10000.0 ** (np.arange(0, 64, 2, dtype=np.float32) / np.float32(64)))
    angle = np.arange(T, dtype=np.float32)[:, None] * inv.astype(np.float32)[None, :]
    parts["cos"] = np.tile(np.cos(angle).T, (4, 1))
    parts["sin"] = np.tile(np.sin(angle).T, (4, 1))
    turn = np.zeros((P, P))
    for m in range(P):
        turn[m + 32 if m % 64 < 32 else m - 32, m] = -1.0 if m % 64 < 32 else 1.0
    parts["turn"] = turn
    t = np.arange(T)
    for g in range(2):
        w = np.where(np.arange(P) < 64, 2 ** (2 * g + 1), 2 ** (2 * g + 2))[:, None]
        parts[f"count{g}"] = 1.0 / np.minimum(t[None, :] + 1, w)
    parts["later"] = (j > i) * -1e30
    at, where = 0, {}
    for name, a in parts.items():
        where[name] = (at, a.shape[1])
        at += a.shape[1]
    return np.concatenate([a.astype(np.float32) for a in parts.values()], 1), where


CONST, CONST_AT = constants()


class Core:

    def __init__(self, nc, ctx, const):
        self.nc, self.ctx, self.const_dram = nc, ctx, const
        self.x = self.sb("x", [P, KD, T])
        self.area_at, self.views = nc.sbuf_base, {}
        self.area = self.sb("area", [P, 10, KD * T])
        self.const_sb = self.sb("const", [P, CONST_KEPT])
        self.cols = self.sb("cols", [P, 470])
        self.mod = self.sb("mod", [P, 2, 48])
        self.stats = self.sb("stats", [P, 2, T])
        self.ps = ctx.enter_context(nc.psum_tensor("ps", [P, 8, 512], F32))
        self.col_at = {}
        self.n_cols = 0
        self.used = []
        self.older = []
        self.count = 0

    def sb(self, name, shape, dt=F32):
        return self.ctx.enter_context(self.nc.sbuf_tensor(name, shape, dt))

    def slot(self, n, *dims):
        size = 1
        for d in dims:
            size *= d
        flat = self.area[:].rearrange("p s n -> p (s n)")[:, int(n * KD * T):int(n * KD * T) + size]
        if len(dims) == 1:
            return flat
        names = "abcd"[:len(dims)]
        return flat.rearrange(f"p ({' '.join(names)}) -> p {' '.join(names)}",
                              **{k: v for k, v in zip(names, dims)})

    def rounded(self, n, *dims):
        at = int(n * KD * T)
        if (at, dims) not in self.views:
            self.views[at, dims] = self.nc.alloc_sbuf_tensor_at(
                f"rounded_{at}_" + "_".join(map(str, dims)), [P, *dims], F32R, offset=self.area_at + 4 * at)
        return self.views[at, dims]

    def rounded_tiles(self, n, tiles=KD):
        return [self.rounded(n + k // KD, min(KD, tiles - k // KD * KD), T)[:, k % KD] for k in range(tiles)]

    def const(self, name, rows=P):
        at, n = CONST_AT[name]
        return self.const_sb[0:rows, at:at + n]

    def col(self, name, k=0, n=1):
        at = self.col_at[name] + k
        return self.cols[:, at:at + n]

    def semaphores(self, *names):
        self.count += 1
        for s in self.older:
            self.nc.release_semaphore(s)
        self.older, self.used = self.used, [self.nc.alloc_semaphore(f"{n}_{self.count}") for n in names]
        return self.used

    def clear_before(self, sp):
        for s in self.older:
            sp.sem_clear(s)

    def clear_all(self):
        self.semaphores()
        with self.nc.Block() as block:
            @block.sync
            def _(sp):
                self.clear_before(sp)


CONST_KEPT = CONST_AT["cos"][0]


def turn_rows(core, loads, groups, extra_loads=(), clear=True):
    nc = core.nc
    rows = core.slot(8, len(groups), P)
    loaded, turned, copied = core.semaphores("rows_loaded", "rows_turned", "columns_copied")
    plan = []
    for g, group in enumerate(groups):
        at = 0
        first = core.n_cols
        for name, view in group:
            n = view.shape[0]
            core.col_at[name] = first + at
            plan.append((g, at, n, view))
            at += n
        core.n_cols += at
        groups[g] = (first, at)
    with nc.Block() as block:
        @block.sync
        def _(sp):
            core.clear_before(sp)
            for dst, src in loads:
                sp.dma_start(dst, src).then_inc(loaded, 16)
            for g, at, n, view in plan:
                sp.dma_start(rows[at:at + n, g, :], view).then_inc(loaded, 16)

        @block.tensor
        def _(pe):
            pe.wait_ge(loaded, 16 * (len(plan) + len(loads)))
            for g, (first, n) in enumerate(groups):
                if g >= 2:
                    pe.wait_ge(copied, g - 1)
                nc.tensor.transpose(core.ps[:, g % 2, 0:n], rows[0:n, g, :],
                                    core.const("ident", n)[:, 0:n]).then_inc(turned, 1)

        @block.vector
        def _(dve):
            for g, (first, n) in enumerate(groups):
                dve.wait_ge(turned, g + 1)
                nc.vector.tensor_copy(core.cols[:, first:first + n], core.ps[:, g % 2, 0:n]).then_inc(copied, 1)


def load_x(core, x_dram):
    nc = core.nc
    rows = core.slot(0, 4, D)
    loaded, turned, copied = core.semaphores("x_loaded", "x_turned", "x_copied")
    with nc.Block() as block:
        @block.sync
        def _(sp):
            core.clear_before(sp)
            sp.dma_start(rows, x_dram.rearrange("o (a p) d -> p (o a) d", p=P)).then_inc(loaded, 16)

        @block.tensor
        def _(pe):
            pe.wait_ge(loaded, 16)
            for k in range(KD):
                if k >= 2:
                    pe.wait_ge(copied, k - 1)
                for a in range(4):
                    last = nc.tensor.transpose(core.ps[:, k % 2, a * P:(a + 1) * P],
                                               rows[:, a, k * P:(k + 1) * P], core.const("ident"))
                last.then_inc(turned, 1)

        @block.vector
        def _(dve):
            for k in range(KD):
                dve.wait_ge(turned, k + 1)
                nc.vector.tensor_copy(core.x[:, k], core.ps[:, k % 2]).then_inc(copied, 1)


def modulation(core, layer, ada_w):
    nc = core.nc
    W = 512
    U = 2
    blocks = 6 * D // W
    ring = core.slot(0, U, KD, W)
    acc = core.slot(4, U, W)
    cond = core.slot(5, KD)
    loaded = core.semaphores("loaded_0", "loaded_1", "weighed", "summed", "cond_ready", "sums_done")
    weighed, summed, cond_ready, sums_done = loaded[2:]
    view = ada_w[layer].rearrange("(k p) n -> p k n", p=P)
    mod = core.mod[:, layer]
    with nc.Block() as block:
        @block.sync
        def _(sp):
            core.clear_before(sp)
            for s in range(U):
                sp.dma_start(ring[:, s], view[:, :, s * W:(s + 1) * W]).then_inc(loaded[s], 16)
            with sp.Fori(1, blocks // U) as i:
                for s in range(U):
                    sp.wait_ge(weighed, (i - 1) * U + s + 1)
                    sp.dma_start(ring[:, s], view[:, :, ds(i * (U * W) + s * W, W)]).then_inc(loaded[s], 16)

        @block.scalar
        def _(act):
            nc.scalar.activation(cond, core.col("c", 0, KD), ACT.Silu).then_inc(cond_ready, 1)

        @block.vector
        def _(dve):
            dve.wait_ge(cond_ready, 1)
            with dve.Fori(0, blocks // U) as i:
                for s in range(U):
                    dve.wait_ge(loaded[s], i * 16 + 16)
                    dve.wait_ge(summed, i * U + s + 1)
                    nc.vector.tensor_scalar(acc[:, s], ring[:, s, 0], cond[:, 0:1], None, ALU.mult)
                    for k in range(1, KD):
                        dve.drain()
                        last = nc.vector.scalar_tensor_tensor(acc[:, s], ring[:, s, k], cond[:, k:k + 1],
                                                              acc[:, s], ALU.mult, ALU.add)
                    last.then_inc(weighed, 1)
            dve.wait_ge(sums_done, 1)
            nc.vector.tensor_tensor(mod, core.ps[:, 0, 0:48], core.col(f"ada_b{layer}", 0, 48), ALU.add)
            dve.drain()
            for part in (1, 2, 4, 5):
                nc.vector.tensor_scalar(mod[:, part * KD:(part + 1) * KD], mod[:, part * KD:(part + 1) * KD],
                                        1.0, None, ALU.add)

        @block.tensor
        def _(pe):
            pe.sem_inc(summed, U)
            with pe.Fori(0, blocks // U) as i:
                for s in range(U):
                    pe.wait_ge(weighed, i * U + s + 1)
                    for m in range(W // P):
                        last = nc.tensor.matmul(core.ps[:, 0, ds(i * (U * W // P) + s * (W // P) + m, 1)],
                                                acc[:, s, m * P:(m + 1) * P], core.const("ones")[:, 0:1],
                                                start=True, stop=True)
                    last.then_inc(summed, 1)
            pe.drain().then_inc(sums_done, 1)


def layer_norm(core, gain, bias):
    nc = core.nc
    z = core.x
    mean, rstd = core.stats[:, 0], core.stats[:, 1]
    square = core.slot(9, 2, T)
    (mean_summed, mean_ready, centred, squared, square_used, var_summed, root_ready, rstd_ready,
     normed, scaled) = core.semaphores(
        "mean_summed", "mean_ready", "centred", "squared", "square_used", "var_summed", "root_ready",
        "rstd_ready", "normed", "scaled")
    with nc.Block() as block:
        @block.sync
        def _(sp):
            core.clear_before(sp)

        @block.tensor
        def _(pe):
            for k in range(KD):
                last = nc.tensor.matmul(core.ps[:, 0], core.const("ones"), z[:, k], start=k == 0, stop=k == KD - 1)
            last.then_inc(mean_summed, 1)
            for k in range(KD):
                pe.wait_ge(squared, k + 1)
                last = nc.tensor.matmul(core.ps[:, 1], core.const("ones"), square[:, k % 2],
                                        start=k == 0, stop=k == KD - 1)
                last.then_inc(square_used, 1)

        @block.scalar
        def _(act):
            for k in range(KD):
                act.wait_ge(centred, k + 1)
                if k >= 2:
                    act.wait_ge(square_used, k - 1)
                nc.scalar.activation(square[:, k % 2], z[:, k], ACT.Square).then_inc(squared, 1)
            act.wait_ge(var_summed, 1)
            nc.scalar.activation(rstd, rstd, ACT.Sqrt).then_inc(root_ready, 1)
            for k in range(KD):
                act.wait_ge(normed, k + 1)
                nc.scalar.activation(core.x[:, k], z[:, k], ACT.Identity, bias=core.col(bias, k),
                                     scale=core.col(gain, k)).then_inc(scaled, 1)

        @block.vector
        def _(dve):
            dve.wait_ge(mean_summed, 1)
            nc.vector.tensor_scalar(mean, core.ps[:, 0], 1.0 / D, None, ALU.mult)
            dve.drain()
            for k in range(KD):
                nc.vector.tensor_tensor(z[:, k], z[:, k], mean, ALU.subtract).then_inc(centred, 1)
            dve.wait_ge(square_used, KD)
            nc.vector.tensor_scalar(rstd, core.ps[:, 1], 1.0 / D, LN_EPS, ALU.mult, ALU.add).then_inc(var_summed, 1)
            dve.wait_ge(root_ready, 1)
            nc.vector.reciprocal(mean, rstd)
            dve.drain()
            for k in range(KD):
                nc.vector.tensor_tensor(z[:, k], z[:, k], mean, ALU.mult).then_inc(normed, 1)


def modulate(core, layer, half, u, shifted=None):
    nc = core.nc
    sh, sc = (0, 1) if half == 0 else (3, 4)
    done, = core.semaphores("modulated")
    with nc.Block() as block:
        @block.sync
        def _(sp):
            core.clear_before(sp)

        @block.vector
        def _(dve):
            for k in range(KD):
                nc.vector.tensor_scalar(u[:, k], core.x[:, k], core.mod[:, layer, sc * KD + k:sc * KD + k + 1],
                                        core.mod[:, layer, sh * KD + k:sh * KD + k + 1], ALU.mult, ALU.add)
            if shifted is not None:
                dve.drain()
                for k in range(KD):
                    nc.vector.tensor_tensor(shifted[:, k, 1:T], u[:, k, 0:T - 1], u[:, k, 1:T], ALU.subtract)
                nc.vector.tensor_scalar(shifted[:, :, 0:1], u[:, :, 0:1], -1.0, None, ALU.mult)


def linear(core, weight, tiles, kt, rhs, ring, vector=None, scalar=None, U=2, parts=1, width=P):
    nc = core.nc
    names = [f"weights_in_slot{s}" for s in range(U)]
    sems = core.semaphores(*names, "products_done", "banks_freed")
    loaded, done, freed = sems[:U], sems[U], sems[U + 1]
    assert tiles % U == 0
    n = tiles // U

    def drain(eng, each):
        with eng.Fori(0, n) as i:
            for s in range(U):
                eng.wait_ge(done, i * U + (U + s + 1))
                each(eng, i * U + s, [core.ps[:, s * parts + q] for q in range(parts)], s).then_inc(freed, 1)

    with nc.Block() as block:
        @block.sync
        def _(sp):
            core.clear_before(sp)
            with sp.Fori(0, n) as i:
                for s in range(U):
                    sp.wait_ge(done, i * U + (s + 1))
                    for q in range(parts):
                        sp.dma_start(ring[:, s * parts + q], weight(i * U + s, q)).then_inc(loaded[s], 16)

        @block.tensor
        def _(pe):
            pe.sem_inc(done, U)
            pe.sem_inc(freed, U)
            with pe.Fori(0, n) as i:
                for s in range(U):
                    pe.wait_ge(loaded[s], i * (16 * parts) + 16 * parts)
                    pe.wait_ge(freed, i * U + (s + 1))
                    for q in range(parts):
                        for k in range(kt):
                            last = nc.tensor.matmul(core.ps[0:width, s * parts + q], ring[:, s * parts + q, k],
                                                    rhs[:, k], start=k == 0, stop=k == kt - 1)
                    last.then_inc(done, 1)

        if vector is not None:
            @block.vector
            def _(dve):
                drain(dve, vector)
        if scalar is not None:
            @block.scalar
            def _(act):
                drain(act, scalar)


def columns(w, j, n=P):
    return w[:, ds(j * P, n)].rearrange("(k p) m -> p k m", p=P)


def products(core, tiles, kt, weight, rhs, ring_at, vector=None, scalar=None, make=None, parts=1, accumulate=False,
             U=4, extra=(), feed=None, split=True, twice=()):
    nc = core.nc
    raw, high, low = rhs
    kr = kt * parts if accumulate else kt
    per = U // parts
    n = tiles // per
    assert n * per == tiles
    w_raw, w_low = core.slot(ring_at, U, kt, P), core.rounded(ring_at, U, kt, P)
    w_high = core.rounded(ring_at + U * kt * P / (KD * T), U, kt, P)
    sems = core.semaphores(*[f"weights_in_slot{s}" for s in range(U)], "weights_high", "weights_split", "products_done",
                           "banks_freed", "rhs_made", "rhs_high", "rhs_split", *extra)
    loaded = sems[:U]
    weights_high, weights_split, done, freed, rhs_made, rhs_high, rhs_split = sems[U:U + 7]
    more = sems[U + 7:] + [freed]

    def banks(t):
        return [core.ps[:, t]] if accumulate else [core.ps[:, t * parts + q] for q in range(parts)]

    def high_part(act, i, s):
        act.wait_ge(loaded[s], i * 16 + (32 if s in twice else 16))
        nc.scalar.copy(w_high[:, s], w_raw[:, s]).then_inc(weights_high, 1)

    def low_part(dve, i, s):
        dve.wait_ge(weights_high, i * U + (s + 1))
        nc.vector.tensor_tensor(w_low[:, s], w_raw[:, s], w_high[:, s].bitcast(F32), ALU.subtract).then_inc(weights_split, 1)

    def rounds(eng, prepare, take):
        def one(i, last):
            for t in range(per):
                for q in range(parts):
                    if t + 1 < per:
                        prepare(eng, i, (t + 1) * parts + q)
                    elif not last:
                        prepare(eng, i + 1, q)
                if take is not None:
                    eng.wait_ge(done, i * U + (U + (t + 1) * parts))
                    end = take(eng, i * per + t, banks(t), t, more)
                    if end is not None:
                        end.then_inc(freed, 1)
        if n > 1:
            with eng.Fori(0, n - 1) as i:
                one(i, False)
        one(n - 1, True)

    with nc.Block() as block:
        @block.sync
        def _(sp):
            core.clear_before(sp)
            if feed is not None:
                feed(sp, w_raw, loaded, done)
            else:
                with sp.Fori(0, n) as i:
                    for s in range(U):
                        sp.wait_ge(done, i * U + (s + 1))
                        sp.dma_start(w_raw[:, s], weight(i * per + s // parts, s % parts)).then_inc(loaded[s], 16)

        @block.tensor
        def _(pe):
            pe.sem_inc(done, U)
            pe.sem_inc(freed, per)

            def one(i, first):
                for s in range(U):
                    t, q = s // parts, s % parts
                    pe.wait_ge(weights_split, i * U + (s + 1))
                    if q == 0:
                        pe.wait_ge(freed, i * per + (t + 1))
                    for k in range(kt):
                        r = q * kt + k if accumulate else k
                        if split and first and (s == 0 or accumulate and s < parts):
                            pe.wait_ge(rhs_split, r + 1)
                        bank = banks(t)[0 if accumulate else q]
                        start, stop = r == 0, r == kr - 1
                        nc.tensor.matmul(bank, w_high[:, s, k], high[r], start=start, stop=False)
                        nc.tensor.matmul(bank, w_high[:, s, k], low[r], start=False, stop=False)
                        last = nc.tensor.matmul(bank, w_low[:, s, k], high[r], start=False, stop=stop)
                    last.then_inc(done, 1)

            one(0, True)
            if n > 1:
                with pe.Fori(1, n) as i:
                    one(i, False)

        @block.scalar
        def _(act):
            high_part(act, 0, 0)
            for k in range(kr if split else 0):
                if make is not None:
                    act.wait_ge(rhs_made, k + 1)
                nc.scalar.copy(high[k], raw[:, k]).then_inc(rhs_high, 1)
            for q in range(1, parts):
                high_part(act, 0, q)
            rounds(act, high_part, scalar)

        @block.vector
        def _(dve):
            if make is not None:
                make(dve, 0).then_inc(rhs_made, 1)
            low_part(dve, 0, 0)
            for k in range(kr if split else 0):
                if make is not None and k + 1 < kr:
                    make(dve, k + 1).then_inc(rhs_made, 1)
                dve.wait_ge(rhs_high, k + 1)
                nc.vector.tensor_tensor(low[k], raw[:, k], high[k].bitcast(F32), ALU.subtract).then_inc(rhs_split, 1)
            for q in range(1, parts):
                low_part(dve, 0, q)
            rounds(dve, low_part, vector)


def flat(t):
    return t.rearrange("p o t -> p (o t)")


def residual(core, layer, half, w, rhs, ring_at, kt=KD, parts=1):
    nc = core.nc

    def out(dve, j, banks, s, more):
        x = flat(core.x[:, ds(j, 1)])
        if layer is None:
            return nc.vector.scalar_tensor_tensor(x, x, ALPHA, banks[0], ALU.mult, ALU.add)
        nc.vector.tensor_scalar(x, x, ALPHA, None, ALU.mult)
        dve.drain()
        return nc.vector.scalar_tensor_tensor(x, banks[0], core.mod[:, layer, ds((2 if half == 0 else 5) * KD + j, 1)], x,
                                              ALU.mult, ALU.add)

    products(core, KD, kt,
             lambda j, q: w[q * kt * P:(q + 1) * kt * P, ds(j * P, P)].rearrange("(k p) m -> p k m", p=P),
             rhs, ring_at, vector=out, parts=parts, accumulate=True)


def modulated(core, layer, half, u):
    sh, sc = (0, 1) if half == 0 else (3, 4)

    def make(dve, k):
        return core.nc.vector.tensor_scalar(u[:, k], core.x[:, k], core.mod[:, layer, sc * KD + k:sc * KD + k + 1],
                                            core.mod[:, layer, sh * KD + k:sh * KD + k + 1], ALU.mult, ALU.add)
    return make


def feed_forward(core, layer, w_in, w_out, gate_first=True, conv=None):
    nc = core.nc
    gq = 0 if gate_first else 1
    gate = core.stats
    h = core.slot(4.5, KF, T)

    def activate(act, j, banks, s, more):
        gated, convolved, freed = more
        if conv is None:
            nc.scalar.activation(gate[:, s], banks[gq], ACT.Silu).then_inc(gated, 1)
        else:
            act.wait_ge(convolved, j + 1)
            nc.scalar.activation(gate[:, s], gate[:, s], ACT.Silu,
                                 bias=core.cols[:, ds(j + conv[1], 1)]).then_inc(gated, 1)

    def weigh(dve, j, banks, s, more):
        gated, convolved, freed = more
        if conv is not None:
            causal_conv(nc, dve, gate[:, s], banks[gq], lambda i: core.cols[:, ds(j + (conv[0] + i * KF), 1)],
                        conv[2]).then_inc(convolved, 1)
        dve.wait_ge(gated, j + 1)
        return nc.vector.tensor_tensor(flat(h[:, ds(j, 1)]), gate[:, s], banks[1 - gq], ALU.mult)

    u, make = core.x, None
    if layer is not None:
        u = core.slot(1, KD, T)
        make = modulated(core, layer, 1, u)
    products(core, KF, KD, lambda j, q: w_in[:, ds(j * P + q * FF, P)].rearrange("(k p) m -> p k m", p=P),
             (u, core.rounded_tiles(0), core.rounded_tiles(1)), 7.25, vector=weigh, scalar=activate, make=make, parts=2,
             extra=("gated", "convolved"))
    residual(core, layer, 1, w_out, (h, core.rounded_tiles(0, KF), core.rounded_tiles(4.5, KF)), 7.25, kt=KF // 2, parts=2)


HR = 16
DECAY = float(np.exp(-0.5))


def rwkv_projections(core, A):
    nc = core.nc
    u, xx = core.slot(0, KD, T), core.slot(1, KD, T)
    mix = core.slot(2, 2, KD, T)
    rkv = core.slot(5, 3 * KD, T)
    lora = core.slot(4, 4096)
    down = {3: lora[:, 0:512].rearrange("p (k m) -> p k m", k=KD), 4: lora[:, 512:1024].rearrange("p (k m) -> p k m", k=KD),
            5: lora[:, 1024:2048].rearrange("p (k m) -> p k m", k=KD)}
    up = {3: lora[0:64, 2048:3072], 4: lora[0:64, 3072:4096]}
    inner = core.lora_inner
    modulate(core, 0, 0, u, xx)

    def lerp(dve, i, k):
        return nc.vector.scalar_tensor_tensor(mix[:, i % 2 if i > 2 else 0, k], xx[:, k], core.col("mu", i * KD + k), u[:, k],
                                              ALU.mult, ALU.add)

    loaded, mixed, summed = core.semaphores("lora_loaded", "mixed", "inner_summed")
    rank = {3: 64, 4: 64, 5: 128}
    with nc.Block() as block:
        @block.sync
        def _(sp):
            core.clear_before(sp)
            for i, name in ((3, "rwkv_w1"), (4, "rwkv_a1"), (5, "rwkv_g1")):
                sp.dma_start(down[i], A[name].rearrange("o (k p) m -> p (o k) m", p=P)).then_inc(loaded, 16)
            for i, name in ((3, "rwkv_w2"), (4, "rwkv_a2")):
                sp.dma_start(up[i], A[name].rearrange("o r n -> (o r) n")).then_inc(loaded, 16)

        @block.vector
        def _(dve):
            for i in (3, 4, 5):
                if i == 5:
                    dve.wait_ge(summed, 1)
                for k in range(KD):
                    lerp(dve, i, k).then_inc(mixed, 1)

        @block.tensor
        def _(pe):
            pe.wait_ge(loaded, 80)
            for i in (3, 4, 5):
                for k in range(KD):
                    pe.wait_ge(mixed, (i - 3) * KD + k + 1)
                    last = nc.tensor.matmul(core.ps[0:rank[i], i], down[i][:, k], mix[:, i % 2, k],
                                            start=k == 0, stop=k == KD - 1)
                last.then_inc(summed, 1)

        @block.scalar
        def _(act):
            for i, f in ((3, ACT.Tanh), (4, ACT.Identity), (5, ACT.Sigmoid)):
                act.wait_ge(summed, i - 2)
                nc.scalar.activation(inner[0:rank[i], i - 3], core.ps[0:rank[i], i], f)

    for m, name in enumerate("rkv"):
        products(core, KD, KD,
                 lambda j, q: A["rwkv_w_rkv"][0, m, :, ds(j * P, P)].rearrange("(k p) m -> p k m", p=P),
                 (mix[:, 0], core.rounded_tiles(3), core.rounded_tiles(2)), 8,
                 scalar=lambda act, j, banks, s, more: nc.scalar.copy(flat(rkv[:, ds(j + m * KD, 1)]), banks[0]),
                 make=lambda dve, k: lerp(dve, m, k))

    lw, a = core.slot(0, KD, T), core.slot(1, KD, T)
    summed, taken = core.semaphores("outer_summed", "banks_taken")
    with nc.Block() as block:
        @block.sync
        def _(sp):
            core.clear_before(sp)

        @block.tensor
        def _(pe):
            for n in range(2 * KD):
                which, k = 3 + n // KD, n % KD
                if n >= 4:
                    pe.wait_ge(taken, n - 3)
                nc.tensor.matmul(core.ps[:, n % 4], up[which][:, k * P:(k + 1) * P], inner[0:64, which - 3],
                                 start=True, stop=True).then_inc(summed, 1)

        @block.scalar
        def _(act):
            for n in range(2 * KD):
                k = n % KD
                act.wait_ge(summed, n + 1)
                nc.scalar.activation((lw if n < KD else a)[:, k], core.ps[:, n % 4], ACT.Sigmoid,
                                     bias=core.col("w0" if n < KD else "a0", k)).then_inc(taken, 1)

        @block.vector
        def _(dve):
            dve.wait_ge(taken, KD)
            nc.vector.tensor_scalar(lw, lw, -DECAY, None, ALU.mult)


def rwkv_decays(core):
    nc = core.nc
    lw, a, r, k, kk = (core.slot(n, KD, T) for n in (0, 1, 5, 6, 2))
    t3, t4 = core.slot(3, KD, T), core.slot(4, KD, T)
    mid, first, ends = core.mid, core.first, core.ends
    (k_scaled, squared, head_summed, floored, rooted, kk_done, product, bonus_summed, running, risen,
     fallen, ends_risen) = core.semaphores(
        "k_scaled", "squared", "head_summed", "floored", "rooted", "kk_done", "bonus_product", "bonus_summed",
        "running_sums", "risen", "fallen", "ends_risen")

    def by_chunk(t):
        return t.rearrange("p k (c t) -> p (k c) t", c=NC)

    with nc.Block() as block:
        @block.sync
        def _(sp):
            core.clear_before(sp)

        @block.scalar
        def _(act):
            for i in range(KD):
                act.wait_ge(k_scaled, i + 1)
                nc.scalar.activation(t3[:, i], kk[:, i], ACT.Square).then_inc(squared, 1)
            for i in range(KD):
                act.wait_ge(floored, i + 1)
                nc.scalar.activation(t4[:, i], t4[:, i], ACT.Sqrt).then_inc(rooted, 1)
            act.wait_ge(running, 1)
            act.wait_ge(bonus_summed, 1)
            nc.scalar.activation(t3, lw, ACT.Exp).then_inc(risen, 1)
            nc.scalar.activation(t4, lw, ACT.Exp, scale=-1.0).then_inc(fallen, 1)
            nc.scalar.activation(first[:], mid[:], ACT.Exp, scale=-1.0)
            nc.scalar.activation(ends[:], ends[:], ACT.Exp).then_inc(ends_risen, 1)

        @block.tensor
        def _(pe):
            for i in range(KD):
                pe.wait_ge(squared, i + 1)
                if i >= 4:
                    pe.wait_ge(floored, i - 3)
                nc.tensor.matmul(core.ps[:, i % 4], core.const("head64"), t3[:, i], start=True,
                                 stop=True).then_inc(head_summed, 1)
            for i in range(KD):
                pe.wait_ge(product, i + 1)
                last = nc.tensor.matmul(core.ps[0:HR, 4], core.const("heads16")[:, i * HR:(i + 1) * HR], t3[:, i],
                                        start=i == 0, stop=i == KD - 1)
            last.then_inc(bonus_summed, 1)

        @block.vector
        def _(dve):
            for i in range(KD):
                nc.vector.tensor_scalar(kk[:, i], k[:, i], core.col("k_k", i), None, ALU.mult).then_inc(k_scaled, 1)
            for i in range(KD):
                dve.wait_ge(head_summed, i + 1)
                nc.vector.tensor_scalar(t4[:, i], core.ps[:, i % 4], 1e-6, None, ALU.add).then_inc(floored, 1)
            for i in range(KD):
                dve.wait_ge(rooted, i + 1)
                nc.vector.reciprocal(t4[:, i], t4[:, i])
            dve.drain()
            nc.vector.tensor_tensor(kk, kk, t4, ALU.mult)
            dve.drain()
            for i in range(KD):
                nc.vector.tensor_scalar(t4[:, i], a[:, i], core.col("k_a", i), core.one_less_k_a[:, i:i + 1],
                                        ALU.mult, ALU.add)
            dve.drain()
            nc.vector.tensor_tensor(k, k, t4, ALU.mult)
            nc.vector.tensor_tensor(a, a, kk, ALU.mult)
            dve.drain()
            for i in range(KD):
                nc.vector.scalar_tensor_tensor(t3[:, i], r[:, i], core.col("r_k", i), k[:, i], ALU.mult,
                                               ALU.mult).then_inc(product, 1)
            for i in range(KD):
                nc.vector.tensor_tensor_scan(t4[:, i], core.const("carry"), lw[:, i], 0.0, ALU.mult, ALU.add)
            dve.drain()
            nc.vector.tensor_copy(mid[:].rearrange("p (n o) -> p n o", o=1), by_chunk(t4)[:, :, C // 2 - 1:C // 2])
            dve.drain()
            nc.vector.tensor_tensor(by_chunk(lw), by_chunk(t4), mid[:].unsqueeze(2).to_broadcast([P, KD * NC, C]),
                                    ALU.subtract)
            dve.drain()
            nc.vector.tensor_copy(ends[:].rearrange("p (n o) -> p n o", o=1), by_chunk(lw)[:, :, C - 1:C])
            dve.drain()
            e4, m4 = (t[:].rearrange("p (k c) -> p k c", c=NC) for t in (ends, mid))
            nc.vector.tensor_tensor(e4[:, :, 0:NC - 1], e4[:, :, 0:NC - 1], m4[:, :, 1:NC], ALU.add)
            dve.drain().then_inc(running, 1)
            dve.wait_ge(bonus_summed, 1)
            nc.vector.tensor_copy(core.bonus[:], core.ps[0:HR, 4])
            dve.wait_ge(risen, 1)
            dve.wait_ge(fallen, 1)
            nc.vector.tensor_tensor(r, r, t3, ALU.mult)
            nc.vector.tensor_tensor(k, k, t4, ALU.mult)
            nc.vector.tensor_tensor(a, a, t4, ALU.mult)
            nc.vector.tensor_tensor(by_chunk(kk)[:, :, 1:C], by_chunk(kk)[:, :, 1:C], by_chunk(t3)[:, :, 0:C - 1],
                                    ALU.mult)
            dve.wait_ge(ends_risen, 1)
            nc.vector.tensor_tensor(by_chunk(kk)[:, :, 0:1], by_chunk(kk)[:, :, 0:1], first[:].unsqueeze(2), ALU.mult)
            nc.vector.memset(e4[:, :, NC - 1:NC], 0.0)


def rwkv_chunks(core):
    nc = core.nc
    R, Aa, B, K, V = (core.slot(n, KD, T) for n in (5, 2, 1, 6, 7))
    HT = KD // 2
    H = HR // 2
    ar = core.slot(0, HT, 2, C)
    b_c, k_c, v_c = (core.area[:, 0, 1024 + n * 512:1536 + n * 512].rearrange("p (k t) -> p k t", k=HT) for n in range(3))
    turned = core.area[:, 0, 2560:4096].rearrange("p (w k t) -> p w k t", w=3, k=HT)
    gram = core.slot(3, H, 4, C)
    X, XT = core.slot(4, H, C), core.area[:, 4, 1024:2048].rearrange("p (h t) -> p h t", h=H)
    W = core.area[:, 4, 2048:3072].rearrange("p (h t) -> p h t", h=H)
    Z = core.area[:, 4, 3072:3584].rearrange("p (h v) -> p h v", h=H)
    Uu = core.area[:, 4, 3584:4096].rearrange("p (h v) -> p h v", h=H)
    S = core.slot(8, HT, 64)
    masks = core.area[:, 8, 1024:1536]
    G = 2
    nlev = len(LEVELS)
    (staged, turned_ps, turned_sb, gram_ps, gram_sb, seed_sb, x_ps, x_sb, w_ps, w_sb, xw_ps, x_new, xt_ps, xt_new,
     z_ps, z_sb, u_ps, u_sb, y_ps, s_ps, s_new, y_sb, gram_seen) = core.semaphores(
        "staged", "turned_ps", "turned_sb", "gram_ps", "gram_sb", "seed_sb", "x_ps", "x_sb", "w_ps", "w_sb", "xw_ps",
        "x_new", "xt_ps", "xt_new", "z_ps", "z_sb", "u_ps", "u_sb", "y_ps", "s_ps", "s_new", "y_sb", "gram_seen")
    ident = core.const("ident")

    def each_step(eng, body):
        with eng.Fori(0, 2) as half:
            with eng.Fori(0, NC) as c:
                body(half, c, half * NC + c)

    def part(t, half, c):
        return t[:, ds(half * HT, HT), ds(c * C, C)]

    def head(t, h):
        return t[64 * (h % 2):64 * (h % 2) + 64, h // 2]

    with nc.Block() as block:
        @block.sync
        def _(sp):
            core.clear_before(sp)

        @block.gpsimd
        def _(pool):
            def body(half, c, n):
                pool.wait_ge(y_ps, n * 1 + 1)
                nc.gpsimd.tensor_copy(b_c, part(B, half, c))
                nc.gpsimd.tensor_copy(k_c, part(K, half, c))
                nc.gpsimd.tensor_copy(v_c, part(V, half, c))
                nc.gpsimd.tensor_copy(ar[:, :, 0], part(Aa, half, c))
                nc.gpsimd.tensor_copy(ar[:, :, 1], part(R, half, c)).then_inc(staged, 1)
            each_step(pool, body)

        @block.tensor
        def _(pe):
            pe.sem_inc(y_ps, 1)

            def body(half, c, n):
                pe.wait_ge(staged, n + 1)
                pe.wait_ge(s_new, n + 1)
                for w, src in enumerate((b_c, k_c, v_c)):
                    for p in range(HT):
                        last = nc.tensor.transpose(core.ps[:, w, p * C:(p + 1) * C], src[:, p], ident)
                    last.then_inc(turned_ps, 1)
                for h in range(H):
                    if h >= 4:
                        pe.wait_ge(gram_sb, n * H + (h - 3))
                    bank = core.ps[:, 4 + h % 4]
                    both = head(ar, h).rearrange("p w t -> p (w t)")
                    nc.tensor.matmul(bank[:, 0:2 * C], head(b_c, h), both, start=True, stop=True)
                    nc.tensor.matmul(bank[:, 2 * C:4 * C], head(k_c, h), both, start=True,
                                     stop=True).then_inc(gram_ps, 1)
                invert_products(core, pe, n, G, ident, lambda h: gram[:, h, 0], X, XT, W,
                                (turned_sb, 3), seed_sb, x_ps, x_sb, w_ps, w_sb, xw_ps, x_new, xt_ps, xt_new)
                for h in range(H):
                    out = core.ps[:, 3 * (h % 2), (h // 2) * 64:(h // 2 + 1) * 64]
                    lo = 64 * (h % 2)
                    nc.tensor.matmul(out, ar[lo:lo + 64, h // 2, 0], S[lo:lo + 64, h // 2], start=True, stop=False)
                    last = nc.tensor.matmul(out, gram[:, h, 2], turned[:, 2, h // 2, lo:lo + 64], start=False, stop=True)
                last.then_inc(z_ps, 1)
                pe.wait_ge(z_sb, n + 1)
                for h in range(H):
                    last = nc.tensor.matmul(core.ps[:, 1, h * 64:(h + 1) * 64], XT[:, h], Z[:, (h % 2) * HT + h // 2], start=True, stop=True)
                last.then_inc(u_ps, 1)
                pe.wait_ge(u_sb, n + 1)
                for h in range(H):
                    lo = 64 * (h % 2)
                    out = core.ps[lo:lo + 64, 2, (h // 2) * 64:(h // 2 + 1) * 64]
                    nc.tensor.matmul(out, turned[:, 0, h // 2, lo:lo + 64], Uu[:, h], start=True, stop=False)
                    last = nc.tensor.matmul(out, turned[:, 1, h // 2, lo:lo + 64], turned[:, 2, h // 2, lo:lo + 64],
                                            start=False, stop=True)
                last.then_inc(s_ps, 1)
                for h in range(H):
                    lo = 64 * (h % 2)
                    out = core.ps[lo:lo + 64, 3, (h // 2) * C:(h // 2 + 1) * C]
                    nc.tensor.matmul(out, S[lo:lo + 64, h // 2], ar[lo:lo + 64, h // 2, 1], start=True, stop=False)
                    nc.tensor.matmul(out, Uu[:, h], gram[:, h, 1], start=False, stop=False)
                    last = nc.tensor.matmul(out, turned[:, 2, h // 2, lo:lo + 64], gram[:, h, 3], start=False, stop=True)
                last.then_inc(y_ps, 1)
            each_step(pe, body)

        @block.scalar
        def _(act):
            def body(half, c, n):
                for w in range(3):
                    act.wait_ge(turned_ps, n * 3 + (w + 1))
                    nc.scalar.copy(turned[:, w].rearrange("p k t -> p (k t)"), core.ps[:, w]).then_inc(turned_sb, 1)
                for g in range(G):
                    act.wait_ge(x_ps, n * G + (g + 1))
                    nc.scalar.copy(X[:, 4 * g:4 * g + 4].rearrange("p h t -> p (h t)"), core.ps[:, g]).then_inc(x_sb, 1)
                act.wait_ge(z_ps, n + 1)
                for odd in range(2):
                    last = nc.scalar.copy(Z[:, odd * HT:(odd + 1) * HT].rearrange("p h v -> p (h v)"),
                                          core.ps[:, 3 * odd, 0:HT * 64])
                last.then_inc(z_sb, 1)
                act.wait_ge(u_ps, n + 1)
                nc.scalar.mul(Uu.rearrange("p h v -> p (h v)"), core.ps[:, 1], -1.0).then_inc(u_sb, 1)
                act.wait_ge(y_ps, n + 2)
                nc.scalar.copy(part(R, half, c), core.ps[:, 3].rearrange("p (k t) -> p k t", k=HT)).then_inc(y_sb, 1)
            each_step(act, body)

        @block.vector
        def _(dve):
            nc.vector.memset(gram, 0.0)
            nc.vector.tensor_copy(masks.rearrange("p (a b) -> p a b", a=2)[:, :, 0:C],
                                  core.const("upper").unsqueeze(1).to_broadcast([P, 2, C]))
            nc.vector.tensor_copy(masks.rearrange("p (a b) -> p a b", a=2)[:, :, C:2 * C],
                                  core.const("upto").unsqueeze(1).to_broadcast([P, 2, C]))
            nc.vector.memset(S, 0.0).then_inc(s_new, 1)
            dve.drain()

            def body(half, c, n):
                for h in range(H):
                    dve.wait_ge(gram_ps, n * H + (h + 1))
                    dve.sem_inc(gram_seen, 1)
                    nc.vector.copy_predicated(gram[:, h].rearrange("p w t -> p (w t)"), masks.bitcast(U32),
                                              core.ps[:, 4 + h % 4]).then_inc(gram_sb, 1)
                dve.drain()
                invert_updates(core, dve, n, G, lambda g: gram[:, 4 * g:4 * g + 4, 0], X, XT, W,
                               seed_sb, x_sb, w_ps, w_sb, xw_ps, x_new, xt_ps, xt_new)
                dve.wait_ge(s_ps, n + 1)
                dve.wait_ge(y_ps, n + 2)
                nc.vector.tensor_tensor(S, S, core.ps[:, 2, 0:HT * 64].rearrange("p (k v) -> p k v", k=HT), ALU.add)
                dve.drain()
                ends = core.ends[:].rearrange("p (k c) -> p k c", c=NC)[:, ds(half * HT, HT), ds(c, 1)]
                nc.vector.tensor_tensor(S, S, ends.to_broadcast([P, HT, 64]), ALU.mult).then_inc(s_new, 1)
                dve.wait_ge(y_sb, n + 1)
            each_step(dve, body)


def invert_products(core, pe, n, G, ident, lower_t, X, XT, W, turned_sb, seed_sb, x_ps, x_sb, w_ps, w_sb, xw_ps, x_new,
                    xt_ps, xt_new):
    nc = core.nc
    nl = len(LEVELS)
    pe.wait_ge(turned_sb[0], n * turned_sb[1] + turned_sb[1])
    for g in range(G):
        pe.wait_ge(seed_sb, n * G + (g + 1))
        for h in range(4):
            last = nc.tensor.transpose(core.ps[:, g, h * C:(h + 1) * C], XT[:, 4 * g + h], ident)
        last.then_inc(x_ps, 1)
    for lev in range(nl):
        final = lev == nl - 1
        for g in range(G):
            if lev == 0:
                pe.wait_ge(x_sb, n * G + (g + 1))
            else:
                pe.wait_ge(x_new, n * (G * (nl - 1)) + (lev - 1) * G + g + 1)
            for h in range(4):
                last = nc.tensor.matmul(core.ps[:, g, h * C:(h + 1) * C], lower_t(4 * g + h), X[:, 4 * g + h],
                                        start=True, stop=True)
            last.then_inc(w_ps, 1)
        for g in range(G):
            pe.wait_ge(w_sb, n * (G * nl) + lev * G + g + 1)
            if lev:
                pe.wait_ge(xt_new, n * (G * nl) + (lev - 1) * G + g + 1)
            if not final:
                for h in range(4):
                    last = nc.tensor.matmul(core.ps[:, 2 + g, h * C:(h + 1) * C], XT[:, 4 * g + h], W[:, 4 * g + h],
                                            start=True, stop=True)
                last.then_inc(xw_ps, 1)
            for h in range(4):
                last = nc.tensor.matmul(core.ps[:, 4 + g, h * C:(h + 1) * C], W[:, 4 * g + h], XT[:, 4 * g + h],
                                        start=True, stop=True)
            last.then_inc(xt_ps, 1)
    pe.wait_ge(xt_new, n * (G * nl) + G * nl)


def invert_updates(core, dve, n, G, lower_t, X, XT, W, seed_sb, x_sb, w_ps, w_sb, xw_ps, x_new, xt_ps, xt_new):
    nc = core.nc
    nl = len(LEVELS)

    def four(t, g):
        return t[:, 4 * g:4 * g + 4]

    def mask(name):
        return core.const(name).unsqueeze(1).to_broadcast([P, 4, C])

    def bank(b):
        return core.ps[:, b].rearrange("p (h t) -> p h t", h=4)

    for g in range(G):
        nc.vector.tensor_tensor(four(XT, g), lower_t(g), mask("corner1"), ALU.mult)
    dve.drain()
    for g in range(G):
        nc.vector.tensor_tensor(four(XT, g), mask("ident"), four(XT, g), ALU.subtract).then_inc(seed_sb, 1)
    for lev, b in enumerate(LEVELS):
        final = lev == nl - 1
        for g in range(G):
            dve.wait_ge(w_ps, n * (G * nl) + lev * G + g + 1)
            nc.vector.tensor_tensor(four(W, g), bank(g), mask(f"corner{b}"), ALU.mult).then_inc(w_sb, 1)
        for g in range(G):
            if not final:
                dve.drain()
                dve.wait_ge(xw_ps, n * (G * (nl - 1)) + lev * G + g + 1)
                if lev == 0:
                    dve.wait_ge(x_sb, n * G + (g + 1))
                nc.vector.tensor_tensor(four(X, g), four(X, g), bank(2 + g), ALU.subtract).then_inc(x_new, 1)
            dve.drain()
            dve.wait_ge(xt_ps, n * (G * nl) + lev * G + g + 1)
            nc.vector.tensor_tensor(four(XT, g), four(XT, g), bank(4 + g), ALU.subtract).then_inc(xt_new, 1)


def rwkv_output(core, A):
    nc = core.nc
    y, v = core.slot(5, KD, T), core.slot(7, KD, T)
    g2 = core.slot(3, D)
    sq = core.slot(4, 4, T)
    (loaded, y_summed, centred, squared, var_summed, floored, rooted, bonus_spread, gate_ps, freed) = core.semaphores(
        "gate_loaded", "y_summed", "centred", "squared", "var_summed", "floored", "rooted", "bonus_spread", "gate_ps",
        "banks_freed")
    bonus_at, _ = CONST_AT["spread16"]
    with nc.Block() as block:
        @block.sync
        def _(sp):
            core.clear_before(sp)
            sp.dma_start(g2, A["rwkv_g2"].rearrange("o r n -> (o r) n")).then_inc(loaded, 16)

        @block.tensor
        def _(pe):
            pe.wait_ge(loaded, 16)
            for k in range(KD):
                b = 4 * (k % 2)
                if k >= 2:
                    pe.wait_ge(freed, k - 1)
                nc.tensor.matmul(core.ps[:, b], core.const("head64"), y[:, k], start=True, stop=True).then_inc(y_summed, 1)
                nc.tensor.matmul(core.ps[:, b + 2], core.const("spread16", HR)[:, k * P:(k + 1) * P], core.bonus[:],
                                 start=True, stop=True).then_inc(bonus_spread, 1)
                nc.tensor.matmul(core.ps[:, b + 3], g2[:, k * P:(k + 1) * P], core.lora_inner[:, 2],
                                 start=True, stop=True).then_inc(gate_ps, 1)
                pe.wait_ge(squared, k + 1)
                nc.tensor.matmul(core.ps[:, b + 1], core.const("head64"), sq[:, k % 2], start=True,
                                 stop=True).then_inc(var_summed, 1)

        @block.scalar
        def _(act):
            for k in range(KD):
                act.wait_ge(centred, k + 1)
                nc.scalar.activation(sq[:, k % 2], y[:, k], ACT.Square).then_inc(squared, 1)
                act.wait_ge(floored, k + 1)
                nc.scalar.activation(sq[:, 2 + k % 2], sq[:, 2 + k % 2], ACT.Sqrt).then_inc(rooted, 1)

        @block.vector
        def _(dve):
            for k in range(KD):
                b = 4 * (k % 2)
                root = sq[:, 2 + k % 2]
                dve.wait_ge(y_summed, k + 1)
                nc.vector.scalar_tensor_tensor(y[:, k], core.ps[:, b], -1.0 / 64, y[:, k], ALU.mult,
                                               ALU.add).then_inc(centred, 1)
                dve.wait_ge(bonus_spread, k + 1)
                nc.vector.tensor_tensor(v[:, k], v[:, k], core.ps[:, b + 2], ALU.mult)
                dve.wait_ge(var_summed, k + 1)
                nc.vector.tensor_scalar(root, core.ps[:, b + 1], 1.0 / 64, 64e-5, ALU.mult, ALU.add).then_inc(floored, 1)
                dve.wait_ge(rooted, k + 1)
                nc.vector.reciprocal(root, root)
                dve.drain()
                nc.vector.scalar_tensor_tensor(y[:, k], y[:, k], core.col("gn_g", k), root, ALU.mult, ALU.mult)
                dve.drain()
                nc.vector.scalar_tensor_tensor(y[:, k], y[:, k], core.col("gn_b", k), v[:, k], ALU.add, ALU.add)
                dve.drain()
                dve.wait_ge(gate_ps, k + 1)
                nc.vector.tensor_tensor(y[:, k], y[:, k], core.ps[:, b + 3], ALU.mult).then_inc(freed, 1)
    residual(core, 0, 0, A["rwkv_w_out"].rearrange("o k n -> (o k) n"),
             (y, core.rounded_tiles(0), core.rounded_tiles(5)), 8)
    layer_norm(core, "ln_g00", "ln_b00")


HG = 8
TAPS = 4


def causal_conv(nc, dve, tmp, ps, tap, taps):
    nc.vector.tensor_scalar(tmp, ps, tap(taps - 1), None, ALU.mult)
    for back in range(1, taps):
        dve.drain()
        last = nc.vector.scalar_tensor_tensor(tmp[:, back:T], ps[:, 0:T - back], tap(taps - 1 - back), tmp[:, back:T],
                                              ALU.mult, ALU.add)
    return last


def gdn_projections(core, A):
    nc = core.nc
    u = core.slot(0, KD, T)
    qkv, z = core.slot(1, 3 * KD, T), core.slot(4, KD, T)
    tmp = core.slot(5, 2, T)
    w = A["gdn_w_in"].rearrange("o k n -> (o k) n")
    conv = core.col_at["conv"]
    high, low = core.rounded_tiles(6), core.rounded_tiles(7)

    def convolve(dve, j, banks, s, more):
        convolved, freed = more
        dve.wait_ge(freed, j + 3)
        causal_conv(nc, dve, tmp[:, s % 2], banks[0], lambda i: core.cols[:, ds(j + (conv + i * 3 * KD), 1)],
                    TAPS).then_inc(convolved, 1)

    def activate(act, j, banks, s, more):
        convolved, freed = more
        act.wait_ge(convolved, j + 1)
        return nc.scalar.activation(flat(qkv[:, ds(j, 1)]), tmp[:, s % 2], ACT.Silu)

    products(core, 3 * KD, KD, lambda j, q: columns(w, j), (u, high, low), 8, vector=convolve, scalar=activate,
             make=modulated(core, 1, 0, u), extra=("convolved",))
    products(core, KD, KD, lambda j, q: w[:, ds(j * P + 3 * D, P)].rearrange("(k p) m -> p k m", p=P), (u, high, low), 8,
             scalar=lambda act, j, banks, s, more: nc.scalar.activation(flat(z[:, ds(j, 1)]), banks[0], ACT.Silu), split=False)

    wg = core.slot(5, KD, 2 * HG)
    small = core.slot(6, 2, 4)
    alog, dt = small[0:HG, 0, 0:1], small[0:HG, 1, 0:1]
    tmp = core.slot(7, 4, T)
    x, soft, pos, g = (tmp[0:HG, i] for i in range(4))
    beta, gc, rise, fall = (core.gate_rows[:, i] for i in range(4))
    loaded, summed, shifted, softened, powered, cum, gates_done, turned = core.semaphores(
        "gates_loaded", "gates_summed", "shifted", "softened", "powered", "cumulated", "gates_done", "turned")
    with nc.Block() as block:
        @block.sync
        def _(sp):
            core.clear_before(sp)
            sp.dma_start(wg, w[:, 4 * D:4 * D + 2 * HG].rearrange("(k p) m -> p k m", p=P)).then_inc(loaded, 16)
            sp.dma_start(alog, A["gdn_a_log"].rearrange("o h -> h o")).then_inc(loaded, 16)
            sp.dma_start(dt, A["gdn_dt_bias"].rearrange("o h -> h o")).then_inc(loaded, 16)

        @block.tensor
        def _(pe):
            pe.wait_ge(loaded, 48)
            for q in range(2):
                for k in range(KD):
                    last = nc.tensor.matmul(core.ps[0:HG, q], wg[:, k, q * HG:(q + 1) * HG], u[:, k],
                                            start=k == 0, stop=k == KD - 1)
            last.then_inc(summed, 1)
            pe.wait_ge(cum, 1)
            for c in range(NC):
                last = nc.tensor.transpose(core.ps[:, 2, c * HG:(c + 1) * HG], gc[:, c * C:(c + 1) * C],
                                           core.const("ident", HG)[:, 0:HG])
            last.then_inc(turned, 1)

        @block.scalar
        def _(act):
            act.wait_ge(summed, 1)
            nc.scalar.activation(beta, core.ps[0:HG, 0], ACT.Sigmoid)
            act.wait_ge(loaded, 48)
            nc.scalar.activation(alog, alog, ACT.Exp)
            act.wait_ge(shifted, 1)
            nc.scalar.activation(soft, x, ACT.Abs)
            act.drain()
            nc.scalar.activation(soft, soft, ACT.Exp, scale=-1.0)
            act.drain()
            nc.scalar.activation(soft, soft, ACT.Ln, bias=1.0).then_inc(softened, 1)
            act.wait_ge(cum, 2)
            nc.scalar.activation(rise, gc, ACT.Exp)
            nc.scalar.activation(fall, fall, ACT.Exp).then_inc(powered, 1)

        @block.vector
        def _(dve):
            dve.wait_ge(summed, 1)
            dve.wait_ge(loaded, 48)
            nc.vector.tensor_scalar(x, core.ps[0:HG, 1], dt, None, ALU.add).then_inc(shifted, 1)
            dve.drain()
            nc.vector.tensor_scalar(pos, x, 0.0, None, ALU.max)
            dve.wait_ge(softened, 1)
            dve.drain()
            nc.vector.tensor_tensor(g, pos, soft, ALU.add)
            dve.drain()
            nc.vector.tensor_scalar(g, g, alog, -1.0, ALU.mult, ALU.mult)
            dve.drain()
            nc.vector.tensor_tensor_scan(gc, core.const("carry", HG), g, 0.0, ALU.mult, ALU.add).then_inc(cum, 1)
            dve.drain()
            g3, f3 = (t.rearrange("p (c t) -> p c t", c=NC) for t in (gc, fall))
            nc.vector.tensor_tensor(f3, g3[:, :, C - 1:C].to_broadcast([HG, NC, C]), g3, ALU.subtract).then_inc(cum, 1)
            dve.wait_ge(turned, 1)
            nc.vector.tensor_copy(core.gate_cols[:], core.ps[:, 2, 0:NC * HG])


def head_norms(core, pairs, eps, mean):
    nc = core.nc
    sq = core.slot(9, 2, T)
    squared, summed, floored, rooted = core.semaphores("squared", "summed", "floored", "rooted")
    with nc.Block() as block:
        @block.sync
        def _(sp):
            core.clear_before(sp)

        @block.scalar
        def _(act):
            for n, (t, rows) in enumerate(pairs):
                for h in range(HG):
                    at = n * HG + h
                    if at >= 2:
                        act.wait_ge(summed, at - 1)
                    nc.scalar.activation(sq[:, at % 2], t[:, h], ACT.Square).then_inc(squared, 1)
            for n, (t, rows) in enumerate(pairs):
                act.wait_ge(floored, n + 1)
                nc.scalar.activation(rows, rows, ACT.Sqrt).then_inc(rooted, 1)

        @block.tensor
        def _(pe):
            for n in range(len(pairs)):
                for h in range(HG):
                    at = n * HG + h
                    pe.wait_ge(squared, at + 1)
                    nc.tensor.matmul(core.ps[0:HG, n], core.const("pick8")[:, HG - 1 - h:2 * HG - 1 - h], sq[:, at % 2],
                                     start=h == 0, stop=h == HG - 1).then_inc(summed, 1)

        @block.vector
        def _(dve):
            for n, (t, rows) in enumerate(pairs):
                dve.wait_ge(summed, (n + 1) * HG)
                nc.vector.tensor_scalar(rows, core.ps[0:HG, n], mean, eps, ALU.mult, ALU.add).then_inc(floored, 1)
            for n, (t, rows) in enumerate(pairs):
                dve.wait_ge(rooted, n + 1)
                nc.vector.reciprocal(rows, rows)


def spread_rows(core, jobs):
    nc = core.nc
    spread, used = core.semaphores("spread", "used")
    with nc.Block() as block:
        @block.sync
        def _(sp):
            core.clear_before(sp)

        @block.tensor
        def _(pe):
            for n, (rows, use) in enumerate(jobs):
                for h in range(HG):
                    at = n * HG + h
                    if at >= 4:
                        pe.wait_ge(used, at - 3)
                    nc.tensor.matmul(core.ps[:, at % 4], core.const("spread8", HG)[:, h * P:(h + 1) * P], rows,
                                     start=True, stop=True).then_inc(spread, 1)

        @block.vector
        def _(dve):
            for n, (rows, use) in enumerate(jobs):
                for h in range(HG):
                    at = n * HG + h
                    dve.wait_ge(spread, at + 1)
                    use(dve, h, core.ps[:, at % 4]).then_inc(used, 1)


def gdn_chunks(core):
    nc = core.nc
    q, k, v, o = (core.slot(n, KD, T) for n in (1, 2, 3, 0))

    def tile8(slot, quarter):
        return core.area[:, slot, quarter * 1024:(quarter + 1) * 1024].rearrange("p (h t) -> p h t", h=HG)

    kq = core.slot(5, HG, 2, C)
    k_c, q_dec = tile8(5, 2), tile8(5, 3)
    k_old, v_beta, k_left, left_t = (tile8(6, n) for n in range(4))
    strict, upto = tile8(7, 0), tile8(7, 1)
    lower_t, intra = tile8(7, 2), tile8(7, 3)
    X, XT, W, S = (tile8(8, n) for n in range(4))
    Z, Uu = tile8(9, 0), tile8(9, 1)
    total = core.total[:, 0:HG]
    beta, gc, rise, fall = (core.gate_rows[:, i] for i in range(4))
    ident = core.const("ident")
    G = 2
    nlev = len(LEVELS)
    (staged, spread, differ, decayed, ready, gram_ps, gram_sb, left_ps, left_sb, seed_sb, x_ps, x_sb, w_ps, w_sb, xw_ps,
     x_new, xt_ps, xt_new, z_ps, z_sb, u_ps, u_sb, s_ps, s_new, o_ps, o_sb) = core.semaphores(
        "staged", "spread", "differ", "decayed", "ready", "gram_ps", "gram_sb", "left_ps", "left_sb", "seed_sb", "x_ps",
        "x_sb", "w_ps", "w_sb", "xw_ps", "x_new", "xt_ps", "xt_new", "z_ps", "z_sb", "u_ps", "u_sb", "s_ps", "s_new",
        "o_ps", "o_sb")

    def pair(b):
        return core.ps[:, b:b + 2].rearrange("p b (h t) -> p (b h) t", h=4)

    def chunk(t, c):
        return t[:, :, ds(c * C, C)]

    with nc.Block() as block:
        @block.sync
        def _(sp):
            core.clear_before(sp)

        @block.gpsimd
        def _(pool):
            with pool.Fori(0, NC) as c:
                pool.wait_ge(o_ps, c + 1)
                nc.gpsimd.tensor_copy(k_c, chunk(k, c))
                nc.gpsimd.tensor_copy(kq[:, :, 1], chunk(q, c)).then_inc(staged, 1)

        @block.tensor
        def _(pe):
            pe.sem_inc(o_ps, 1)
            with pe.Fori(0, NC) as c:
                pe.wait_ge(s_new, c + 1)
                pe.wait_ge(o_sb, c + 1)
                for n, rows in enumerate((gc, beta, rise, fall)):
                    for h in range(HG):
                        last = nc.tensor.matmul(core.ps[:, 2 * n + h // 4, (h % 4) * C:(h % 4 + 1) * C],
                                                core.const("spread8", HG)[:, h * P:(h + 1) * P], rows[:, ds(c * C, C)],
                                                start=True, stop=True)
                    last.then_inc(spread, 1)
                pe.wait_ge(ready, c + 1)
                pe.wait_ge(staged, c + 1)
                for h in range(HG):
                    bank = core.ps[:, h // 2, (h % 2) * 2 * C:(h % 2 + 1) * 2 * C]
                    last = nc.tensor.matmul(bank, k_c[:, h], kq[:, h].rearrange("p w t -> p (w t)"), start=True, stop=True)
                    if h % 2:
                        last.then_inc(gram_ps, 1)
                for h in range(HG):
                    last = nc.tensor.transpose(core.ps[:, 4 + h // 4, (h % 4) * C:(h % 4 + 1) * C], k_left[:, h], ident)
                last.then_inc(left_ps, 1)
                invert_products(core, pe, c, G, ident, lambda h: lower_t[:, h], X, XT, W, (left_sb, 1), seed_sb,
                                x_ps, x_sb, w_ps, w_sb, xw_ps, x_new, xt_ps, xt_new)
                for h in range(HG):
                    out = core.ps[:, h // 4, (h % 4) * C:(h % 4 + 1) * C]
                    nc.tensor.matmul(out, k_old[:, h], S[:, h], start=True, stop=False)
                    last = nc.tensor.matmul(out, v_beta[:, h], ident, start=False, stop=True)
                last.then_inc(z_ps, 1)
                pe.wait_ge(z_sb, c + 1)
                for h in range(HG):
                    last = nc.tensor.matmul(core.ps[:, 2 + h // 4, (h % 4) * C:(h % 4 + 1) * C], XT[:, h], Z[:, h],
                                            start=True, stop=True)
                last.then_inc(u_ps, 1)
                pe.wait_ge(u_sb, c + 1)
                for h in range(HG):
                    last = nc.tensor.matmul(core.ps[:, 4 + h // 4, (h % 4) * C:(h % 4 + 1) * C], left_t[:, h], Uu[:, h],
                                            start=True, stop=True)
                last.then_inc(s_ps, 1)
                for h in range(HG):
                    out = core.ps[:, 6 + h // 4, (h % 4) * C:(h % 4 + 1) * C]
                    nc.tensor.matmul(out, S[:, h], q_dec[:, h], start=True, stop=False)
                    last = nc.tensor.matmul(out, Uu[:, h], intra[:, h], start=False, stop=True)
                last.then_inc(o_ps, 1)

        @block.scalar
        def _(act):
            act.sem_inc(o_sb, 1)
            with act.Fori(0, NC) as c:
                act.wait_ge(differ, c + 1)
                nc.scalar.activation(upto, upto, ACT.Exp).then_inc(decayed, 1)
                act.wait_ge(left_ps, c + 1)
                nc.scalar.copy(left_t, pair(4)).then_inc(left_sb, 1)
                for g in range(G):
                    act.wait_ge(x_ps, c * G + (g + 1))
                    nc.scalar.copy(X[:, 4 * g:4 * g + 4].rearrange("p h t -> p (h t)"), core.ps[:, g]).then_inc(x_sb, 1)
                act.wait_ge(z_ps, c + 1)
                nc.scalar.copy(Z, pair(0)).then_inc(z_sb, 1)
                act.wait_ge(u_ps, c + 1)
                nc.scalar.copy(Uu, pair(2)).then_inc(u_sb, 1)
                act.wait_ge(o_ps, c + 2)
                nc.scalar.copy(chunk(o, c), pair(6)).then_inc(o_sb, 1)

        @block.vector
        def _(dve):
            nc.vector.memset(S, 0.0).then_inc(s_new, 1)
            with dve.Fori(0, NC) as c:
                dve.wait_ge(spread, c * 4 + 1)
                for h in range(HG):
                    last = nc.vector.tensor_scalar(upto[:, h], pair(0)[:, h], core.gate_cols[:, ds(c * HG + h, 1)], 0.0,
                                                   ALU.subtract, ALU.min)
                last.then_inc(differ, 1)
                dve.wait_ge(spread, c * 4 + 4)
                nc.vector.tensor_tensor(kq[:, :, 0], chunk(k, c), pair(2), ALU.mult)
                nc.vector.tensor_tensor(v_beta, chunk(v, c), pair(2), ALU.mult)
                nc.vector.tensor_tensor(q_dec, chunk(q, c), pair(4), ALU.mult)
                nc.vector.tensor_tensor(k_left, chunk(k, c), pair(6), ALU.mult)
                nc.vector.tensor_copy(total, pair(4)[:, :, C - 1])
                dve.drain()
                for g in range(G):
                    last = nc.vector.scalar_tensor_tensor(k_old[:, 4 * g:4 * g + 4], kq[:, 4 * g:4 * g + 4, 0], -1.0,
                                                          pair(4)[:, 4 * g:4 * g + 4], ALU.mult, ALU.mult)
                last.then_inc(ready, 1)
                dve.wait_ge(decayed, c + 1)
                nc.vector.tensor_tensor(strict, upto, core.const("upper").unsqueeze(1).to_broadcast([P, HG, C]), ALU.mult)
                dve.drain()
                nc.vector.tensor_tensor(upto, upto, core.const("upto").unsqueeze(1).to_broadcast([P, HG, C]), ALU.mult)
                dve.drain()
                for b in range(4):
                    dve.wait_ge(gram_ps, c * 4 + (b + 1))
                    grams = core.ps[:, b].rearrange("p (h w t) -> p h w t", h=2, w=2)
                    nc.vector.tensor_tensor(lower_t[:, 2 * b:2 * b + 2], grams[:, :, 0], strict[:, 2 * b:2 * b + 2], ALU.mult)
                    nc.vector.tensor_tensor(intra[:, 2 * b:2 * b + 2], grams[:, :, 1], upto[:, 2 * b:2 * b + 2],
                                            ALU.mult).then_inc(gram_sb, 1)
                dve.drain()
                invert_updates(core, dve, c, G, lambda g: lower_t[:, 4 * g:4 * g + 4], X, XT, W,
                               seed_sb, x_sb, w_ps, w_sb, xw_ps, x_new, xt_ps, xt_new)
                dve.wait_ge(s_ps, c + 1)
                dve.wait_ge(o_ps, c + 2)
                nc.vector.tensor_tensor(S, S, total.unsqueeze(2).to_broadcast([P, HG, C]), ALU.mult)
                dve.drain()
                nc.vector.tensor_tensor(S, S, pair(4), ALU.add).then_inc(s_new, 1)


def gdn_mixer(core, A):
    nc = core.nc
    gdn_projections(core, A)
    q, k, o, z = (core.slot(n, KD, T) for n in (1, 2, 0, 4))
    head_norms(core, [(q, core.norm_rows[:, 0]), (k, core.norm_rows[:, 1])], 1e-6, 1.0)
    spread_rows(core, [
        (core.norm_rows[:, 0], lambda dve, h, bank: nc.vector.scalar_tensor_tensor(
            q[:, h], q[:, h], float(P) ** -0.5, bank, ALU.mult, ALU.mult)),
        (core.norm_rows[:, 1], lambda dve, h, bank: nc.vector.tensor_tensor(k[:, h], k[:, h], bank, ALU.mult))])
    gdn_chunks(core)
    head_norms(core, [(o, core.norm_rows[:, 0])], 1e-6, 1.0 / P)

    def gate(dve, h, bank):
        nc.vector.scalar_tensor_tensor(o[:, h], o[:, h], core.col("norm_g"), z[:, h], ALU.mult, ALU.mult)
        dve.drain()
        return nc.vector.tensor_tensor(o[:, h], o[:, h], bank, ALU.mult)

    spread_rows(core, [(core.norm_rows[:, 0], gate)])
    residual(core, 1, 0, A["gdn_w_out"].rearrange("o k n -> (o k) n"),
             (o, core.rounded_tiles(2), core.rounded_tiles(0)), 8)
    layer_norm(core, "ln_g10", "ln_b10")


Q_LORA, KV_LORA, NOPE, ROPE, HM = 384, 256, 128, 64, 4
KQ, KKV = Q_LORA // P, KV_LORA // P
LAT = Q_LORA + KV_LORA
REST = LAT + ROPE
GATES = REST + 4 * 256
RMS_EPS = 1e-6
CQ, CKV, KR, XP, XQK, XV, XO = 0, 3, 5, 6, 8, 10, 12
NPROJ = 14


def layer_projections(core, A, layer):
    nc = core.nc
    x, proj = core.x, core.slot(0, 16, T)
    w = A["w_in_2"][ds(layer, 1)].rearrange("o k n -> (o k) n")

    U = NPROJ // 2

    def feed(sp, ring, loaded, done):
        for j in range(NPROJ):
            if j >= U:
                sp.wait_ge(done, j + 1)
            to, into = ring[:, j % U], loaded[j % U]
            if j == KR:
                for half in range(2):
                    sp.dma_start(to[:, :, half * ROPE:(half + 1) * ROPE],
                                 w[:, LAT:REST].rearrange("(k p) m -> p k m", p=P)).then_inc(into, 16)
            else:
                sp.dma_start(to, w[:, (j * P if j < KR else REST + (j - XP) * P):][:, 0:P].rearrange(
                    "(k p) m -> p k m", p=P)).then_inc(into, 16)

    products(core, NPROJ, KD, None, (x, core.rounded_tiles(2), core.rounded_tiles(3)), 4,
             scalar=lambda act, j, banks, s, more: nc.scalar.copy(flat(proj[:, ds(j, 1)]), banks[0]), U=U, feed=feed, twice=(KR,))

    wg = core.slot(5, KD, 2 * HM)
    bias = core.total[0:HM, 0:2]
    li, xf = core.m_rows[:, 0], core.m_rows[:, 1]
    tables = core.slot(3, KD * T)[:, 3 * T:3 * T + CONST.shape[1] - CONST_KEPT]
    loaded, summed = core.semaphores("loaded", "summed")
    with nc.Block() as block:
        @block.sync
        def _(sp):
            core.clear_before(sp)
            sp.dma_start(wg, w[:, GATES:GATES + 2 * HM].rearrange("(k p) m -> p k m", p=P)).then_inc(loaded, 16)
            for n, name in enumerate(("b_i_2", "b_f_2")):
                sp.dma_start(bias[:, n:n + 1], A[name][ds(layer, 1)].rearrange("o h -> h o")).then_inc(loaded, 16)
            sp.dma_start(tables, core.const_dram[:, CONST_KEPT:CONST.shape[1]]).then_inc(loaded, 16)
            sp.wait_ge(loaded, 64)

        @block.tensor
        def _(pe):
            pe.wait_ge(loaded, 64)
            for q in range(2):
                for k in range(KD):
                    last = nc.tensor.matmul(core.ps[0:HM, 1 + q], wg[:, k, q * HM:(q + 1) * HM], x[:, k],
                                            start=k == 0, stop=k == KD - 1)
            last.then_inc(summed, 1)

        @block.vector
        def _(dve):
            dve.wait_ge(summed, 1)
            nc.vector.tensor_scalar(li, core.ps[0:HM, 1], bias[:, 0:1], None, ALU.add)
            nc.vector.tensor_scalar(xf, core.ps[0:HM, 2], bias[:, 1:2], None, ALU.add)


def table(core, name):
    at, n = CONST_AT[name]
    return core.slot(3, KD * T)[:, 3 * T + at - CONST_KEPT:3 * T + at - CONST_KEPT + n]


def latent_heads(core, A, layer):
    nc = core.nc
    proj, spare = core.slot(0, 16, T), core.slot(0, 16, T)[:, NPROJ:]
    wq, wkv = core.slot(4, KQ, HM * (NOPE + ROPE)), core.slot(5, KKV, HM * 2 * NOPE)
    v = core.slot(5, KD * T)[:, 2048:4096].rearrange("p (a n) -> p a n", a=4)
    qn, kn = core.slot(2, HM, T), core.slot(2, KD, T)[:, HM:2 * HM]
    qp, kp = core.slot(3, 2, T), core.slot(3, KD, T)[:, 2]
    sq = core.slot(9, 2, T)
    rstd = core.slot(9, KD, T)[:, 2:4]
    scale = float((NOPE + ROPE) ** -0.5)
    (loaded, squared, square_used, floored, rooted, normed, q_ps, q_out, kv_ps, kv_out, v_ps, v_out, raw, turned,
     turned_used) = core.semaphores(
        "loaded", "squared", "square_used", "floored", "rooted", "normed", "q_ps", "q_out", "kv_ps", "kv_out", "v_ps",
        "v_out", "raw", "turned", "turned_used")
    latents = ((CQ, KQ, "g_qn", 1.0 / Q_LORA), (CKV, KKV, "g_kvn", 1.0 / KV_LORA))
    rotary = (qp[:, 0], qp[:, 1], kp)
    with nc.Block() as block:
        @block.sync
        def _(sp):
            core.clear_before(sp)
            sp.dma_start(wq, A["w_uq_2"][ds(layer, 1)].rearrange("o (k p) n -> p (o k) n", p=P)).then_inc(loaded, 16)
            sp.dma_start(wkv, A["w_ukv_2"][ds(layer, 1)].rearrange("o (k p) n -> p (o k) n", p=P)).then_inc(loaded, 16)

        @block.scalar
        def _(act):
            n = 0
            for first, kt, g, mean in latents:
                for k in range(kt):
                    if n >= 2:
                        act.wait_ge(square_used, n - 1)
                    nc.scalar.activation(sq[:, n % 2], proj[:, first + k], ACT.Square).then_inc(squared, 1)
                    n += 1
            for i in range(2):
                act.wait_ge(floored, i + 1)
                nc.scalar.activation(rstd[:, i], rstd[:, i], ACT.Sqrt).then_inc(rooted, 1)
            for h in range(HM):
                act.wait_ge(q_ps, h + 1)
                nc.scalar.mul(qn[:, h], core.ps[:, 2 + h % 2], scale).then_inc(q_out, 1)
            for j in range(2):
                act.wait_ge(q_ps, HM + j + 1)
                nc.scalar.mul(qp[:, j], core.ps[:, 2 + j], scale).then_inc(q_out, 1)
            for h in range(HM):
                act.wait_ge(kv_ps, h + 1)
                nc.scalar.copy(kn[:, h], core.ps[:, 4 + h % 2]).then_inc(kv_out, 1)
            for a in range(4):
                act.wait_ge(v_ps, a + 1)
                nc.scalar.copy(v[:, a], core.ps[:, 6 + a % 2]).then_inc(v_out, 1)

        @block.tensor
        def _(pe):
            n = 0
            for i, (first, kt, g, mean) in enumerate(latents):
                for k in range(kt):
                    pe.wait_ge(squared, n + 1)
                    nc.tensor.matmul(core.ps[:, i], core.const("ones"), sq[:, n % 2], start=k == 0,
                                     stop=k == kt - 1).then_inc(square_used, 1)
                    n += 1
            pe.wait_ge(loaded, 32)
            pe.wait_ge(normed, KQ)
            for h in range(HM):
                if h >= 2:
                    pe.wait_ge(q_out, h - 1)
                for k in range(KQ):
                    last = nc.tensor.matmul(core.ps[:, 2 + h % 2], wq[:, k, h * (NOPE + ROPE):h * (NOPE + ROPE) + NOPE],
                                            proj[:, CQ + k], start=k == 0, stop=k == KQ - 1)
                last.then_inc(q_ps, 1)
            for j in range(2):
                pe.wait_ge(q_out, HM - 1 + j)
                for half in range(2):
                    at = (2 * j + half) * (NOPE + ROPE) + NOPE
                    for k in range(KQ):
                        last = nc.tensor.matmul(core.ps[half * ROPE:(half + 1) * ROPE, 2 + j], wq[:, k, at:at + ROPE],
                                                proj[:, CQ + k], start=k == 0, stop=k == KQ - 1)
                last.then_inc(q_ps, 1)
            pe.wait_ge(normed, KQ + KKV)
            for h in range(HM):
                if h >= 2:
                    pe.wait_ge(kv_out, h - 1)
                for k in range(KKV):
                    last = nc.tensor.matmul(core.ps[:, 4 + h % 2], wkv[:, k, h * 2 * NOPE:h * 2 * NOPE + NOPE],
                                            proj[:, CKV + k], start=k == 0, stop=k == KKV - 1)
                last.then_inc(kv_ps, 1)
            values = wkv.rearrange("p k (h m) -> p k h m", h=HM)
            for a in range(4):
                if a >= 2:
                    pe.wait_ge(v_out, a - 1)
                for k in range(KKV):
                    last = nc.tensor.matmul(core.ps[:, 6 + a % 2], proj[:, CKV + k, a * P:(a + 1) * P],
                                            values[:, k, :, NOPE:2 * NOPE], start=k == 0, stop=k == KKV - 1)
                last.then_inc(v_ps, 1)
            for i, t in enumerate((qp[:, 0], qp[:, 1], proj[:, KR])):
                if i < 2:
                    pe.wait_ge(q_out, HM + i + 1)
                else:
                    pe.wait_ge(turned_used, 1)
                nc.tensor.matmul(core.ps[:, i % 2], table(core, "turn"), t, start=True, stop=True).then_inc(turned, 1)

        @block.vector
        def _(dve):
            n = 0
            for i, (first, kt, g, mean) in enumerate(latents):
                n += kt
                dve.wait_ge(square_used, n)
                nc.vector.tensor_scalar(rstd[:, i], core.ps[:, i], mean, RMS_EPS, ALU.mult, ALU.add).then_inc(floored, 1)
            for i, (first, kt, g, mean) in enumerate(latents):
                dve.wait_ge(rooted, i + 1)
                nc.vector.reciprocal(rstd[:, i], rstd[:, i])
                dve.drain()
                for k in range(kt):
                    nc.vector.scalar_tensor_tensor(proj[:, first + k], proj[:, first + k], core.col(g, k), rstd[:, i],
                                                   ALU.mult, ALU.mult).then_inc(normed, 1)
            for i, (t, out) in enumerate(((qp[:, 0], qp[:, 0]), (qp[:, 1], qp[:, 1]), (proj[:, KR], kp))):
                dve.wait_ge(turned, i + 1)
                nc.vector.tensor_tensor(spare[:, 0], core.ps[:, i % 2], table(core, "sin"), ALU.mult).then_inc(turned_used, 1)
                nc.vector.tensor_tensor(spare[:, 1], t, table(core, "cos"), ALU.mult)
                dve.drain()
                nc.vector.tensor_tensor(out, spare[:, 0], spare[:, 1], ALU.add)
                dve.drain()


def latent_attention(core):
    nc = core.nc
    v = core.slot(5, KD * T)[:, 2048:4096].rearrange("p (a n) -> p a n", a=4)
    qn, kn = core.slot(2, HM, T), core.slot(2, KD, T)[:, HM:2 * HM]
    qp, kp = core.slot(3, 2, T), core.slot(3, KD, T)[:, 2]
    prob, prob_t = core.slot(6, 2, T), core.slot(6, KD, T)[:, 2:4]
    out = core.slot(7, KD, T)
    small = core.mid[:]
    items = [(h, a) for h in range(HM) for a in range(4)]
    (s_ps, masked, peak, risen, weighed, t_ps, t_out, o_ps, o_out) = core.semaphores(
        "s_ps", "masked", "peak", "risen", "weighed", "t_ps", "t_out", "o_ps", "o_out")
    with nc.Block() as block:
        @block.sync
        def _(sp):
            core.clear_before(sp)

        @block.tensor
        def _(pe):
            def scores(n):
                h, a = items[n]
                lo, end = 64 * (h % 2), (a + 1) * P
                if n >= 2:
                    pe.wait_ge(risen, n - 1)
                bank = core.ps[:, n % 2, 0:end]
                nc.tensor.matmul(bank, qn[:, h, a * P:end], kn[:, h, 0:end], start=True, stop=False)
                nc.tensor.matmul(bank, qp[lo:lo + 64, h // 2, a * P:end], kp[lo:lo + 64, 0:end], start=False,
                                 stop=True).then_inc(s_ps, 1)

            def values(n):
                h, a = items[n]
                pe.wait_ge(weighed, n + 1)
                if n >= 2:
                    pe.wait_ge(t_out, n - 1)
                for b in range(a + 1):
                    last = nc.tensor.transpose(core.ps[:, 2 + n % 2, b * P:(b + 1) * P], prob[:, n % 2, b * P:(b + 1) * P],
                                               core.const("ident"))
                last.then_inc(t_ps, 1)
                pe.wait_ge(t_out, n + 1)
                if n >= 2:
                    pe.wait_ge(o_out, n - 1)
                for b in range(a + 1):
                    last = nc.tensor.matmul(core.ps[:, 4 + n % 2, 0:P], v[:, b, h * NOPE:(h + 1) * NOPE],
                                            prob_t[:, n % 2, b * P:(b + 1) * P], start=b == 0, stop=b == a)
                last.then_inc(o_ps, 1)

            scores(0)
            for n in range(len(items)):
                if n + 1 < len(items):
                    scores(n + 1)
                values(n)

        @block.vector
        def _(dve):
            for n, (h, a) in enumerate(items):
                end = (a + 1) * P
                bank = core.ps[:, n % 2]
                top, total, part = (small[:, 3 * (n % 2) + i:3 * (n % 2) + i + 1] for i in range(3))
                dve.wait_ge(s_ps, n + 1)
                nc.vector.tensor_tensor(bank[:, a * P:end], bank[:, a * P:end], table(core, "later"), ALU.add)
                dve.drain()
                nc.vector.tensor_reduce(top, bank[:, 0:end], AX_X, ALU.max, negate=True).then_inc(peak, 1)
                dve.wait_ge(risen, n + 1)
                nc.vector.reciprocal(part, total)
                dve.drain()
                nc.vector.tensor_scalar(prob[:, n % 2, 0:end], prob[:, n % 2, 0:end], part, None,
                                        ALU.mult).then_inc(weighed, 1)

        @block.scalar
        def _(act):
            for n, (h, a) in enumerate(items):
                end = (a + 1) * P
                top, total = (small[:, 3 * (n % 2) + i:3 * (n % 2) + i + 1] for i in range(2))
                act.wait_ge(peak, n + 1)
                if n >= 2:
                    act.wait_ge(t_ps, n - 1)
                nc.scalar.activation(prob[:, n % 2, 0:end], core.ps[:, n % 2, 0:end], ACT.Exp, bias=top,
                                     accum_out=total).then_inc(risen, 1)
                act.wait_ge(t_ps, n + 1)
                if n >= 2:
                    act.wait_ge(o_ps, n - 1)
                nc.scalar.copy(prob_t[:, n % 2, 0:end], core.ps[:, 2 + n % 2, 0:end]).then_inc(t_out, 1)
                act.wait_ge(o_ps, n + 1)
                nc.scalar.copy(out[:, h, a * P:end], core.ps[:, 4 + n % 2, 0:P]).then_inc(o_out, 1)


def pool_and_prepare(core, A, layer):
    nc = core.nc
    proj, out = core.slot(0, 16, T), core.slot(7, KD, T)
    sums = core.slot(4, 4, T)
    weights = core.slot(5, KD * T)[:, 0:6 * 64].rearrange("p (w k m) -> p w k m", w=3, k=2)
    conv, q, k = core.slot(8, 2, T), core.slot(8, KD, T)[:, 2:4], core.slot(8, KD, T)[:, 4:6]
    v = core.slot(8, KD * T)[:, 6 * T:6 * T + 4 * 256].rearrange("p (a n) -> p a n", a=4)
    li, xf, soft, B, F, M, floor = (core.m_rows[:, i] for i in range(7))
    ones_row = core.slot(6, KD * T)[0:HM, 7 * T:8 * T]
    (loaded, convolved, activated, pooled, p_ps, qk_ps, qk_out, v_ps, soft_done, rows_done, floor_done,
     cols_ps) = core.semaphores(
        "loaded", "convolved", "activated", "pooled", "p_ps", "qk_ps", "qk_out", "v_ps", "soft_done", "rows_done",
        "floor_done", "cols_ps")
    with nc.Block() as block:
        @block.sync
        def _(sp):
            core.clear_before(sp)
            for w, name in enumerate(("w_pool_2", "w_mq_2", "w_mk_2")):
                for lo in range(2):
                    for t in range(2):
                        sp.dma_start(weights[64 * lo:64 * lo + 64, w, t],
                                     A[name][ds(layer, 1), 2 * t + lo].rearrange("o c m -> (o c) m")).then_inc(loaded, 16)

        @block.vector
        def _(dve):
            for t in range(2):
                tap = lambda j: core.col("w_mconv", j * 2 + t)
                causal_conv(nc, dve, conv[:, t], proj[:, XQK + t], tap, TAPS).then_inc(convolved, 1)
            nc.vector.memset(ones_row, 1.0)
            nc.vector.tensor_scalar(F, xf, 0.0, None, ALU.min)
            dve.wait_ge(soft_done, 1)
            dve.drain()
            nc.vector.tensor_tensor(xf, F, soft, ALU.subtract)
            dve.drain()
            nc.vector.tensor_tensor_scan(B, ones_row, xf, 0.0, ALU.mult, ALU.add)
            dve.drain()
            nc.vector.tensor_tensor(F, li, B, ALU.subtract)
            dve.drain()
            nc.vector.tensor_tensor_scan(M, F, F, 0.0, ALU.max, ALU.max)
            dve.drain()
            nc.vector.tensor_tensor(floor, B, M, ALU.add).then_inc(rows_done, 1)
            for t in range(2):
                x = proj[:, XP + t]
                src = x
                at = 0
                for step in range(2 * t + 2):
                    lo = 64 if step == 2 * t + 1 else 0
                    dst, shift = sums[:, at % 4], 1 << step
                    if lo:
                        nc.vector.tensor_copy(dst[0:64], src[0:64])
                    nc.vector.tensor_copy(dst[lo:P, 0:shift], src[lo:P, 0:shift])
                    nc.vector.tensor_tensor(dst[lo:P, shift:T], src[lo:P, shift:T], src[lo:P, 0:T - shift], ALU.add)
                    dve.drain()
                    src = dst
                    at += 1
                nc.vector.tensor_tensor(src, src, table(core, f"count{t}"), ALU.mult)
                dve.drain()
                nc.vector.tensor_tensor(x, src, x, ALU.subtract).then_inc(pooled, 1)
                dve.drain()
            for t in range(2):
                dve.wait_ge(p_ps, t + 1)
                nc.vector.tensor_scalar(out[:, HM + t], core.ps[:, t], core.col("s_pool", t), None, ALU.mult)
            dve.wait_ge(cols_ps, 1)
            nc.vector.tensor_copy(core.first[:, 0:4 * HM], core.ps[:, 6, 0:4 * HM])

        @block.scalar
        def _(act):
            nc.scalar.activation(soft, xf, ACT.Abs)
            act.drain()
            nc.scalar.activation(soft, soft, ACT.Exp, scale=-1.0)
            act.drain()
            nc.scalar.activation(soft, soft, ACT.Ln, bias=1.0).then_inc(soft_done, 1)
            for t in range(2):
                act.wait_ge(convolved, t + 1)
                nc.scalar.activation(conv[:, t], conv[:, t], ACT.Silu, bias=core.col("b_mconv", t)).then_inc(activated, 1)
            for t in range(2):
                act.wait_ge(qk_ps, t + 1)
                nc.scalar.copy(q[:, t], core.ps[:, 2 + t])
                nc.scalar.mul(k[:, t], core.ps[:, 4 + t], 64.0 ** -0.5).then_inc(qk_out, 1)
            for a in range(2):
                act.wait_ge(v_ps, a + 1)
                nc.scalar.copy(v[:, 2 * a:2 * a + 2].rearrange("p a n -> p (a n)"), core.ps[:, 7 - 5 * a])
            act.wait_ge(rows_done, 1)
            nc.scalar.activation(floor, floor, ACT.Exp, scale=-1.0).then_inc(floor_done, 1)

        @block.tensor
        def _(pe):
            pe.wait_ge(loaded, 12 * 16)
            for t in range(2):
                pe.wait_ge(activated, t + 1)
                for w in (1, 2):
                    for lo in (0, 64):
                        last = nc.tensor.matmul(core.ps[lo:lo + 64, 2 * w + t], weights[lo:lo + 64, w, t],
                                                conv[lo:lo + 64, t], start=True, stop=True)
                last.then_inc(qk_ps, 1)
            pe.wait_ge(qk_out, 2)
            for a in range(4):
                for t in range(2):
                    bank = core.ps[:, 7 - 5 * (a // 2)]
                    at = (a % 2) * 256 + t * P
                    last = nc.tensor.transpose(bank[:, at:at + P], proj[:, XV + t, a * P:(a + 1) * P], core.const("ident"))
                if a % 2:
                    last.then_inc(v_ps, 1)
            pe.wait_ge(rows_done, 1)
            for a in range(4):
                last = nc.tensor.transpose(core.ps[:, 6, a * HM:(a + 1) * HM], F[:, a * P:(a + 1) * P],
                                           core.const("ident", HM)[:, 0:HM])
            last.then_inc(cols_ps, 1)
            for t in range(2):
                pe.wait_ge(pooled, t + 1)
                for lo in (0, 64):
                    last = nc.tensor.matmul(core.ps[lo:lo + 64, t], weights[lo:lo + 64, 0, t],
                                            proj[lo:lo + 64, XP + t], start=True, stop=True)
                last.then_inc(p_ps, 1)


def mlstm(core):
    nc = core.nc
    proj, out = core.slot(0, 16, T), core.slot(7, KD, T)
    q, k = core.slot(8, KD, T)[:, 2:4], core.slot(8, KD, T)[:, 4:6]
    v = core.slot(8, KD * T)[:, 6 * T:6 * T + 4 * 256].rearrange("p (a n) -> p a n", a=4)
    M, floor, den = core.m_rows[:, 5], core.m_rows[:, 6], core.m_rows[:, 2]
    weight, gram = core.slot(4, 2, T), core.slot(4, KD, T)[:, 2:4]
    sq, rstd = core.slot(4, KD, T)[:, 4:6], core.slot(4, KD, T)[:, 6:8]
    items = [(h, a) for h in range(HM) for a in range(4)]
    (m_ps, s_ps, differ, risen, weighed, used, den_abs, den_done, den_ps, centred_ps, centred,
     squared, var_ps, floored, rooted, opened) = core.semaphores(
        "m_ps", "s_ps", "differ", "risen", "weighed", "used", "den_abs", "den_done", "den_ps",
        "centred_ps", "centred", "squared", "var_ps", "floored", "rooted", "opened")
    with nc.Block() as block:
        @block.sync
        def _(sp):
            core.clear_before(sp)

        @block.tensor
        def _(pe):
            def scores(n):
                h, a = items[n]
                lo = 64 * (h % 2)
                if a == 0:
                    if h >= 2:
                        pe.wait_ge(differ, 4 * (h - 1))
                    nc.tensor.matmul(core.ps[:, h % 2], core.const("spread8", HM)[:, h * P:(h + 1) * P], M,
                                     start=True, stop=True).then_inc(m_ps, 1)
                if n >= 2:
                    pe.wait_ge(weighed, n - 1)
                nc.tensor.matmul(core.ps[:, 2 + n % 2, a * P:T], k[lo:lo + 64, h // 2, a * P:(a + 1) * P],
                                 q[lo:lo + 64, h // 2, a * P:T], start=True, stop=True).then_inc(s_ps, 1)

            def values(n):
                h, a = items[n]
                lo = 64 * (h % 2)
                pe.wait_ge(weighed, n + 1)
                g = gram[:, n % 2, a * P:T]
                nc.tensor.matmul(core.ps[lo:lo + 64, 4 + h // 2, a * P:T], v[:, a, h * 64:(h + 1) * 64], g,
                                 start=a == 0, stop=a == 3, skip_group_check=True)
                nc.tensor.matmul(core.ps[0:HM, 6, a * P:T], core.const("pick8")[:, HG - 1 - h:HG - 1 - h + HM], g,
                                 start=n == 0, stop=n == len(items) - 1, skip_group_check=True).then_inc(used, 1)

            scores(0)
            for n in range(len(items)):
                if n + 1 < len(items):
                    scores(n + 1)
                values(n)
            pe.wait_ge(den_done, 1)
            for t in range(2):
                nc.tensor.matmul(core.ps[:, t], core.const("spread16", HM)[:, t * P:(t + 1) * P], den, start=True,
                                 stop=True).then_inc(den_ps, 1)
            for t in range(2):
                pe.wait_ge(den_abs, 2 + t)
                nc.tensor.matmul(core.ps[:, 2 + t], core.const("head64"), out[:, 6 + t], start=True,
                                 stop=True).then_inc(centred_ps, 1)
            for t in range(2):
                pe.wait_ge(squared, t + 1)
                nc.tensor.matmul(core.ps[:, 4 + t], core.const("head64"), sq[:, t], start=True,
                                 stop=True).then_inc(var_ps, 1)

        @block.vector
        def _(dve):
            def weigh(n):
                h, a = items[n]
                dve.wait_ge(s_ps, n + 1)
                dve.wait_ge(risen, n + 1)
                if n >= 2:
                    dve.wait_ge(used, n - 1)
                w, g = weight[:, n % 2], gram[:, n % 2]
                nc.vector.tensor_tensor(w[:, a * P:(a + 1) * P], w[:, a * P:(a + 1) * P], core.const("upto"), ALU.mult)
                dve.drain()
                nc.vector.tensor_tensor(g[:, a * P:T], core.ps[:, 2 + n % 2, a * P:T], w[:, a * P:T],
                                        ALU.mult).then_inc(weighed, 1)

            for n, (h, a) in enumerate(items):
                dve.wait_ge(m_ps, h + 1)
                if n >= 2:
                    dve.wait_ge(weighed, n - 1)
                w = weight[:, n % 2, a * P:T]
                nc.vector.tensor_scalar(w, core.ps[:, h % 2, a * P:T], core.first[:, a * HM + h:a * HM + h + 1], 0.0,
                                        ALU.subtract, ALU.max).then_inc(differ, 1)
                if n >= 1:
                    weigh(n - 1)
            weigh(len(items) - 1)
            dve.wait_ge(den_abs, 1)
            nc.vector.tensor_tensor(den, den, floor, ALU.max)
            dve.drain()
            nc.vector.reciprocal(den, den).then_inc(den_done, 1)
            for t in range(2):
                dve.wait_ge(den_ps, t + 1)
                nc.vector.tensor_copy(rstd[:, t], core.ps[:, t])
                dve.drain()
                nc.vector.tensor_tensor(out[:, 6 + t], core.ps[:, 4 + t], rstd[:, t], ALU.mult).then_inc(den_abs, 1)
            for t in range(2):
                dve.wait_ge(centred_ps, t + 1)
                dve.drain()
                nc.vector.scalar_tensor_tensor(out[:, 6 + t], core.ps[:, 2 + t], -1.0 / 64, out[:, 6 + t], ALU.mult,
                                               ALU.add).then_inc(centred, 1)
            for t in range(2):
                dve.wait_ge(var_ps, t + 1)
                nc.vector.tensor_scalar(rstd[:, t], core.ps[:, 4 + t], 1.0 / 64, LN_EPS, ALU.mult,
                                        ALU.add).then_inc(floored, 1)
            for t in range(2):
                dve.wait_ge(rooted, t + 1)
                nc.vector.reciprocal(rstd[:, t], rstd[:, t])
                dve.drain()
                nc.vector.scalar_tensor_tensor(out[:, 6 + t], out[:, 6 + t], core.col("g_mh", t), rstd[:, t], ALU.mult,
                                               ALU.mult)
                dve.drain()
                dve.wait_ge(opened, t + 1)
                nc.vector.tensor_tensor(out[:, 6 + t], out[:, 6 + t], proj[:, XO + t], ALU.mult)

        @block.scalar
        def _(act):
            for n, (h, a) in enumerate(items):
                act.wait_ge(differ, n + 1)
                nc.scalar.activation(weight[:, n % 2, a * P:T], weight[:, n % 2, a * P:T], ACT.Exp,
                                     scale=-1.0).then_inc(risen, 1)
            act.wait_ge(used, len(items))
            nc.scalar.activation(den, core.ps[0:HM, 6], ACT.Abs).then_inc(den_abs, 1)
            for t in range(2):
                act.wait_ge(centred, t + 1)
                nc.scalar.activation(sq[:, t], out[:, 6 + t], ACT.Square).then_inc(squared, 1)
            for t in range(2):
                act.wait_ge(floored, t + 1)
                nc.scalar.activation(rstd[:, t], rstd[:, t], ACT.Sqrt).then_inc(rooted, 1)
            for t in range(2):
                nc.scalar.activation(proj[:, XO + t], proj[:, XO + t], ACT.Sigmoid).then_inc(opened, 1)


def store_output(core, out):
    nc = core.nc
    rows = core.slot(0, 4, D)
    turned, copied, stored = core.semaphores("turned", "copied", "stored")
    with nc.Block() as block:
        @block.sync
        def _(sp):
            core.clear_before(sp)
            for a in range(4):
                sp.wait_ge(copied, 2 * (a + 1))
                sp.dma_start(out[0, a * P:(a + 1) * P, :], rows[:, a]).then_inc(stored, 16)
            sp.wait_ge(stored, 64)

        @block.tensor
        def _(pe):
            for a in range(4):
                for half in range(2):
                    n = 2 * a + half
                    if n >= 4:
                        pe.wait_ge(copied, n - 3)
                    for j in range(4):
                        last = nc.tensor.transpose(core.ps[:, n % 4, j * P:(j + 1) * P],
                                                   core.x[:, 4 * half + j, a * P:(a + 1) * P], core.const("ident"))
                    last.then_inc(turned, 1)

        @block.vector
        def _(dve):
            for n in range(8):
                dve.wait_ge(turned, n + 1)
                nc.vector.tensor_copy(rows[:, n // 2, (n % 2) * 512:(n % 2 + 1) * 512], core.ps[:, n % 4]).then_inc(copied, 1)


def network(nc, A, const, out, stop=None):
    with ExitStack() as ctx:
        core = Core(nc, ctx, const)
        core.lora_inner = core.sb("lora_inner", [P, 3, T])
        core.mid, core.first, core.ends = (core.sb(n, [P, KD * NC]) for n in ("mid", "first", "ends"))
        core.bonus = core.sb("bonus", [HR, T])
        core.gate_rows = core.slot(9, KD, T)[0:HG, 4:8]
        core.gate_cols, core.total = core.first, core.mid
        core.norm_rows = core.lora_inner[0:HG]
        core.one_less_k_a = core.sb("one_less_k_a", [P, KD])

        def rows(ap, pattern, **sizes):
            return ap.rearrange(pattern, **sizes)

        def vec(name, layer=0):
            return A[name][layer:layer + 1].rearrange("o (r p) -> (o r) p", p=P)

        groups = [
            [("ada_b0", vec("ada_b", 0))] +
            [(f"ln_g{i}{j}", A["ln_g"][i, j:j + 1].rearrange("o (r p) -> (o r) p", p=P)) for i in range(2) for j in range(2)] +
            [(f"ln_b{i}{j}", A["ln_b"][i, j:j + 1].rearrange("o (r p) -> (o r) p", p=P)) for i in range(2) for j in range(2)] +
            [("c", vec("c"))],
            [("ada_b1", vec("ada_b", 1)), ("mu", A["rwkv_mu"].rearrange("o i (r p) -> (o i r) p", p=P))] +
            [(n, vec("rwkv_" + n)) for n in ("w0", "a0", "k_k", "k_a")],
            [("r_k", A["rwkv_r_k"].rearrange("o (r a) n -> (o r) (a n)", a=2))] +
            [(n, vec("rwkv_" + n)) for n in ("gn_g", "gn_b")] +
            [("conv", A["gdn_conv"].rearrange("o i (r p) -> (o i r) p", p=P)), ("norm_g", A["gdn_norm_g"])],
            [("ln0_g", A["ln0_g_2"].rearrange("(r p) -> r p", p=P)), ("ln0_b", A["ln0_b_2"].rearrange("(r p) -> r p", p=P))],
        ]
        turn_rows(core, [(core.const_sb[:], const[:, 0:CONST_KEPT])], groups)
        load_x(core, A["x"])
        modulation(core, 0, A["ada_w"])
        one_less(core)
        rwkv_projections(core, A)
        rwkv_decays(core)
        rwkv_chunks(core)
        rwkv_output(core, A)
        feed_forward(core, 0, A["ffn_w_in"][0], A["ffn_w_out"][0])
        layer_norm(core, "ln_g01", "ln_b01")
        modulation(core, 1, A["ada_w"])
        gdn_mixer(core, A)
        feed_forward(core, 1, A["ffn_w_in"][1], A["ffn_w_out"][1])
        layer_norm(core, "ln_g11", "ln_b11")

        layer_norm(core, "ln0_g", "ln0_b")
        core.m_rows = core.slot(6, KD, T)[0:HM]
        core.clear_all()
        with nc.Fori(0, 2) as layer:
            core.n_cols = 0

            def of_layer(name, pattern="o (r p) -> (o r) p"):
                return A[name + "_2"][ds(layer, 1)].rearrange(pattern, p=P)

            turn_rows(core, [], [
                [(n, of_layer(n)) for n in ("g_qn", "g_kvn", "s_pool", "b_mconv", "g_mh", "ln1_g", "ln1_b", "ln2_g", "ln2_b")] +
                [("w_mconv", of_layer("w_mconv", "o i (r p) -> (o i r) p"))],
                [("w_fconv", of_layer("w_fconv", "o i (r p) -> (o i r) p")), ("b_fconv", of_layer("b_fconv"))],
            ])
            layer_projections(core, A, layer)
            latent_heads(core, A, layer)
            pool_and_prepare(core, A, layer)
            mlstm(core)
            latent_attention(core)
            mixed = core.slot(7, KD, T)
            residual(core, None, 0, flat_rows(A["w_out_2"], layer), (mixed, core.rounded_tiles(0), core.rounded_tiles(7)), 8)
            layer_norm(core, "ln1_g", "ln1_b")
            feed_forward(core, None, flat_rows(A["w_up_2"], layer), flat_rows(A["w_down_2"], layer), gate_first=False,
                         conv=(core.col_at["w_fconv"], core.col_at["b_fconv"], 3))
            layer_norm(core, "ln2_g", "ln2_b")
            core.clear_all()
        store_output(core, out)


def flat_rows(w, layer):
    return w[ds(layer, 1)].rearrange("o k n -> (o k) n")


def one_less(core):
    nc = core.nc
    core.semaphores()
    with nc.Block() as block:
        @block.sync
        def _(sp):
            core.clear_before(sp)

        @block.vector
        def _(dve):
            nc.vector.tensor_scalar(core.one_less_k_a[:], core.col("k_a", 0, KD), -1.0, 1.0, ALU.mult, ALU.add)


_OUTS = [((1, T, D), "float32")]


def kernel(**inputs):
    import concourse.bacc as _bacc
    from concourse.bass_utils import run_bass_kernel_spmd as _run

    nc = _bacc.Bacc("TRN2", target_bir_lowering=False, num_devices=1)
    arrays, A = {}, {}
    for name, value in inputs.items():
        if name.split("_")[0] in ("diff", "swa"):
            continue
        a = np.ascontiguousarray(value)
        arrays[f"in_{name}_dram"] = a
        A[name] = nc.dram_tensor(f"in_{name}_dram", a.shape, mybir.dt.from_np(a.dtype), kind="ExternalInput").ap()
    arrays["const_dram"] = CONST
    const = nc.dram_tensor("const_dram", CONST.shape, F32, kind="ExternalInput").ap()
    shape, dtype = _OUTS[0]
    out = nc.dram_tensor("out_0_dram", shape, mybir.dt.from_np(np.dtype(dtype)), kind="ExternalOutput").ap()
    network(nc, A, const, out)
    r = _run(nc, [arrays], core_ids=[0])
    return r.results[0]["out_0_dram"]
```

```python
from contextlib import ExitStack

import concourse.bass as bass
import numpy as np
from concourse import mybir

F32 = mybir.dt.float32
F32R = mybir.dt.float32r
U32 = mybir.dt.uint32
ALU = mybir.AluOpType
ACT = mybir.ActivationFunctionType
AX_X = mybir.AxisListType.X
ds = bass.ds

P = 128
T = 512
D = 1024
KD = D // P
FF = 2816
KF = FF // P
C = 128
NC = T // C
ALPHA = 4.0 ** 0.25
LN_EPS = 1e-5
LEVELS = (2, 4, 8, 16, 32, 64)


def constants():
    i = np.arange(P)[:, None]
    j = np.arange(P)[None, :]
    parts = {
        "ident": np.eye(P),
        "ones": np.ones((P, P)),
        "head64": (i // 64 == j // 64) * 1.0,
        "upper": (i < j) * 1.0,
        "upto": (i <= j) * 1.0,
        "corner1": ((j % 2 == 1) & (i == j - 1)) * 1.0,
    }
    for b in LEVELS:
        parts[f"corner{b}"] = (((i // b) % 2 == 1) & (j // b == i // b - 1)) * 1.0
    parts["heads16"] = np.concatenate(
        [np.stack([(np.arange(P) // 64 + 2 * p == h) for h in range(16)], 1) for p in range(8)], 1) * 1.0
    spread16 = np.zeros((P, 8 * P))
    for p in range(8):
        for m in range(P):
            spread16[2 * p + m // 64, p * P + m] = 1.0
    parts["spread16"] = spread16
    spread8 = np.zeros((P, 8 * P))
    for h in range(8):
        spread8[h, h * P:(h + 1) * P] = 1.0
    parts["spread8"] = spread8
    parts["pick8"] = np.broadcast_to((np.arange(15) == 7) * 1.0, (P, 15))
    parts["carry"] = np.broadcast_to((np.arange(T) % C != 0) * 1.0, (P, T))
    inv = 1.0 / (10000.0 ** (np.arange(0, 64, 2, dtype=np.float32) / np.float32(64)))
    angle = np.arange(T, dtype=np.float32)[:, None] * inv.astype(np.float32)[None, :]
    parts["cos"] = np.tile(np.cos(angle).T, (4, 1))
    parts["sin"] = np.tile(np.sin(angle).T, (4, 1))
    turn = np.zeros((P, P))
    for m in range(P):
        turn[m + 32 if m % 64 < 32 else m - 32, m] = -1.0 if m % 64 < 32 else 1.0
    parts["turn"] = turn
    t = np.arange(T)
    for g in range(2):
        w = np.where(np.arange(P) < 64, 2 ** (2 * g + 1), 2 ** (2 * g + 2))[:, None]
        parts[f"count{g}"] = 1.0 / np.minimum(t[None, :] + 1, w)
    parts["later"] = (j > i) * -1e30
    at, where = 0, {}
    for name, a in parts.items():
        where[name] = (at, a.shape[1])
        at += a.shape[1]
    return np.concatenate([a.astype(np.float32) for a in parts.values()], 1), where


CONST, CONST_AT = constants()


class Core:

    def __init__(self, nc, ctx, const):
        self.nc, self.ctx, self.const_dram = nc, ctx, const
        self.x = self.sb("x", [P, KD, T])
        self.area_at, self.views = nc.sbuf_base, {}
        self.area = self.sb("area", [P, 10, KD * T])
        self.const_sb = self.sb("const", [P, CONST_KEPT])
        self.cols = self.sb("cols", [P, 470])
        self.mod = self.sb("mod", [P, 2, 48])
        self.stats = self.sb("stats", [P, 2, T])
        self.cond = self.sb("cond", [P, KD])
        self.ps = ctx.enter_context(nc.psum_tensor("ps", [P, 8, 512], F32))
        self.col_at = {}
        self.n_cols = 0
        self.x_loaded, self.const_loaded, *self.ada_loaded = (
            nc.alloc_semaphore(n) for n in ("x_loaded", "const_loaded", "ada_loaded0", "ada_loaded1"))
        self.used = []
        self.older = []
        self.count = 0

    def sb(self, name, shape, dt=F32):
        return self.ctx.enter_context(self.nc.sbuf_tensor(name, shape, dt))

    def slot(self, n, *dims):
        size = 1
        for d in dims:
            size *= d
        flat = self.area[:].rearrange("p s n -> p (s n)")[:, int(n * KD * T):int(n * KD * T) + size]
        if len(dims) == 1:
            return flat
        names = "abcd"[:len(dims)]
        return flat.rearrange(f"p ({' '.join(names)}) -> p {' '.join(names)}",
                              **{k: v for k, v in zip(names, dims)})

    def rounded(self, n, *dims):
        at = int(n * KD * T)
        if (at, dims) not in self.views:
            self.views[at, dims] = self.nc.alloc_sbuf_tensor_at(
                f"rounded_{at}_" + "_".join(map(str, dims)), [P, *dims], F32R, offset=self.area_at + 4 * at)
        return self.views[at, dims]

    def rounded_tiles(self, n, tiles=KD):
        return [self.rounded(n + k // KD, min(KD, tiles - k // KD * KD), T)[:, k % KD] for k in range(tiles)]

    def const(self, name, rows=P):
        at, n = CONST_AT[name]
        return self.const_sb[0:rows, at:at + n]

    def col(self, name, k=0, n=1):
        at = self.col_at[name] + k
        return self.cols[:, at:at + n]

    def semaphores(self, *names):
        self.count += 1
        for s in self.older:
            self.nc.release_semaphore(s)
        self.older, self.used = self.used, [self.nc.alloc_semaphore(f"{n}_{self.count}") for n in names]
        return self.used

    def clear_before(self, sp):
        for s in self.older:
            sp.sem_clear(s)

    def clear_all(self):
        self.semaphores()
        with self.nc.Block() as block:
            @block.sync
            def _(sp):
                self.clear_before(sp)


CONST_KEPT = CONST_AT["cos"][0]


def turn_rows(core, groups, before=None, after=None):
    nc = core.nc
    rows = core.slot(8, len(groups), P)
    loaded, turned, copied = core.semaphores("rows_loaded", "rows_turned", "columns_copied")
    plan = []
    for g, group in enumerate(groups):
        at = 0
        first = core.n_cols
        for name, view in group:
            n = view.shape[0]
            core.col_at[name] = first + at
            plan.append((g, at, n, view))
            at += n
        core.n_cols += at
        groups[g] = (first, at)
    with nc.Block() as block:
        @block.sync
        def _(sp):
            core.clear_before(sp)
            if before is not None:
                before(sp, loaded)
            for g, at, n, view in plan:
                sp.dma_start(rows[at:at + n, g, :], view).then_inc(loaded, 16)
            if after is not None:
                after(sp)

        @block.tensor
        def _(pe):
            pe.wait_ge(loaded, 16 * (len(plan) + (before is not None)))
            for g, (first, n) in enumerate(groups):
                if g >= 2:
                    pe.wait_ge(copied, g - 1)
                nc.tensor.transpose(core.ps[:, g % 2, 0:n], rows[0:n, g, :],
                                    core.const("ident", n)[:, 0:n]).then_inc(turned, 1)

        @block.vector
        def _(dve):
            for g, (first, n) in enumerate(groups):
                dve.wait_ge(turned, g + 1)
                nc.vector.tensor_copy(core.cols[:, first:first + n], core.ps[:, g % 2, 0:n]).then_inc(copied, 1)


def ada_view(ada_w, layer):
    return ada_w[layer].rearrange("(k p) n -> p k n", p=P)


ADA_WIDTH = 512


def early_loads(core, A):
    def after(sp):
        sp.dma_start(core.slot(0, 4, D), A["x"].rearrange("o (a p) d -> p (o a) d", p=P)).then_inc(core.x_loaded, 16)
        at = CONST_AT["ones"][0]
        sp.dma_start(core.const_sb[:, at:], core.const_dram[:, at:CONST_KEPT]).then_inc(core.const_loaded, 16)
        for s in range(2):
            sp.dma_start(core.slot(1 + s, KD, ADA_WIDTH), ada_view(A["ada_w"], 0)[:, :, s * ADA_WIDTH:(s + 1) * ADA_WIDTH]
                         ).then_inc(core.ada_loaded[s], 16)
    return after


def turn_x(core):
    nc = core.nc
    rows = core.slot(0, 4, D)
    turned, copied = core.semaphores("x_turned", "x_copied")
    with nc.Block() as block:
        @block.sync
        def _(sp):
            core.clear_before(sp)

        @block.tensor
        def _(pe):
            pe.wait_ge(core.x_loaded, 16)
            for k in range(KD):
                if k >= 2:
                    pe.wait_ge(copied, k - 1)
                for a in range(4):
                    last = nc.tensor.transpose(core.ps[:, k % 2, a * P:(a + 1) * P],
                                               rows[:, a, k * P:(k + 1) * P], core.const("ident"))
                last.then_inc(turned, 1)

        @block.vector
        def _(dve):
            for k in range(KD):
                dve.wait_ge(turned, k + 1)
                nc.vector.tensor_copy(core.x[:, k], core.ps[:, k % 2]).then_inc(copied, 1)


def add_bias(core, dve, layer, first, tiles):
    nc = core.nc
    mod = core.mod[:, layer]
    nc.vector.tensor_tensor(mod[:, first:first + tiles], core.ps[:, 7, first:first + tiles],
                            core.col(f"ada_b{layer}", first, tiles), ALU.add)
    dve.drain()
    for part in (1, 2, 4, 5):
        if first <= part * KD < first + tiles:
            nc.vector.tensor_scalar(mod[:, part * KD:(part + 1) * KD], mod[:, part * KD:(part + 1) * KD],
                                    1.0, None, ALU.add)


def weigh_rows(core, dve, acc, rows):
    nc = core.nc
    last = nc.vector.tensor_scalar(acc, rows[:, 0], core.cond[:, 0:1], None, ALU.mult)
    for k in range(1, KD):
        dve.drain()
        last = nc.vector.scalar_tensor_tensor(acc, rows[:, k], core.cond[:, k:k + 1], acc, ALU.mult, ALU.add)
    return last


def modulation(core, layer, ada_w, blocks):
    nc = core.nc
    W = ADA_WIDTH
    U = 2
    ring = core.slot(1, U, KD, W)
    acc = core.slot(4, U, W)
    loaded = core.ada_loaded
    weighed, summed, cond_ready, sums_done = core.semaphores("weighed", "summed", "cond_ready", "sums_done")
    view = ada_view(ada_w, layer)
    with nc.Block() as block:
        @block.sync
        def _(sp):
            core.clear_before(sp)
            with sp.Fori(1, blocks // U) as i:
                for s in range(U):
                    sp.wait_ge(weighed, (i - 1) * U + s + 1)
                    sp.dma_start(ring[:, s], view[:, :, ds(i * (U * W) + s * W, W)]).then_inc(loaded[s], 16)

        @block.scalar
        def _(act):
            nc.scalar.activation(core.cond[:], core.col("c", 0, KD), ACT.Silu).then_inc(cond_ready, 1)

        @block.vector
        def _(dve):
            dve.wait_ge(cond_ready, 1)
            with dve.Fori(0, blocks // U) as i:
                for s in range(U):
                    dve.wait_ge(loaded[s], i * 16 + 16)
                    dve.wait_ge(summed, i * U + s + 1)
                    weigh_rows(core, dve, acc[:, s], ring[:, s]).then_inc(weighed, 1)
            dve.wait_ge(sums_done, 1)
            add_bias(core, dve, layer, 0, blocks * W // P)

        @block.tensor
        def _(pe):
            pe.sem_inc(summed, U)
            pe.wait_ge(core.const_loaded, 16)
            with pe.Fori(0, blocks // U) as i:
                for s in range(U):
                    pe.wait_ge(weighed, i * U + s + 1)
                    for m in range(W // P):
                        last = nc.tensor.matmul(core.ps[:, 7, ds(i * (U * W // P) + s * (W // P) + m, 1)],
                                                acc[:, s, m * P:(m + 1) * P], core.const("ones")[:, 0:1],
                                                start=True, stop=True)
                    last.then_inc(summed, 1)
            pe.drain().then_inc(sums_done, 1)


class Ride:

    def __init__(self, core, layer, ada_w, first, width, rounds, ring_at, acc_at):
        self.layer, self.first, self.width, self.rounds = layer, first, width, rounds
        self.view = ada_view(ada_w, layer)
        self.ring, self.acc = core.slot(ring_at, 2, KD, width), core.slot(acc_at, 2, width)


def layer_norm(core, gain, bias, summed=True):
    nc = core.nc
    z = core.x
    mean, rstd = core.stats[:, 0], core.stats[:, 1]
    square = core.slot(9, 2, T)
    (mean_summed, centred, squared, square_used, var_summed, root_ready, normed) = core.semaphores(
        "mean_summed", "centred", "squared", "square_used", "var_summed", "root_ready", "normed")
    with nc.Block() as block:
        @block.sync
        def _(sp):
            core.clear_before(sp)

        @block.tensor
        def _(pe):
            if summed:
                nc.tensor.matmul(core.ps[:, 0], core.const("ones"), core.stats[:, 0], start=True,
                                 stop=True).then_inc(mean_summed, 1)
            else:
                for k in range(KD):
                    last = nc.tensor.matmul(core.ps[:, 0], core.const("ones"), z[:, k], start=k == 0, stop=k == KD - 1)
                last.then_inc(mean_summed, 1)
            for k in range(KD):
                pe.wait_ge(squared, k + 1)
                nc.tensor.matmul(core.ps[:, 1], core.const("ones"), square[:, k % 2], start=k == 0,
                                 stop=k == KD - 1).then_inc(square_used, 1)

        @block.scalar
        def _(act):
            squares(core, act, square, centred, square_used, squared)
            act.wait_ge(var_summed, 1)
            nc.scalar.activation(rstd, rstd, ACT.Sqrt).then_inc(root_ready, 1)
            for k in range(KD):
                act.wait_ge(normed, k + 1)
                nc.scalar.activation(core.x[:, k], z[:, k], ACT.Identity, bias=core.col(bias, k), scale=core.col(gain, k))

        @block.vector
        def _(dve):
            dve.wait_ge(mean_summed, 1)
            nc.vector.tensor_scalar(mean, core.ps[:, 0], 1.0 / D, None, ALU.mult)
            dve.drain()
            for k in range(KD):
                nc.vector.tensor_tensor(z[:, k], z[:, k], mean, ALU.subtract).then_inc(centred, 1)
            dve.wait_ge(square_used, KD)
            nc.vector.tensor_scalar(rstd, core.ps[:, 1], 1.0 / D, LN_EPS, ALU.mult, ALU.add).then_inc(var_summed, 1)
            dve.wait_ge(root_ready, 1)
            nc.vector.reciprocal(mean, rstd)
            dve.drain()
            for k in range(KD):
                nc.vector.tensor_tensor(z[:, k], z[:, k], mean, ALU.mult).then_inc(normed, 1)


def squares(core, act, square, centred, square_used, squared, between=None):
    for k in range(KD):
        act.wait_ge(centred, k + 1)
        if k >= 2:
            act.wait_ge(square_used, k - 1)
        core.nc.scalar.activation(square[:, k % 2], core.x[:, k], ACT.Square).then_inc(squared, 1)
        if between is not None:
            between(k)


def modulate(core, layer, half, u, shifted=None):
    nc = core.nc
    sh, sc = (0, 1) if half == 0 else (3, 4)
    done, = core.semaphores("modulated")
    with nc.Block() as block:
        @block.sync
        def _(sp):
            core.clear_before(sp)

        @block.vector
        def _(dve):
            for k in range(KD):
                nc.vector.tensor_scalar(u[:, k], core.x[:, k], core.mod[:, layer, sc * KD + k:sc * KD + k + 1],
                                        core.mod[:, layer, sh * KD + k:sh * KD + k + 1], ALU.mult, ALU.add)
            if shifted is not None:
                dve.drain()
                for k in range(KD):
                    nc.vector.tensor_tensor(shifted[:, k, 1:T], u[:, k, 0:T - 1], u[:, k, 1:T], ALU.subtract)
                nc.vector.tensor_scalar(shifted[:, :, 0:1], u[:, :, 0:1], -1.0, None, ALU.mult)


def linear(core, weight, tiles, kt, rhs, ring, vector=None, scalar=None, U=2, parts=1, width=P):
    nc = core.nc
    names = [f"weights_in_slot{s}" for s in range(U)]
    sems = core.semaphores(*names, "products_done", "banks_freed")
    loaded, done, freed = sems[:U], sems[U], sems[U + 1]
    assert tiles % U == 0
    n = tiles // U

    def drain(eng, each):
        with eng.Fori(0, n) as i:
            for s in range(U):
                eng.wait_ge(done, i * U + (U + s + 1))
                each(eng, i * U + s, [core.ps[:, s * parts + q] for q in range(parts)], s).then_inc(freed, 1)

    with nc.Block() as block:
        @block.sync
        def _(sp):
            core.clear_before(sp)
            with sp.Fori(0, n) as i:
                for s in range(U):
                    sp.wait_ge(done, i * U + (s + 1))
                    for q in range(parts):
                        sp.dma_start(ring[:, s * parts + q], weight(i * U + s, q)).then_inc(loaded[s], 16)

        @block.tensor
        def _(pe):
            pe.sem_inc(done, U)
            pe.sem_inc(freed, U)
            with pe.Fori(0, n) as i:
                for s in range(U):
                    pe.wait_ge(loaded[s], i * (16 * parts) + 16 * parts)
                    pe.wait_ge(freed, i * U + (s + 1))
                    for q in range(parts):
                        for k in range(kt):
                            last = nc.tensor.matmul(core.ps[0:width, s * parts + q], ring[:, s * parts + q, k],
                                                    rhs[:, k], start=k == 0, stop=k == kt - 1)
                    last.then_inc(done, 1)

        if vector is not None:
            @block.vector
            def _(dve):
                drain(dve, vector)
        if scalar is not None:
            @block.scalar
            def _(act):
                drain(act, scalar)


def columns(w, j, n=P):
    return w[:, ds(j * P, n)].rearrange("(k p) m -> p k m", p=P)


def products(core, tiles, kt, weight, rhs, ring_at, vector=None, scalar=None, make=None, parts=1, accumulate=False,
             U=4, extra=(), feed=None, split=True, twice=(), norm=None, square_at=None, sums=None, ride=None):
    nc = core.nc
    raw, high, low = rhs
    kr = kt * parts if accumulate else kt
    per = U // parts
    n = tiles // per
    assert n * per == tiles
    ahead_high, ahead_low = (3, 2) if parts == 1 else (1, 1)
    w_raw, w_low = core.slot(ring_at, U, kt, P), core.rounded(ring_at, U, kt, P)
    w_high = core.rounded(ring_at + U * kt * P / (KD * T), U, kt, P)
    sems = core.semaphores(*[f"weights_in_slot{s}" for s in range(U)], "weights_high", "weights_split", "products_done",
                           "banks_freed", "rhs_made", "rhs_high", "rhs_split", "mean_summed", "centred", "squared",
                           "square_used", "var_summed", "root_ready", "normed", "scaled", "ride_loaded0", "ride_loaded1",
                           "ride_weighed", "ride_summed", *extra)
    loaded = sems[:U]
    (weights_high, weights_split, done, freed, rhs_made, rhs_high, rhs_split, mean_summed, centred, squared, square_used,
     var_summed, root_ready, normed, scaled, ride_loaded0, ride_loaded1, ride_weighed, ride_summed) = sems[U:U + 19]
    ride_loaded = (ride_loaded0, ride_loaded1)
    more = sems[U + 19:] + [freed]
    if norm is not None:
        mean, rstd = core.stats[:, 0], core.stats[:, 1]
        square = core.slot(square_at, 2, T)

    def banks(t):
        return [core.ps[:, t]] if accumulate else [core.ps[:, t * parts + q] for q in range(parts)]

    def high_part(act, i, s):
        act.wait_ge(loaded[s], i * 16 + (32 if s in twice else 16))
        nc.scalar.copy(w_high[:, s], w_raw[:, s]).then_inc(weights_high, 1)

    def low_part(dve, i, s):
        dve.wait_ge(weights_high, i * U + (s + 1))
        nc.vector.tensor_tensor(w_low[:, s], w_raw[:, s], w_high[:, s].bitcast(F32), ALU.subtract).then_inc(weights_split, 1)

    def rounds(eng, ahead, prepare, take, ride=None):
        def one(i, last, rider):
            for t in range(per):
                for q in range(parts):
                    if t + ahead < per:
                        prepare(eng, i, (t + ahead) * parts + q)
                    elif not last:
                        prepare(eng, i + 1, (t + ahead - per) * parts + q)
                if rider is not None:
                    rider(eng, i, t)
                if take is not None:
                    eng.wait_ge(done, i * U + (U + (t + 1) * parts))
                    end = take(eng, i * per + t, banks(t), t, more)
                    if end is not None:
                        end.then_inc(freed, 1)

        ridden = 0 if ride is None else min(ride_rounds, n - 1)
        if ridden:
            with eng.Fori(0, ridden) as i:
                one(i, False, ride)
        if n - 1 > ridden:
            with eng.Fori(ridden, n - 1) as i:
                one(i, False, None)
        one(n - 1, True, ride if ride is not None and ride_rounds == n else None)

    ride_rounds = 0 if ride is None else ride.rounds

    def weigh_ride(dve, i, t):
        dve.wait_ge(ride_loaded[t % 2], i * (16 * (per // 2)) + 16 * (t // 2 + 1))
        dve.wait_ge(ride_summed, i * per + (t + 1))
        weigh_rows(core, dve, ride.acc[:, t % 2], ride.ring[:, t % 2]).then_inc(ride_weighed, 1)

    with nc.Block() as block:
        @block.sync
        def _(sp):
            core.clear_before(sp)
            if feed is not None:
                feed(sp, w_raw, loaded, done)
                return

            def load_unit(i, s):
                sp.wait_ge(done, i * U + (s + 1))
                sp.dma_start(w_raw[:, s], weight(i * per + s // parts, s % parts)).then_inc(loaded[s], 16)

            def load_ride(i, t):
                sp.wait_ge(ride_weighed, i * per + (t + 1))
                sp.dma_start(ride.ring[:, t % 2],
                             ride.view[:, :, ds(i * (per * ride.width) + (ride.first * P + t * ride.width), ride.width)]
                             ).then_inc(ride_loaded[t % 2], 16)

            late = per // 2 if parts == 1 else 0

            def one(i, first, riding):
                for s in range(U):
                    load_unit(i, s)
                    if riding and s % parts == parts - 1:
                        t = s // parts - late
                        if t >= 0:
                            load_ride(i, t)
                        elif not first:
                            load_ride(i - 1, t + per)

            if ride_rounds:
                one(0, True, True)
                if ride_rounds > 1:
                    with sp.Fori(1, ride_rounds) as i:
                        one(i, False, True)
                for t in range(per - late, per):
                    load_ride(ride_rounds - 1, t)
            if n > ride_rounds:
                with sp.Fori(ride_rounds, n) as i:
                    one(i, False, False)

        @block.tensor
        def _(pe):
            pe.sem_inc(done, U)
            pe.sem_inc(freed, per)
            if ride is not None:
                pe.sem_inc(ride_summed, 2)
            if norm is not None:
                nc.tensor.matmul(core.ps[:, 7], core.const("ones"), core.stats[:, 0], start=True,
                                 stop=True).then_inc(mean_summed, 1)
                for k in range(KD):
                    pe.wait_ge(squared, k + 1)
                    nc.tensor.matmul(core.ps[:, 6], core.const("ones"), square[:, k % 2], start=k == 0,
                                     stop=k == KD - 1).then_inc(square_used, 1)

            def one(i, first, riding):
                for s in range(U):
                    t, q = s // parts, s % parts
                    pe.wait_ge(weights_split, i * U + (s + 1))
                    if q == 0:
                        pe.wait_ge(freed, i * per + (t + 1))
                    for k in range(kt):
                        r = q * kt + k if accumulate else k
                        if split and first and (s == 0 or accumulate and s < parts):
                            pe.wait_ge(rhs_split, r + 1)
                        bank = banks(t)[0 if accumulate else q]
                        start, stop = r == 0, r == kr - 1
                        nc.tensor.matmul(bank, w_high[:, s, k], high[r], start=start, stop=False)
                        nc.tensor.matmul(bank, w_high[:, s, k], low[r], start=False, stop=False)
                        last = nc.tensor.matmul(bank, w_low[:, s, k], high[r], start=False, stop=stop)
                    last.then_inc(done, 1)
                    if riding and q == parts - 1:
                        pe.wait_ge(ride_weighed, i * per + (t + 3))
                        wide = ride.width // P
                        for m in range(wide):
                            last = nc.tensor.matmul(core.ps[:, 7, ds(i * (per * wide) + (ride.first + t * wide + m), 1)],
                                                    ride.acc[:, t % 2, m * P:(m + 1) * P], core.const("ones")[:, 0:1],
                                                    start=True, stop=True)
                        last.then_inc(ride_summed, 1)

            one(0, True, ride_rounds > 0)
            if ride_rounds > 1:
                with pe.Fori(1, ride_rounds) as i:
                    one(i, False, True)
            if n > max(ride_rounds, 1):
                with pe.Fori(max(ride_rounds, 1), n) as i:
                    one(i, False, False)

        @block.scalar
        def _(act):
            if norm is not None:
                gain, bias = norm

                def between(k):
                    if k >= KD - ahead_high * parts:
                        high_part(act, 0, k - (KD - ahead_high * parts))

                squares(core, act, square, centred, square_used, squared, between)
                act.wait_ge(var_summed, 1)
                nc.scalar.activation(rstd, rstd, ACT.Sqrt).then_inc(root_ready, 1)
                for k in range(KD + 1):
                    if k < KD:
                        act.wait_ge(normed, k + 1)
                        nc.scalar.activation(core.x[:, k], core.x[:, k], ACT.Identity, bias=core.col(bias, k),
                                             scale=core.col(gain, k)).then_inc(scaled, 1)
                    if k >= 1:
                        if make is not None:
                            act.wait_ge(rhs_made, k)
                        else:
                            act.wait_ge(scaled, k)
                        nc.scalar.copy(high[k - 1], raw[:, k - 1]).then_inc(rhs_high, 1)
            else:
                high_part(act, 0, 0)
                for k in range(kr if split else 0):
                    if make is not None:
                        act.wait_ge(rhs_made, k + 1)
                    nc.scalar.copy(high[k], raw[:, k]).then_inc(rhs_high, 1)
                for q in range(1, ahead_high * parts):
                    high_part(act, 0, q)
            rounds(act, ahead_high, high_part, scalar)

        @block.vector
        def _(dve):
            def low_rhs(k):
                dve.wait_ge(rhs_high, k + 1)
                nc.vector.tensor_tensor(low[k], raw[:, k], high[k].bitcast(F32), ALU.subtract).then_inc(rhs_split, 1)

            if ride is not None:
                dve.sem_inc(ride_weighed, 2)
            if norm is not None:
                dve.wait_ge(mean_summed, 1)
                nc.vector.tensor_scalar(mean, core.ps[:, 7], 1.0 / D, None, ALU.mult)
                dve.drain()
                for k in range(KD):
                    nc.vector.tensor_tensor(core.x[:, k], core.x[:, k], mean, ALU.subtract).then_inc(centred, 1)
                for q in range(ahead_low * parts):
                    low_part(dve, 0, q)
                dve.wait_ge(square_used, KD)
                nc.vector.tensor_scalar(rstd, core.ps[:, 6], 1.0 / D, LN_EPS, ALU.mult, ALU.add).then_inc(var_summed, 1)
                dve.wait_ge(root_ready, 1)
                nc.vector.reciprocal(mean, rstd)
                dve.drain()
                for k in range(KD + 2):
                    if k < KD:
                        nc.vector.tensor_tensor(core.x[:, k], core.x[:, k], mean, ALU.mult).then_inc(normed, 1)
                    if make is not None and 1 <= k < KD + 1:
                        dve.wait_ge(scaled, k)
                        make(dve, k - 1).then_inc(rhs_made, 1)
                    if k >= 2:
                        low_rhs(k - 2)
            else:
                if make is not None:
                    make(dve, 0).then_inc(rhs_made, 1)
                low_part(dve, 0, 0)
                for k in range(kr if split else 0):
                    if make is not None and k + 1 < kr:
                        make(dve, k + 1).then_inc(rhs_made, 1)
                    low_rhs(k)
                for q in range(1, ahead_low * parts):
                    low_part(dve, 0, q)
            if sums is not None:
                nc.vector.memset(sums, 0.0)
                dve.drain()
            rounds(dve, ahead_low, low_part, vector, weigh_ride if ride is not None else None)
            if ride is not None:
                tiles_done = ride_rounds * per
                dve.wait_ge(ride_summed, tiles_done + 2)
                add_bias(core, dve, ride.layer, ride.first, tiles_done * ride.width // P)


def flat(t):
    return t.rearrange("p o t -> p (o t)")


def residual(core, layer, half, w, rhs, ring_at, kt=KD, parts=1):
    nc = core.nc

    def out(dve, j, banks, s, more):
        freed, = more
        x = flat(core.x[:, ds(j, 1)])
        if layer is None:
            nc.vector.scalar_tensor_tensor(x, x, ALPHA, banks[0], ALU.mult, ALU.add).then_inc(freed, 1)
        else:
            nc.vector.tensor_scalar(x, x, ALPHA, None, ALU.mult)
            dve.drain()
            nc.vector.scalar_tensor_tensor(x, banks[0], core.mod[:, layer, ds((2 if half == 0 else 5) * KD + j, 1)], x,
                                           ALU.mult, ALU.add).then_inc(freed, 1)
        dve.drain()
        nc.vector.tensor_tensor(core.stats[:, 0], core.stats[:, 0], x, ALU.add)

    products(core, KD, kt,
             lambda j, q: w[q * kt * P:(q + 1) * kt * P, ds(j * P, P)].rearrange("(k p) m -> p k m", p=P),
             rhs, ring_at, vector=out, parts=parts, accumulate=True, sums=core.stats[:, 0])


def modulated(core, layer, half, u):
    sh, sc = (0, 1) if half == 0 else (3, 4)

    def make(dve, k):
        return core.nc.vector.tensor_scalar(u[:, k], core.x[:, k], core.mod[:, layer, sc * KD + k:sc * KD + k + 1],
                                            core.mod[:, layer, sh * KD + k:sh * KD + k + 1], ALU.mult, ALU.add)
    return make


def feed_forward(core, layer, norm, w_in, w_out, gate_first=True, conv=None, ride=None):
    nc = core.nc
    gq = 0 if gate_first else 1
    gate = core.stats
    h = core.slot(4.5, KF, T)

    def activate(act, j, banks, s, more):
        gated, convolved, freed = more
        if conv is None:
            nc.scalar.activation(gate[:, s], banks[gq], ACT.Silu).then_inc(gated, 1)
        else:
            act.wait_ge(convolved, j + 1)
            nc.scalar.activation(gate[:, s], gate[:, s], ACT.Silu,
                                 bias=core.cols[:, ds(j + conv[1], 1)]).then_inc(gated, 1)

    def weigh(dve, j, banks, s, more):
        gated, convolved, freed = more
        if conv is not None:
            causal_conv(nc, dve, gate[:, s], banks[gq], lambda i: core.cols[:, ds(j + (conv[0] + i * KF), 1)],
                        conv[2]).then_inc(convolved, 1)
        dve.wait_ge(gated, j + 1)
        return nc.vector.tensor_tensor(flat(h[:, ds(j, 1)]), gate[:, s], banks[1 - gq], ALU.mult)

    u, make = core.x, None
    if layer is not None:
        u = core.slot(1, KD, T)
        make = modulated(core, layer, 1, u)
    products(core, KF, KD, lambda j, q: w_in[:, ds(j * P + q * FF, P)].rearrange("(k p) m -> p k m", p=P),
             (u, core.rounded_tiles(0), core.rounded_tiles(1)), 7.25, vector=weigh, scalar=activate, make=make, parts=2,
             extra=("gated", "convolved"), norm=norm, square_at=9.25, ride=ride)
    residual(core, layer, 1, w_out, (h, core.rounded_tiles(0, KF), core.rounded_tiles(4.5, KF)), 7.25, kt=KF // 2, parts=2)


HR = 16
DECAY = float(np.exp(-0.5))


def rwkv_projections(core, A):
    nc = core.nc
    u, xx = core.slot(0, KD, T), core.slot(1, KD, T)
    mix = core.slot(2, 2, KD, T)
    rkv = core.slot(5, 3 * KD, T)
    lora = core.slot(4, 4096)
    down = {3: lora[:, 0:512].rearrange("p (k m) -> p k m", k=KD), 4: lora[:, 512:1024].rearrange("p (k m) -> p k m", k=KD),
            5: lora[:, 1024:2048].rearrange("p (k m) -> p k m", k=KD)}
    up = core.lora_up = {3: lora[0:64, 2048:3072], 4: lora[0:64, 3072:4096]}
    inner = core.lora_inner
    modulate(core, 0, 0, u, xx)

    def lerp(dve, i, k):
        return nc.vector.scalar_tensor_tensor(mix[:, i % 2 if i > 2 else 0, k], xx[:, k], core.col("mu", i * KD + k), u[:, k],
                                              ALU.mult, ALU.add)

    loaded, mixed, summed = core.semaphores("lora_loaded", "mixed", "inner_summed")
    rank = {3: 64, 4: 64, 5: 128}
    with nc.Block() as block:
        @block.sync
        def _(sp):
            core.clear_before(sp)
            for i, name in ((3, "rwkv_w1"), (4, "rwkv_a1"), (5, "rwkv_g1")):
                sp.dma_start(down[i], A[name].rearrange("o (k p) m -> p (o k) m", p=P)).then_inc(loaded, 16)
            for i, name in ((3, "rwkv_w2"), (4, "rwkv_a2")):
                sp.dma_start(up[i], A[name].rearrange("o r n -> (o r) n")).then_inc(loaded, 16)

        @block.vector
        def _(dve):
            for i in (3, 4, 5):
                if i == 5:
                    dve.wait_ge(summed, 1)
                for k in range(KD):
                    lerp(dve, i, k).then_inc(mixed, 1)

        @block.tensor
        def _(pe):
            pe.wait_ge(loaded, 80)
            for i in (3, 4, 5):
                for k in range(KD):
                    pe.wait_ge(mixed, (i - 3) * KD + k + 1)
                    last = nc.tensor.matmul(core.ps[0:rank[i], i], down[i][:, k], mix[:, i % 2, k],
                                            start=k == 0, stop=k == KD - 1)
                last.then_inc(summed, 1)

        @block.scalar
        def _(act):
            for i, f in ((3, ACT.Tanh), (4, ACT.Identity), (5, ACT.Sigmoid)):
                act.wait_ge(summed, i - 2)
                nc.scalar.activation(inner[0:rank[i], i - 3], core.ps[0:rank[i], i], f)

    for m, name in enumerate("rkv"):
        products(core, KD, KD,
                 lambda j, q: A["rwkv_w_rkv"][0, m, :, ds(j * P, P)].rearrange("(k p) m -> p k m", p=P),
                 (mix[:, 0], core.rounded_tiles(3), core.rounded_tiles(2)), 8,
                 scalar=lambda act, j, banks, s, more: nc.scalar.copy(flat(rkv[:, ds(j + m * KD, 1)]), banks[0]),
                 make=lambda dve, k: lerp(dve, m, k),
                 ride=Ride(core, 0, A["ada_w"], (m + 1) * 2 * KD, 256, 2, 7, 4) if m < 2 else None)


def rwkv_decays(core):
    nc = core.nc
    lw, a, r, k, kk = (core.slot(n, KD, T) for n in (0, 1, 5, 6, 2))
    t3, t4, square, factor = (core.slot(n, KD, T) for n in (3, 4, 8, 9))
    mid, first, ends = core.mid, core.first, core.ends
    rows = core.bonus[:]
    (outer_summed, taken, k_scaled, squared, head_summed, floored, rooted, inverted, spread, kk_done, product, bonus_summed, running, risen,
     fallen, ends_risen) = core.semaphores(
        "outer_summed", "banks_taken", "k_scaled", "squared", "head_summed", "floored", "rooted", "inverted", "spread", "kk_done", "bonus_product",
        "bonus_summed", "running_sums", "risen", "fallen", "ends_risen")

    def by_chunk(t):
        return t.rearrange("p k (c t) -> p (k c) t", c=NC)

    with nc.Block() as block:
        @block.sync
        def _(sp):
            core.clear_before(sp)

        @block.scalar
        def _(act):
            def sigmoids(t, bias, first):
                for i in range(KD):
                    act.wait_ge(outer_summed, first + i + 1)
                    nc.scalar.activation(t[:, i], core.ps[:, (first + i) % 4], ACT.Sigmoid,
                                         bias=core.col(bias, i)).then_inc(taken, 1)

            sigmoids(lw, "w0", 0)
            for i in range(KD):
                act.wait_ge(k_scaled, i + 1)
                nc.scalar.activation(square[:, i], kk[:, i], ACT.Square).then_inc(squared, 1)
            sigmoids(a, "a0", KD)
            act.wait_ge(floored, 1)
            nc.scalar.activation(rows, rows, ACT.Sqrt).then_inc(rooted, 1)
            act.wait_ge(running, 1)
            nc.scalar.activation(t3, lw, ACT.Exp, scale=-DECAY).then_inc(risen, 1)
            nc.scalar.activation(t4, lw, ACT.Exp, scale=DECAY).then_inc(fallen, 1)
            nc.scalar.activation(first[:], mid[:], ACT.Exp, scale=DECAY)
            nc.scalar.activation(ends[:], ends[:], ACT.Exp, scale=-DECAY).then_inc(ends_risen, 1)

        @block.tensor
        def _(pe):
            for which in (3, 4):
                for i in range(KD):
                    n = (which - 3) * KD + i
                    if n >= 4:
                        pe.wait_ge(taken, n - 3)
                    nc.tensor.matmul(core.ps[:, n % 4], core.lora_up[which][:, i * P:(i + 1) * P],
                                     core.lora_inner[0:64, which - 3], start=True, stop=True).then_inc(outer_summed, 1)
                if which == 3:
                    for i in range(KD):
                        pe.wait_ge(squared, i + 1)
                        last = nc.tensor.matmul(core.ps[0:HR, 5], core.const("heads16")[:, i * HR:(i + 1) * HR], square[:, i],
                                                start=i == 0, stop=i == KD - 1)
                    last.then_inc(head_summed, 1)
            pe.wait_ge(taken, 2 * KD)
            pe.wait_ge(inverted, 1)
            for i in range(KD):
                if i >= 4:
                    pe.wait_ge(kk_done, i - 3)
                nc.tensor.matmul(core.ps[:, i % 4], core.const("spread16", HR)[:, i * P:(i + 1) * P], rows, start=True,
                                 stop=True).then_inc(spread, 1)
            for i in range(KD):
                pe.wait_ge(product, i + 1)
                last = nc.tensor.matmul(core.ps[0:HR, 4], core.const("heads16")[:, i * HR:(i + 1) * HR], factor[:, i],
                                        start=i == 0, stop=i == KD - 1)
            last.then_inc(bonus_summed, 1)

        @block.vector
        def _(dve):
            for i in range(KD):
                nc.vector.tensor_scalar(kk[:, i], k[:, i], core.col("k_k", i), None, ALU.mult).then_inc(k_scaled, 1)
            for i in range(KD):
                dve.wait_ge(taken, i + 1)
                nc.vector.tensor_tensor_scan(factor[:, i], core.const("carry"), lw[:, i], 0.0, ALU.mult, ALU.add)
            dve.drain()
            nc.vector.tensor_copy(mid[:].rearrange("p (n o) -> p n o", o=1), by_chunk(factor)[:, :, C // 2 - 1:C // 2])
            dve.drain()
            nc.vector.tensor_tensor(by_chunk(lw), by_chunk(factor), mid[:].unsqueeze(2).to_broadcast([P, KD * NC, C]),
                                    ALU.subtract)
            dve.drain()
            nc.vector.tensor_copy(ends[:].rearrange("p (n o) -> p n o", o=1), by_chunk(lw)[:, :, C - 1:C])
            dve.drain()
            e4, m4 = (t[:].rearrange("p (k c) -> p k c", c=NC) for t in (ends, mid))
            nc.vector.tensor_tensor(e4[:, :, 0:NC - 1], e4[:, :, 0:NC - 1], m4[:, :, 1:NC], ALU.add)
            dve.drain().then_inc(running, 1)
            dve.wait_ge(head_summed, 1)
            nc.vector.tensor_scalar(rows, core.ps[0:HR, 5], 1e-6, None, ALU.add).then_inc(floored, 1)
            for i in range(KD):
                dve.wait_ge(taken, KD + i + 1)
                nc.vector.tensor_scalar(factor[:, i], a[:, i], core.col("k_a", i), core.one_less_k_a[:, i:i + 1],
                                        ALU.mult, ALU.add)
            dve.drain()
            nc.vector.tensor_tensor(k, k, factor, ALU.mult)
            dve.drain()
            for i in range(KD):
                nc.vector.scalar_tensor_tensor(factor[:, i], r[:, i], core.col("r_k", i), k[:, i], ALU.mult,
                                               ALU.mult).then_inc(product, 1)
            dve.wait_ge(rooted, 1)
            nc.vector.reciprocal(rows, rows).then_inc(inverted, 1)
            dve.drain()
            dve.wait_ge(fallen, 1)
            nc.vector.tensor_tensor(k, k, t4, ALU.mult)
            nc.vector.tensor_tensor(r, r, t3, ALU.mult)
            for i in range(KD):
                dve.wait_ge(spread, i + 1)
                nc.vector.tensor_tensor(kk[:, i], kk[:, i], core.ps[:, i % 4], ALU.mult).then_inc(kk_done, 1)
            dve.drain()
            nc.vector.tensor_tensor(a, a, kk, ALU.mult)
            dve.drain()
            nc.vector.tensor_tensor(a, a, t4, ALU.mult)
            nc.vector.tensor_tensor(by_chunk(kk)[:, :, 1:C], by_chunk(kk)[:, :, 1:C], by_chunk(t3)[:, :, 0:C - 1],
                                    ALU.mult)
            dve.wait_ge(ends_risen, 1)
            nc.vector.tensor_tensor(by_chunk(kk)[:, :, 0:1], by_chunk(kk)[:, :, 0:1], first[:].unsqueeze(2), ALU.mult)
            dve.wait_ge(bonus_summed, 1)
            nc.vector.tensor_copy(core.bonus[:], core.ps[0:HR, 4])


def rwkv_chunks(core):
    nc = core.nc
    R, Aa, B, K, V = (core.slot(n, KD, T) for n in (5, 2, 1, 6, 7))
    HT = KD // 2
    H = HR // 2

    def place(slot, at, *dims):
        return core.slot(slot + at / (KD * T), *dims)

    ar = core.slot(0, 2, HT, 2, C)
    b_c, k_c, v_c = (place(0, 2048 + n * 512, HT, C) for n in range(3))
    masks = place(0, 3584, 512)
    turned = core.slot(8, 2, 3, HT * C)
    gram = (core.slot(3, H, 4, C), core.slot(9, H, 4, C))
    XT, X, W = core.slot(4, 2, H, C), place(4, 2048, H, C), place(4, 3072, H, C)
    Z, Uu = place(8, 3072, H, 64), place(8, 3584, H, 64)
    S = core.stats[:].rearrange("p a t -> p (a t)").rearrange("p (k v) -> p k v", k=KD)
    G = 2
    (staged, turned_ps, turned_sb, gram_ps, gram_sb, gram_seen, seed_sb, x_ps, x_sb, w_ps, w_sb, xw_ps, x_new, xt_ps,
     xt_sb, xt_last_ps, xt_last, z_ps, z_sb, u_ps, u_sb, y_ps, s_ps, s_new, y_sb) = core.semaphores(
        "staged", "turned_ps", "turned_sb", "gram_ps", "gram_sb", "gram_seen", "seed_sb", "x_ps", "x_sb", "w_ps", "w_sb",
        "xw_ps", "x_new", "xt_ps", "xt_sb", "xt_last_ps", "xt_last", "z_ps", "z_sb", "u_ps", "u_sb", "y_ps", "s_ps",
        "s_new", "y_sb")
    inverse = (seed_sb, x_ps, x_sb, w_ps, w_sb, xw_ps, x_new, xt_ps, xt_sb, xt_last_ps, xt_last)
    ident = core.const("ident")

    def steps(eng, front, tail):
        front(0, 0, None)
        with eng.Fori(0, NC - 1) as c:
            front(c * 2 + 1, 1, (c * 2, 0, c))
            front(c * 2 + 2, 0, (c * 2 + 1, 1, c))
        front(2 * NC - 1, 1, (2 * NC - 2, 0, NC - 1))
        tail(2 * NC - 1, 1, NC - 1)

    def part(t, half, c):
        return t[:, half * HT:(half + 1) * HT, ds(c * C, C)]

    def head(t, h):
        return t[64 * (h % 2):64 * (h % 2) + 64, h // 2]

    with nc.Block() as block:
        @block.sync
        def _(sp):
            core.clear_before(sp)

        @block.gpsimd
        def _(pool):
            def stage(half, c):
                nc.gpsimd.tensor_copy(b_c, part(B, half, c))
                nc.gpsimd.tensor_copy(k_c, part(K, half, c))
                nc.gpsimd.tensor_copy(v_c, part(V, half, c))
                nc.gpsimd.tensor_copy(ar[:, half, :, 0], part(Aa, half, c))
                nc.gpsimd.tensor_copy(ar[:, half, :, 1], part(R, half, c)).then_inc(staged, 1)

            nc.gpsimd.memset(gram[1], 0.0)
            pool.drain()
            pool.wait_ge(gram_ps, H)
            stage(1, 0)
            with pool.Fori(1, NC) as c:
                for half in range(2):
                    pool.wait_ge(gram_ps, c * (2 * H) + half * H)
                    pool.wait_ge(y_ps, c * 2 + (half - 1))
                    stage(half, c)

        @block.tensor
        def _(pe):
            def z_products(n, s, c):
                pe.wait_ge(s_new, n + 2)
                for p in range(HT):
                    nc.tensor.matmul(core.ps[:, 6, p * P:(p + 1) * P], ar[:, s, p, 0], S[:, s * HT + p], start=True,
                                     stop=False, skip_group_check=True)
                    for h in (2 * p, 2 * p + 1):
                        last = nc.tensor.matmul(core.ps[:, 6, h * 64:(h + 1) * 64], gram[s][:, h, 2],
                                                turned[:, s, 2, h * 64:(h + 1) * 64], start=False, stop=True,
                                                skip_group_check=True)
                last.then_inc(z_ps, 1)

            def u_products(n, s, c):
                pe.wait_ge(xt_last, n * G + G)
                pe.wait_ge(z_sb, n + 1)
                for h in range(H):
                    last = nc.tensor.matmul(core.ps[:, 6, h * 64:(h + 1) * 64], XT[:, s, h], Z[:, h],
                                            start=True, stop=True)
                last.then_inc(u_ps, 1)

            def state_and_output(n, s, c):
                pe.wait_ge(u_sb, n + 1)
                for p in range(HT):
                    pair, out = slice(p * P, (p + 1) * P), core.ps[:, 7, p * P:(p + 1) * P]
                    nc.tensor.matmul(out, turned[:, s, 0, pair], Uu[:, 2 * p:2 * p + 2].rearrange("p h v -> p (h v)"),
                                     start=True, stop=False)
                    last = nc.tensor.matmul(out, turned[:, s, 1, pair], turned[:, s, 2, pair], start=False, stop=True)
                last.then_inc(s_ps, 1)
                for p in range(HT):
                    nc.tensor.matmul(core.ps[:, 6, p * C:(p + 1) * C], S[:, s * HT + p], ar[:, s, p, 1], start=True,
                                     stop=False, skip_group_check=True)
                    for h in (2 * p, 2 * p + 1):
                        lo = 64 * (h % 2)
                        out = core.ps[lo:lo + 64, 6, p * C:(p + 1) * C]
                        nc.tensor.matmul(out, Uu[:, h], gram[s][:, h, 1], start=False, stop=False, skip_group_check=True)
                        last = nc.tensor.matmul(out, turned[:, s, 2, h * 64:(h + 1) * 64], gram[s][:, h, 3], start=False,
                                                stop=True, skip_group_check=True)
                last.then_inc(y_ps, 1)

            def front(n, s, before):
                pe.wait_ge(staged, n + 1)
                for w, src in enumerate((b_c, k_c, v_c)):
                    for p in range(HT):
                        last = nc.tensor.transpose(core.ps[:, w, p * C:(p + 1) * C], src[:, p], ident)
                    last.then_inc(turned_ps, 1)
                if before is not None:
                    pe.wait_ge(xt_last, n * G)
                for h in range(H):
                    if h >= 3:
                        pe.wait_ge(gram_sb, n * H + (h - 2))
                    bank = core.ps[:, 3 + h % 3]
                    both = head(ar[:, s], h).rearrange("p w t -> p (w t)")
                    nc.tensor.matmul(bank[:, 0:2 * C], head(b_c, h), both, start=True, stop=True)
                    nc.tensor.matmul(bank[:, 2 * C:4 * C], head(k_c, h), both, start=True,
                                     stop=True).then_inc(gram_ps, 1)
                if before is not None:
                    z_products(*before)
                pe.wait_ge(turned_sb, n * 3 + 3)
                invert_seeds(core, pe, n, G, ident, XT[:, s], *inverse)
                for lev in range(len(LEVELS)):
                    invert_level(core, pe, n, G, lev, ident, lambda h: gram[s][:, h, 0], X, XT[:, s], W, *inverse)
                    if before is not None and lev == 0:
                        u_products(*before)
                    if before is not None and lev == 1:
                        state_and_output(*before)

            def tail(n, s, c):
                z_products(n, s, c)
                u_products(n, s, c)
                state_and_output(n, s, c)

            steps(pe, front, tail)

        @block.scalar
        def _(act):
            def z_out(n, s, c):
                act.wait_ge(z_ps, n + 1)
                nc.scalar.copy(Z.rearrange("p h v -> p (h v)"), core.ps[:, 6]).then_inc(z_sb, 1)

            def u_out(n, s, c):
                act.wait_ge(u_ps, n + 1)
                nc.scalar.mul(Uu.rearrange("p h v -> p (h v)"), core.ps[:, 6], -1.0).then_inc(u_sb, 1)

            def y_out(n, s, c):
                act.wait_ge(y_ps, n + 1)
                nc.scalar.copy(part(R, s, c), core.ps[:, 6].rearrange("p (k t) -> p k t", k=HT)).then_inc(y_sb, 1)

            def front(n, s, before):
                for w in range(3):
                    act.wait_ge(turned_ps, n * 3 + (w + 1))
                    nc.scalar.copy(turned[:, s, w], core.ps[:, w]).then_inc(turned_sb, 1)
                if before is not None:
                    z_out(*before)
                invert_copies(core, act, n, G, 0, X, XT[:, s], *inverse)
                if before is not None:
                    u_out(*before)
                for lev in range(1, len(LEVELS)):
                    invert_copies(core, act, n, G, lev, X, XT[:, s], *inverse)
                    if before is not None and lev == 1:
                        y_out(*before)

            def tail(n, s, c):
                z_out(n, s, c)
                u_out(n, s, c)
                y_out(n, s, c)

            for to, of in ((b_c, B), (k_c, K), (v_c, V), (ar[:, 0, :, 0], Aa), (ar[:, 0, :, 1], R)):
                last = nc.scalar.copy(to, part(of, 0, 0))
            last.then_inc(staged, 1)
            steps(act, front, tail)

        @block.vector
        def _(dve):
            nc.vector.memset(gram[0], 0.0)
            nc.vector.tensor_copy(masks.rearrange("p (a b) -> p a b", a=2)[:, :, 0:C],
                                  core.const("upper").unsqueeze(1).to_broadcast([P, 2, C]))
            nc.vector.tensor_copy(masks.rearrange("p (a b) -> p a b", a=2)[:, :, C:2 * C],
                                  core.const("upto").unsqueeze(1).to_broadcast([P, 2, C]))
            nc.vector.memset(S, 0.0).then_inc(s_new, 2)
            dve.drain()

            def new_state(n, s, c):
                dve.wait_ge(s_ps, n + 1)
                dve.wait_ge(y_ps, n + 1)
                here = S[:, s * HT:(s + 1) * HT]
                added = core.ps[:, 7].rearrange("p (k v) -> p k v", k=HT)
                for own in (slice(0, 64), slice(64, 128)):
                    nc.vector.tensor_tensor(here[own, :, own], here[own, :, own], added[own, :, own], ALU.add)
                dve.drain()
                dve.wait_ge(y_sb, n + 1)
                ends = core.ends[:].rearrange("p (k c) -> p k c", c=NC)[:, s * HT:(s + 1) * HT, ds(c, 1)]
                nc.vector.tensor_tensor(here, here, ends.to_broadcast([P, HT, P]), ALU.mult).then_inc(s_new, 1)

            def front(n, s, before):
                for h in range(H):
                    dve.wait_ge(gram_ps, n * H + (h + 1))
                    dve.sem_inc(gram_seen, 1)
                    nc.vector.copy_predicated(gram[s][:, h].rearrange("p w t -> p (w t)"), masks.bitcast(U32),
                                              core.ps[:, 3 + h % 3]).then_inc(gram_sb, 1)
                dve.drain()
                invert_start(core, dve, n, G, lambda g: gram[s][:, 4 * g:4 * g + 4, 0], XT[:, s], *inverse)
                for lev in range(len(LEVELS)):
                    if before is not None and lev == 3:
                        new_state(*before)
                    invert_update(core, dve, n, G, lev, X, XT[:, s], W, *inverse)
                dve.drain()

            steps(dve, front, new_state)


def four(t, g):
    return t[:, 4 * g:4 * g + 4]


def bank_of_four(core, b):
    return core.ps[:, b].rearrange("p (h t) -> p h t", h=4)



def invert_seeds(core, pe, n, G, ident, XT, seed_sb, x_ps, *rest):
    for g in range(G):
        pe.wait_ge(seed_sb, n * G + (g + 1))
        for h in range(4):
            last = core.nc.tensor.transpose(core.ps[:, g, h * C:(h + 1) * C], XT[:, 4 * g + h], ident)
        last.then_inc(x_ps, 1)


def invert_level(core, pe, n, G, lev, ident, lower_t, X, XT, W, seed_sb, x_ps, x_sb, w_ps, w_sb, xw_ps, x_new, xt_ps, xt_sb,
                 xt_last_ps, xt_last):
    nc = core.nc
    nl = len(LEVELS)
    for g in range(G):
        if lev == 0:
            pe.wait_ge(x_sb, n * G + (g + 1))
        else:
            pe.wait_ge(x_new, n * (G * (nl - 1)) + ((lev - 1) * G + g + 1))
            for h in range(4):
                last = nc.tensor.transpose(core.ps[:, 4 + g, h * C:(h + 1) * C], X[:, 4 * g + h], ident)
            last.then_inc(xt_ps, 1)
        for h in range(4):
            last = nc.tensor.matmul(core.ps[:, g, h * C:(h + 1) * C], lower_t(4 * g + h), X[:, 4 * g + h],
                                    start=True, stop=True)
        last.then_inc(w_ps, 1)
    for g in range(G):
        pe.wait_ge(w_sb, n * (G * nl) + (lev * G + g + 1))
        if lev:
            pe.wait_ge(xt_sb, n * (G * (nl - 1)) + ((lev - 1) * G + g + 1))
        for h in range(4):
            if lev < nl - 1:
                last = nc.tensor.matmul(core.ps[:, 2 + g, h * C:(h + 1) * C], XT[:, 4 * g + h], W[:, 4 * g + h],
                                        start=True, stop=True)
            else:
                last = nc.tensor.matmul(core.ps[:, 4 + g, h * C:(h + 1) * C], W[:, 4 * g + h], XT[:, 4 * g + h],
                                        start=True, stop=True)
        last.then_inc(xw_ps if lev < nl - 1 else xt_last_ps, 1)


def invert_copies(core, act, n, G, lev, X, XT, seed_sb, x_ps, x_sb, w_ps, w_sb, xw_ps, x_new, xt_ps, xt_sb, *rest):
    nc = core.nc
    for g in range(G):
        if lev == 0:
            act.wait_ge(x_ps, n * G + (g + 1))
            nc.scalar.copy(four(X, g), bank_of_four(core, g)).then_inc(x_sb, 1)
        else:
            act.wait_ge(xt_ps, n * (G * (len(LEVELS) - 1)) + ((lev - 1) * G + g + 1))
            nc.scalar.copy(four(XT, g), bank_of_four(core, 4 + g)).then_inc(xt_sb, 1)


def invert_start(core, dve, n, G, lower_t, XT, seed_sb, *rest):
    nc = core.nc
    for g in range(G):
        nc.vector.tensor_tensor(four(XT, g), lower_t(g), core.const("corner1").unsqueeze(1).to_broadcast([P, 4, C]), ALU.mult)
    dve.drain()
    for g in range(G):
        nc.vector.tensor_tensor(four(XT, g), core.const("ident").unsqueeze(1).to_broadcast([P, 4, C]), four(XT, g),
                                ALU.subtract).then_inc(seed_sb, 1)


def invert_update(core, dve, n, G, lev, X, XT, W, seed_sb, x_ps, x_sb, w_ps, w_sb, xw_ps, x_new, xt_ps, xt_sb, xt_last_ps,
                  xt_last):
    nc = core.nc
    nl = len(LEVELS)
    for g in range(G):
        dve.wait_ge(w_ps, n * (G * nl) + (lev * G + g + 1))
        nc.vector.tensor_tensor(four(W, g), bank_of_four(core, g),
                                core.const(f"corner{LEVELS[lev]}").unsqueeze(1).to_broadcast([P, 4, C]),
                                ALU.mult).then_inc(w_sb, 1)
    for g in range(G):
        if lev == 0:
            dve.wait_ge(x_sb, n * G + (g + 1))
        if lev < nl - 1:
            dve.wait_ge(xw_ps, n * (G * (nl - 1)) + (lev * G + g + 1))
            nc.vector.tensor_tensor(four(X, g), four(X, g), bank_of_four(core, 2 + g), ALU.subtract).then_inc(x_new, 1)
        else:
            dve.wait_ge(xt_sb, n * (G * (nl - 1)) + ((lev - 1) * G + g + 1))
            dve.wait_ge(xt_last_ps, n * G + (g + 1))
            nc.vector.tensor_tensor(four(XT, g), four(XT, g), bank_of_four(core, 4 + g), ALU.subtract).then_inc(xt_last, 1)
    dve.drain()


def rwkv_output(core, A):
    nc = core.nc
    y, v = core.slot(5, KD, T), core.slot(7, KD, T)
    g2 = core.slot(3, D)
    sq = core.slot(4, 2, T)
    rows = core.slot(4, 4, T)[0:HR, 2]
    (loaded, y_summed, centred, squared, var_summed, floored, rooted, inverted, bonus_spread, bonus_done, spread, gate_ps,
     freed) = core.semaphores(
        "gate_loaded", "y_summed", "centred", "squared", "var_summed", "floored", "rooted", "inverted", "bonus_spread",
        "bonus_done", "spread", "gate_ps", "banks_freed")
    by_head = lambda k: core.const("spread16", HR)[:, k * P:(k + 1) * P]
    with nc.Block() as block:
        @block.sync
        def _(sp):
            core.clear_before(sp)
            sp.dma_start(g2, A["rwkv_g2"].rearrange("o r n -> (o r) n")).then_inc(loaded, 16)

        @block.tensor
        def _(pe):
            for k in range(KD + 2):
                if k < KD:
                    if k >= 3:
                        pe.wait_ge(centred, k - 2)
                    nc.tensor.matmul(core.ps[:, k % 3], core.const("head64"), y[:, k], start=True,
                                     stop=True).then_inc(y_summed, 1)
                if k >= 2:
                    pe.wait_ge(squared, k - 1)
                    nc.tensor.matmul(core.ps[0:HR, 3], core.const("heads16")[:, (k - 2) * HR:(k - 1) * HR], sq[:, k % 2],
                                     start=k == 2, stop=k == KD + 1).then_inc(var_summed, 1)
            for k in range(KD):
                if k >= 2:
                    pe.wait_ge(bonus_done, k - 1)
                nc.tensor.matmul(core.ps[:, 4 + k % 2], by_head(k), core.bonus[:], start=True, stop=True).then_inc(bonus_spread, 1)
            pe.wait_ge(loaded, 16)
            for k in range(KD):
                if k >= 2:
                    pe.wait_ge(freed, k - 1)
                nc.tensor.matmul(core.ps[:, k % 2], g2[:, k * P:(k + 1) * P], core.lora_inner[:, 2],
                                 start=True, stop=True).then_inc(gate_ps, 1)
                if k == 0:
                    pe.wait_ge(inverted, 1)
                nc.tensor.matmul(core.ps[:, 6 + k % 2], by_head(k), rows, start=True, stop=True).then_inc(spread, 1)

        @block.scalar
        def _(act):
            for k in range(KD):
                act.wait_ge(centred, k + 1)
                if k >= 2:
                    act.wait_ge(var_summed, k - 1)
                nc.scalar.activation(sq[:, k % 2], y[:, k], ACT.Square).then_inc(squared, 1)
            act.wait_ge(floored, 1)
            nc.scalar.activation(rows, rows, ACT.Sqrt).then_inc(rooted, 1)

        @block.vector
        def _(dve):
            for k in range(KD):
                dve.wait_ge(y_summed, k + 1)
                nc.vector.scalar_tensor_tensor(y[:, k], core.ps[:, k % 3], -1.0 / 64, y[:, k], ALU.mult,
                                               ALU.add).then_inc(centred, 1)

            def bonus(k):
                dve.wait_ge(bonus_spread, k + 1)
                nc.vector.tensor_tensor(v[:, k], v[:, k], core.ps[:, 4 + k % 2], ALU.mult).then_inc(bonus_done, 1)

            bonus(0)
            dve.wait_ge(var_summed, KD)
            nc.vector.tensor_scalar(rows, core.ps[0:HR, 3], 1.0 / 64, 64e-5, ALU.mult, ALU.add).then_inc(floored, 1)
            for k in range(1, 4):
                bonus(k)
            dve.wait_ge(rooted, 1)
            nc.vector.reciprocal(rows, rows).then_inc(inverted, 1)
            for k in range(4, KD):
                bonus(k)
            for k in range(KD):
                dve.wait_ge(spread, k + 1)
                nc.vector.scalar_tensor_tensor(y[:, k], y[:, k], core.col("gn_g", k), core.ps[:, 6 + k % 2], ALU.mult, ALU.mult)
                dve.drain()
                nc.vector.scalar_tensor_tensor(y[:, k], y[:, k], core.col("gn_b", k), v[:, k], ALU.add, ALU.add)
                dve.drain()
                dve.wait_ge(gate_ps, k + 1)
                nc.vector.tensor_tensor(y[:, k], y[:, k], core.ps[:, k % 2], ALU.mult).then_inc(freed, 1)
    residual(core, 0, 0, A["rwkv_w_out"].rearrange("o k n -> (o k) n"),
             (y, core.rounded_tiles(0), core.rounded_tiles(5)), 8)



HG = 8
TAPS = 4


def causal_conv(nc, dve, tmp, ps, tap, taps):
    nc.vector.tensor_scalar(tmp, ps, tap(taps - 1), None, ALU.mult)
    for back in range(1, taps):
        dve.drain()
        last = nc.vector.scalar_tensor_tensor(tmp[:, back:T], ps[:, 0:T - back], tap(taps - 1 - back), tmp[:, back:T],
                                              ALU.mult, ALU.add)
    return last


def gdn_projections(core, A):
    nc = core.nc
    u = core.slot(0, KD, T)
    qkv, z = core.slot(1, 3 * KD, T), core.slot(4, KD, T)
    tmp = core.slot(5, 2, T)
    w = A["gdn_w_in"].rearrange("o k n -> (o k) n")
    conv = core.col_at["conv"]
    high, low = core.rounded_tiles(6), core.rounded_tiles(7)

    def convolve(dve, j, banks, s, more):
        convolved, freed = more
        dve.wait_ge(freed, j + 3)
        causal_conv(nc, dve, tmp[:, s % 2], banks[0], lambda i: core.cols[:, ds(j + (conv + i * 3 * KD), 1)],
                    TAPS).then_inc(convolved, 1)

    def activate(act, j, banks, s, more):
        convolved, freed = more
        act.wait_ge(convolved, j + 1)
        return nc.scalar.activation(flat(qkv[:, ds(j, 1)]), tmp[:, s % 2], ACT.Silu)

    products(core, 3 * KD, KD, lambda j, q: columns(w, j), (u, high, low), 8, vector=convolve, scalar=activate,
             make=modulated(core, 1, 0, u), extra=("convolved",), norm=("ln_g01", "ln_b01"), square_at=4)
    products(core, KD, KD, lambda j, q: w[:, ds(j * P + 3 * D, P)].rearrange("(k p) m -> p k m", p=P), (u, high, low), 8,
             scalar=lambda act, j, banks, s, more: nc.scalar.activation(flat(z[:, ds(j, 1)]), banks[0], ACT.Silu), split=False)



def gdn_gates(core, A):
    nc = core.nc
    u, q, k = (core.slot(n, KD, T) for n in (0, 1, 2))
    w = A["gdn_w_in"].rearrange("o k n -> (o k) n")
    wg = core.slot(5, KD, 2 * HG)
    small = core.slot(6, 2, 4)
    alog, dt = small[0:HG, 0, 0:1], small[0:HG, 1, 0:1]
    tmp = core.slot(7, 4, T)
    x, soft, pos, g = (tmp[0:HG, i] for i in range(4))
    beta_k, gc, rise, fall = (core.gate_rows[:, i] for i in range(4))
    q_norm, k_norm = core.norm_rows[:, 0], core.norm_rows[:, 1]
    sq = core.slot(9, 2, T)
    (loaded, summed, shifted, softened, powered, cum, turned, squared, square_used, floored, rooted, beta_ready,
     inverted) = core.semaphores(
        "gates_loaded", "gates_summed", "shifted", "softened", "powered", "cumulated", "turned", "squared", "square_used",
        "floored", "rooted", "beta_ready", "inverted")
    with nc.Block() as block:
        @block.sync
        def _(sp):
            core.clear_before(sp)
            sp.dma_start(wg, w[:, 4 * D:4 * D + 2 * HG].rearrange("(k p) m -> p k m", p=P)).then_inc(loaded, 16)
            sp.dma_start(alog, A["gdn_a_log"].rearrange("o h -> h o")).then_inc(loaded, 16)
            sp.dma_start(dt, A["gdn_dt_bias"].rearrange("o h -> h o")).then_inc(loaded, 16)

        @block.tensor
        def _(pe):
            def norms(i):
                for h in range(HG):
                    pe.wait_ge(squared, i * HG + h + 1)
                    nc.tensor.matmul(core.ps[0:HG, 3 + i], core.const("pick8")[:, HG - 1 - h:2 * HG - 1 - h],
                                     sq[:, h % 2], start=h == 0, stop=h == HG - 1).then_inc(square_used, 1)

            norms(0)
            pe.wait_ge(loaded, 48)
            for i in (1, 0):
                for at in range(KD):
                    last = nc.tensor.matmul(core.ps[0:HG, i], wg[:, at, i * HG:(i + 1) * HG], u[:, at],
                                            start=at == 0, stop=at == KD - 1)
                last.then_inc(summed, 1)
            norms(1)
            pe.wait_ge(cum, 1)
            pe.wait_ge(inverted, 1)
            for i, rows in enumerate((gc, k_norm)):
                for c in range(NC):
                    last = nc.tensor.transpose(core.ps[:, 5 + i, c * HG:(c + 1) * HG], rows[:, c * C:(c + 1) * C],
                                               core.const("ident", HG)[:, 0:HG])
            last.then_inc(turned, 1)

        @block.scalar
        def _(act):
            for i, t in enumerate((k, q)):
                for h in range(HG):
                    at = i * HG + h
                    if at >= 2:
                        act.wait_ge(square_used, at - 1)
                    nc.scalar.activation(sq[:, at % 2], t[:, h], ACT.Square).then_inc(squared, 1)
                if i == 0:
                    act.wait_ge(loaded, 48)
                    nc.scalar.activation(alog, alog, ACT.Exp)
                    act.wait_ge(shifted, 1)
                    nc.scalar.activation(soft, x, ACT.Abs)
                    act.drain()
                    nc.scalar.activation(soft, soft, ACT.Exp, scale=-1.0)
                    act.drain()
                    nc.scalar.activation(soft, soft, ACT.Ln, bias=1.0).then_inc(softened, 1)
            act.wait_ge(cum, 2)
            nc.scalar.activation(rise, gc, ACT.Exp)
            nc.scalar.activation(fall, fall, ACT.Exp).then_inc(powered, 1)
            act.wait_ge(summed, 2)
            nc.scalar.activation(core.norm_rows[:, 2], core.ps[0:HG, 0], ACT.Sigmoid).then_inc(beta_ready, 1)
            for i, rows in enumerate((k_norm, q_norm)):
                act.wait_ge(floored, i + 1)
                nc.scalar.activation(rows, rows, ACT.Sqrt).then_inc(rooted, 1)

        @block.vector
        def _(dve):
            dve.wait_ge(summed, 1)
            dve.wait_ge(loaded, 48)
            nc.vector.tensor_scalar(x, core.ps[0:HG, 1], dt, None, ALU.add).then_inc(shifted, 1)
            dve.drain()
            nc.vector.tensor_scalar(pos, x, 0.0, None, ALU.max)
            dve.wait_ge(square_used, HG)
            nc.vector.tensor_scalar(k_norm, core.ps[0:HG, 3], 1e-6, None, ALU.add).then_inc(floored, 1)
            dve.wait_ge(softened, 1)
            dve.drain()
            nc.vector.tensor_tensor(g, pos, soft, ALU.add)
            dve.drain()
            nc.vector.tensor_scalar(g, g, alog, -1.0, ALU.mult, ALU.mult)
            dve.drain()
            nc.vector.tensor_tensor_scan(gc, core.const("carry", HG), g, 0.0, ALU.mult, ALU.add).then_inc(cum, 1)
            dve.drain()
            g3, f3 = (t.rearrange("p (c t) -> p c t", c=NC) for t in (gc, fall))
            nc.vector.tensor_tensor(f3, g3[:, :, C - 1:C].to_broadcast([HG, NC, C]), g3, ALU.subtract).then_inc(cum, 1)
            dve.wait_ge(square_used, 2 * HG)
            nc.vector.tensor_scalar(q_norm, core.ps[0:HG, 4], 1e-6, float(P), ALU.add, ALU.mult).then_inc(floored, 1)
            dve.wait_ge(rooted, 1)
            nc.vector.reciprocal(k_norm, k_norm).then_inc(inverted, 1)
            dve.wait_ge(rooted, 2)
            nc.vector.reciprocal(q_norm, q_norm)
            dve.drain()
            dve.wait_ge(beta_ready, 1)
            nc.vector.tensor_tensor(beta_k, core.norm_rows[:, 2], k_norm, ALU.mult)
            dve.wait_ge(powered, 1)
            nc.vector.tensor_tensor(fall, fall, k_norm, ALU.mult)
            dve.wait_ge(turned, 1)
            nc.vector.tensor_copy(core.gate_cols[:], core.ps[:, 5, 0:NC * HG])
            nc.vector.tensor_copy(core.norm_cols[:], core.ps[:, 6, 0:NC * HG])


def gdn_output(core):
    nc = core.nc
    o, z = core.slot(0, KD, T), core.slot(4, KD, T)
    q_norm, rows, q_square = (core.norm_rows[:, i] for i in range(3))
    sq = core.slot(9, 2, T)
    squared, summed, floored, rooted, inverted, spread, used = core.semaphores(
        "squared", "summed", "floored", "rooted", "inverted", "spread", "used")
    with nc.Block() as block:
        @block.sync
        def _(sp):
            core.clear_before(sp)

        @block.scalar
        def _(act):
            for h in range(HG):
                if h >= 2:
                    act.wait_ge(summed, h - 1)
                nc.scalar.activation(sq[:, h % 2], o[:, h], ACT.Square).then_inc(squared, 1)
            act.wait_ge(floored, 1)
            nc.scalar.activation(rows, rows, ACT.Sqrt).then_inc(rooted, 1)

        @block.tensor
        def _(pe):
            for h in range(HG):
                pe.wait_ge(squared, h + 1)
                nc.tensor.matmul(core.ps[0:HG, 4], core.const("pick8")[:, HG - 1 - h:2 * HG - 1 - h], sq[:, h % 2],
                                 start=h == 0, stop=h == HG - 1).then_inc(summed, 1)
            pe.wait_ge(inverted, 1)
            for h in range(HG):
                if h >= 4:
                    pe.wait_ge(used, h - 3)
                nc.tensor.matmul(core.ps[:, h % 4], core.const("spread8", HG)[:, h * P:(h + 1) * P], rows,
                                 start=True, stop=True).then_inc(spread, 1)

        @block.vector
        def _(dve):
            nc.vector.tensor_tensor(q_square, q_norm, q_norm, ALU.mult)
            for h in range(HG):
                nc.vector.scalar_tensor_tensor(z[:, h], z[:, h], core.col("norm_g"), o[:, h], ALU.mult, ALU.mult)
            dve.drain()
            dve.wait_ge(summed, HG)
            nc.vector.scalar_tensor_tensor(rows, core.ps[0:HG, 4], 1.0 / P, q_square, ALU.mult, ALU.mult)
            dve.drain()
            nc.vector.tensor_scalar(rows, rows, 1e-6, None, ALU.add).then_inc(floored, 1)
            dve.wait_ge(rooted, 1)
            nc.vector.reciprocal(rows, rows)
            dve.drain()
            nc.vector.tensor_tensor(rows, rows, q_norm, ALU.mult).then_inc(inverted, 1)
            for h in range(HG):
                dve.wait_ge(spread, h + 1)
                nc.vector.tensor_tensor(o[:, h], z[:, h], core.ps[:, h % 4], ALU.mult).then_inc(used, 1)


def gdn_chunks(core):
    nc = core.nc
    q, k, v, o = (core.slot(n, KD, T) for n in (1, 2, 3, 0))

    def tile8(slot, quarter):
        return core.area[:, slot, quarter * 1024:(quarter + 1) * 1024].rearrange("p (h t) -> p h t", h=HG)

    kq = core.slot(5, HG, 2, C)
    k_c, k_left = tile8(5, 2), tile8(5, 3)
    k_old, v_beta = core.slot(6, 2, HG, C), core.slot(6.5, 2, HG, C)
    left_t, upto = core.slot(7, 2, HG, C), core.slot(7.5, 2, HG, C)
    XT, X, W = core.slot(8, 2, HG, C), tile8(8, 2), tile8(8, 3)
    strict, Z = tile8(9, 0), tile8(9, 1)
    S = core.stats[:].rearrange("p a t -> p (a t)").rearrange("p (h t) -> p h t", h=HG)
    total = core.total[:, 0:2 * HG].rearrange("p (s h) -> p s h", s=2)
    beta_k, gc, rise, fall = (core.gate_rows[:, i] for i in range(4))
    beta = core.norm_rows[:, 2]
    ident = core.const("ident")
    G = 2
    (staged, spread, differ, keys_made, decayed, ready, gram_ps, gram_sb, left_ps, left_sb, seed_sb, x_ps, x_sb, w_ps, w_sb, xw_ps,
     x_new, xt_ps, xt_sb, xt_last_ps, xt_last, z_ps, z_sb, u_ps, u_sb, s_ps, s_new, o_ps, o_sb) = core.semaphores(
        "staged", "spread", "differ", "keys_made", "decayed", "ready", "gram_ps", "gram_sb", "left_ps", "left_sb", "seed_sb", "x_ps",
        "x_sb", "w_ps", "w_sb", "xw_ps", "x_new", "xt_ps", "xt_sb", "xt_last_ps", "xt_last", "z_ps", "z_sb", "u_ps",
        "u_sb", "s_ps", "s_new", "o_ps", "o_sb")
    inverse = (seed_sb, x_ps, x_sb, w_ps, w_sb, xw_ps, x_new, xt_ps, xt_sb, xt_last_ps, xt_last)

    def steps(eng, front, tail):
        front(0, 0, None)
        with eng.Fori(0, NC // 2 - 1) as i:
            front(i * 2 + 1, 1, (i * 2, 0))
            front(i * 2 + 2, 0, (i * 2 + 1, 1))
        front(NC - 1, 1, (NC - 2, 0))
        tail(NC - 1, 1)

    def pair(b):
        return core.ps[:, b:b + 2].rearrange("p b (h t) -> p (b h) t", h=4)

    def chunk(t, c):
        return t[:, :, ds(c * C, C)]

    with nc.Block() as block:
        @block.sync
        def _(sp):
            core.clear_before(sp)

        @block.gpsimd
        def _(pool):
            def stage(c):
                nc.gpsimd.tensor_copy(k_c, chunk(k, c))
                nc.gpsimd.tensor_copy(kq[:, :, 1], chunk(q, c)).then_inc(staged, 1)

            stage(0)
            with pool.Fori(1, NC) as c:
                pool.wait_ge(gram_ps, c * 4)
                stage(c)

        @block.tensor
        def _(pe):
            def out(h):
                return core.ps[:, 6 + h // 4, (h % 4) * C:(h % 4 + 1) * C]

            def z_products(n, s):
                pe.wait_ge(s_new, n + 1)
                for h in range(HG):
                    nc.tensor.matmul(out(h), k_old[:, s, h], S[:, h], start=True, stop=False)
                    last = nc.tensor.matmul(out(h), v_beta[:, s, h], ident, start=False, stop=True)
                last.then_inc(z_ps, 1)

            def u_products(n, s):
                pe.wait_ge(xt_last, n * G + G)
                pe.wait_ge(z_sb, n + 1)
                for h in range(HG):
                    last = nc.tensor.matmul(out(h), XT[:, s, h], Z[:, h], start=True, stop=True)
                last.then_inc(u_ps, 1)

            def o_products(n, s):
                pe.wait_ge(u_sb, n + 1)
                for h in range(HG):
                    nc.tensor.matmul(out(h), S[:, h], q[:, h, ds(n * C, C)], start=True, stop=False)
                    last = nc.tensor.matmul(out(h), Z[:, h], upto[:, s, h], start=False, stop=True)
                last.then_inc(o_ps, 1)

            def state_products(n, s):
                pe.wait_ge(o_sb, n + 1)
                for h in range(HG):
                    last = nc.tensor.matmul(out(h), left_t[:, s, h], Z[:, h], start=True, stop=True)
                last.then_inc(s_ps, 1)

            def front(n, s, before):
                if before is not None:
                    pe.wait_ge(xt_last, n * G)
                for i, rows in enumerate((gc, beta_k, rise, fall, beta)):
                    if i == 3:
                        pe.wait_ge(differ, n + 1)
                    if i == 4:
                        pe.wait_ge(keys_made, n + 1)
                    for h in range(HG):
                        last = nc.tensor.matmul(core.ps[:, 2 * (i % 3) + h // 4, (h % 4) * C:(h % 4 + 1) * C],
                                                core.const("spread8", HG)[:, h * P:(h + 1) * P], rows[:, ds(n * C, C)],
                                                start=True, stop=True)
                    last.then_inc(spread, 1)
                if before is not None:
                    z_products(*before)
                pe.wait_ge(ready, n + 1)
                pe.wait_ge(staged, n + 1)
                for h in range(HG):
                    bank = core.ps[:, h // 2, (h % 2) * 2 * C:(h % 2 + 1) * 2 * C]
                    last = nc.tensor.matmul(bank, k_c[:, h], kq[:, h].rearrange("p w t -> p (w t)"), start=True, stop=True)
                    if h % 2:
                        last.then_inc(gram_ps, 1)
                for h in range(HG):
                    last = nc.tensor.transpose(core.ps[:, 4 + h // 4, (h % 4) * C:(h % 4 + 1) * C], k_left[:, h], ident)
                last.then_inc(left_ps, 1)
                pe.wait_ge(left_sb, n + 1)
                invert_seeds(core, pe, n, G, ident, XT[:, s], *inverse)
                for lev in range(len(LEVELS)):
                    invert_level(core, pe, n, G, lev, ident, lambda h: strict[:, h], X, XT[:, s], W, *inverse)
                    if before is not None and lev == 0:
                        u_products(*before)
                    if before is not None and lev == 1:
                        o_products(*before)
                    if before is not None and lev == 2:
                        state_products(*before)

            def tail(n, s):
                z_products(n, s)
                u_products(n, s)
                o_products(n, s)
                state_products(n, s)

            steps(pe, front, tail)

        @block.scalar
        def _(act):
            def z_out(n, s):
                act.wait_ge(z_ps, n + 1)
                nc.scalar.copy(Z, pair(6)).then_inc(z_sb, 1)

            def u_out(n, s):
                act.wait_ge(u_ps, n + 1)
                nc.scalar.copy(Z, pair(6)).then_inc(u_sb, 1)

            def o_out(n, s):
                act.wait_ge(o_ps, n + 1)
                nc.scalar.copy(chunk(o, n), pair(6)).then_inc(o_sb, 1)

            def front(n, s, before):
                act.wait_ge(differ, n + 1)
                nc.scalar.activation(upto[:, s], upto[:, s], ACT.Exp).then_inc(decayed, 1)
                if before is not None:
                    z_out(*before)
                act.wait_ge(left_ps, n + 1)
                nc.scalar.copy(left_t[:, s], pair(4)).then_inc(left_sb, 1)
                invert_copies(core, act, n, G, 0, X, XT[:, s], *inverse)
                if before is not None:
                    u_out(*before)
                for lev in range(1, len(LEVELS)):
                    invert_copies(core, act, n, G, lev, X, XT[:, s], *inverse)
                    if before is not None and lev == 1:
                        o_out(*before)

            def tail(n, s):
                z_out(n, s)
                u_out(n, s)
                o_out(n, s)

            steps(act, front, tail)

        @block.vector
        def _(dve):
            nc.vector.memset(S, 0.0).then_inc(s_new, 1)
            dve.drain()

            def new_state(n, s):
                dve.wait_ge(s_ps, n + 1)
                nc.vector.tensor_tensor(S, S, total[:, s].unsqueeze(2).to_broadcast([P, HG, C]), ALU.mult)
                dve.drain()
                nc.vector.tensor_tensor(S, S, pair(6), ALU.add).then_inc(s_new, 1)

            def front(n, s, before):
                dve.wait_ge(spread, n * 5 + 1)
                for h in range(HG):
                    last = nc.vector.tensor_scalar(upto[:, s, h], pair(0)[:, h], core.gate_cols[:, ds(n * HG + h, 1)], 0.0,
                                                   ALU.subtract, ALU.min)
                last.then_inc(differ, 1)
                dve.wait_ge(spread, n * 5 + 2)
                nc.vector.tensor_tensor(kq[:, :, 0], chunk(k, n), pair(2), ALU.mult).then_inc(keys_made, 1)
                dve.drain()
                dve.wait_ge(spread, n * 5 + 3)
                nc.vector.scalar_tensor_tensor(k_old[:, s], kq[:, :, 0], -1.0, pair(4), ALU.mult, ALU.mult)
                nc.vector.tensor_copy(total[:, s], pair(4)[:, :, C - 1])
                dve.wait_ge(staged, n + 1)
                nc.vector.tensor_tensor(chunk(q, n), chunk(q, n), pair(4), ALU.mult)
                dve.wait_ge(spread, n * 5 + 4)
                nc.vector.tensor_tensor(k_left, chunk(k, n), pair(0), ALU.mult)
                dve.wait_ge(spread, n * 5 + 5)
                nc.vector.tensor_tensor(v_beta[:, s], chunk(v, n), pair(2), ALU.mult).then_inc(ready, 1)
                dve.wait_ge(decayed, n + 1)
                for mask, to in (("upper", strict), ("upto", upto[:, s])):
                    for h in range(HG):
                        nc.vector.scalar_tensor_tensor(to[:, h], upto[:, s, h], core.norm_cols[:, ds(n * HG + h, 1)],
                                                       core.const(mask), ALU.mult, ALU.mult)
                    dve.drain()
                for b in range(4):
                    dve.wait_ge(gram_ps, n * 4 + (b + 1))
                    grams = core.ps[:, b].rearrange("p (h w t) -> p h w t", h=2, w=2)
                    here = slice(2 * b, 2 * b + 2)
                    nc.vector.tensor_tensor(strict[:, here], grams[:, :, 0], strict[:, here], ALU.mult)
                    nc.vector.tensor_tensor(upto[:, s, here], grams[:, :, 1], upto[:, s, here], ALU.mult).then_inc(gram_sb, 1)
                dve.drain()
                invert_start(core, dve, n, G, lambda g: four(strict, g), XT[:, s], *inverse)
                for lev in range(len(LEVELS)):
                    if before is not None and lev == 4:
                        new_state(*before)
                    invert_update(core, dve, n, G, lev, X, XT[:, s], W, *inverse)

            steps(dve, front, new_state)


def gdn_mixer(core, A):
    gdn_projections(core, A)
    gdn_gates(core, A)
    gdn_chunks(core)
    gdn_output(core)
    residual(core, 1, 0, A["gdn_w_out"].rearrange("o k n -> (o k) n"),
             (core.slot(0, KD, T), core.rounded_tiles(2), core.rounded_tiles(0)), 8)


Q_LORA, KV_LORA, NOPE, ROPE, HM = 384, 256, 128, 64, 4
KQ, KKV = Q_LORA // P, KV_LORA // P
LAT = Q_LORA + KV_LORA
REST = LAT + ROPE
GATES = REST + 4 * 256
RMS_EPS = 1e-6
CQ, CKV, KR, XP, XQK, XV, XO = 0, 3, 5, 6, 8, 10, 12
NPROJ = 14


def layer_projections(core, A, layer):
    nc = core.nc
    x, proj = core.x, core.slot(0, 16, T)
    w = A["w_in_2"][ds(layer, 1)].rearrange("o k n -> (o k) n")

    U = NPROJ // 2

    def feed(sp, ring, loaded, done):
        for j in range(NPROJ):
            if j >= U:
                sp.wait_ge(done, j + 1)
            to, into = ring[:, j % U], loaded[j % U]
            if j == KR:
                for half in range(2):
                    sp.dma_start(to[:, :, half * ROPE:(half + 1) * ROPE],
                                 w[:, LAT:REST].rearrange("(k p) m -> p k m", p=P)).then_inc(into, 16)
            else:
                sp.dma_start(to, w[:, (j * P if j < KR else REST + (j - XP) * P):][:, 0:P].rearrange(
                    "(k p) m -> p k m", p=P)).then_inc(into, 16)

    products(core, NPROJ, KD, None, (x, core.rounded_tiles(2), core.rounded_tiles(3)), 4,
             scalar=lambda act, j, banks, s, more: nc.scalar.copy(flat(proj[:, ds(j, 1)]), banks[0]), U=U, feed=feed, twice=(KR,))


def table(core, name):
    at, n = CONST_AT[name]
    return core.slot(3, KD * T)[:, 3 * T + at - CONST_KEPT:3 * T + at - CONST_KEPT + n]


def heads_and_pool(core, A, layer):
    nc = core.nc
    proj, spare = core.slot(0, 16, T), core.slot(0, 16, T)[:, NPROJ:]
    w = A["w_in_2"][ds(layer, 1)].rearrange("o k n -> (o k) n")
    wq, wkv = core.slot(4, KQ, HM * (NOPE + ROPE)), core.slot(5, KKV, HM * 2 * NOPE)
    v = core.slot(5, KD * T)[:, 2048:4096].rearrange("p (a n) -> p a n", a=4)
    qn, kn = core.slot(2, HM, T), core.slot(2, KD, T)[:, HM:2 * HM]
    qp, kp = core.slot(3, 2, T), core.slot(3, KD, T)[:, 2]
    tables = core.slot(3, KD * T)[:, 3 * T:3 * T + CONST.shape[1] - CONST_KEPT]
    sq = core.slot(9, 2, T)
    rstd = core.slot(9, KD, T)[:, 2:4]
    scale = float((NOPE + ROPE) ** -0.5)
    latents = ((CQ, KQ, "g_qn", 1.0 / Q_LORA), (CKV, KKV, "g_kvn", 1.0 / KV_LORA))
    out = core.slot(7, KD, T)
    sums = core.slot(9, KD, T)[:, 4:8]
    wg = core.slot(4, KD * T)[:, 2304:2304 + KD * 2 * HM].rearrange("p (k m) -> p k m", k=KD)
    weights = core.slot(4, KD * T)[:, 2432:2432 + 6 * 64].rearrange("p (w k m) -> p w k m", w=3, k=2)
    bias = core.total[0:HM, 0:2]
    conv, mq, mk = core.slot(8, 2, T), core.slot(8, KD, T)[:, 2:4], core.slot(8, KD, T)[:, 4:6]
    mv = core.slot(8, KD * T)[:, 6 * T:6 * T + 4 * 256].rearrange("p (a n) -> p a n", a=4)
    li, xf, soft, B, F, M, floor = (core.m_rows[:, i] for i in range(7))
    ones_row = core.slot(6, KD * T)[0:HM, 7 * T:8 * T]
    (gates_loaded, loaded, gates_ps, gates_out, squared, square_used, floored, rooted, normed, q_ps, q_out, kv_ps, kv_out,
     v_ps, v_out, turned, turned_used, rotated, convolved, activated, pooled, p_ps, qk_ps, qk_out, mv_ps, mv_out,
     soft_done, rows_done, floor_done, cols_ps) = core.semaphores(
        "gates_loaded", "loaded", "gates_ps", "gates_out", "squared", "square_used", "floored", "rooted", "normed", "q_ps",
        "q_out", "kv_ps", "kv_out", "v_ps", "v_out", "turned", "turned_used", "rotated", "convolved", "activated", "pooled",
        "p_ps", "qk_ps", "qk_out", "mv_ps", "mv_out", "soft_done", "rows_done", "floor_done", "cols_ps")
    with nc.Block() as block:
        @block.sync
        def _(sp):
            core.clear_before(sp)
            sp.dma_start(wg, w[:, GATES:GATES + 2 * HM].rearrange("(k p) m -> p k m", p=P)).then_inc(gates_loaded, 16)
            for n, name in enumerate(("b_i_2", "b_f_2")):
                sp.dma_start(bias[:, n:n + 1], A[name][ds(layer, 1)].rearrange("o h -> h o")).then_inc(gates_loaded, 16)
            sp.dma_start(wq, A["w_uq_2"][ds(layer, 1)].rearrange("o (k p) n -> p (o k) n", p=P)).then_inc(loaded, 16)
            sp.dma_start(wkv, A["w_ukv_2"][ds(layer, 1)].rearrange("o (k p) n -> p (o k) n", p=P)).then_inc(loaded, 16)
            sp.dma_start(tables, core.const_dram[:, CONST_KEPT:CONST.shape[1]]).then_inc(loaded, 16)
            for i, name in enumerate(("w_pool_2", "w_mq_2", "w_mk_2")):
                for lo in range(2):
                    for t in range(2):
                        sp.dma_start(weights[64 * lo:64 * lo + 64, i, t],
                                     A[name][ds(layer, 1), 2 * t + lo].rearrange("o c m -> (o c) m")).then_inc(loaded, 16)

        @block.scalar
        def _(act):
            n = 0
            for first, kt, g, mean in latents:
                for k in range(kt):
                    if n >= 2:
                        act.wait_ge(square_used, n - 1)
                    nc.scalar.activation(sq[:, n % 2], proj[:, first + k], ACT.Square).then_inc(squared, 1)
                    n += 1
            for i in range(2):
                act.wait_ge(floored, i + 1)
                nc.scalar.activation(rstd[:, i], rstd[:, i], ACT.Sqrt).then_inc(rooted, 1)
            act.wait_ge(gates_out, 1)
            nc.scalar.activation(soft, xf, ACT.Abs)
            act.drain()
            nc.scalar.activation(soft, soft, ACT.Exp, scale=-1.0)
            act.drain()
            nc.scalar.activation(soft, soft, ACT.Ln, bias=1.0).then_inc(soft_done, 1)
            for h in range(HM):
                act.wait_ge(q_ps, h + 1)
                nc.scalar.mul(qn[:, h], core.ps[:, 2 + h % 2], scale).then_inc(q_out, 1)
            for j in range(2):
                act.wait_ge(q_ps, HM + j + 1)
                nc.scalar.mul(qp[:, j], core.ps[:, 2 + j], scale).then_inc(q_out, 1)
            for t in range(2):
                act.wait_ge(convolved, t + 1)
                nc.scalar.activation(conv[:, t], conv[:, t], ACT.Silu, bias=core.col("b_mconv", t)).then_inc(activated, 1)
            for h in range(HM):
                act.wait_ge(kv_ps, h + 1)
                nc.scalar.copy(kn[:, h], core.ps[:, 4 + h % 2]).then_inc(kv_out, 1)
            for a in range(4):
                act.wait_ge(v_ps, a + 1)
                nc.scalar.copy(v[:, a], core.ps[:, 6 + a % 2]).then_inc(v_out, 1)
            for t in range(2):
                act.wait_ge(qk_ps, t + 1)
                nc.scalar.copy(mq[:, t], core.ps[:, 2 + t])
                nc.scalar.mul(mk[:, t], core.ps[:, 4 + t], 64.0 ** -0.5).then_inc(qk_out, 1)
            for a in range(2):
                act.wait_ge(mv_ps, a + 1)
                nc.scalar.copy(mv[:, 2 * a:2 * a + 2].rearrange("p a n -> p (a n)"), core.ps[:, 6 + a])
            act.wait_ge(rows_done, 1)
            nc.scalar.activation(floor, floor, ACT.Exp, scale=-1.0).then_inc(floor_done, 1)

        @block.tensor
        def _(pe):
            pe.wait_ge(gates_loaded, 48)
            for q in range(2):
                for k in range(KD):
                    last = nc.tensor.matmul(core.ps[0:HM, 2 + q], wg[:, k, q * HM:(q + 1) * HM], core.x[:, k],
                                            start=k == 0, stop=k == KD - 1)
            last.then_inc(gates_ps, 1)
            n = 0
            for i, (first, kt, g, mean) in enumerate(latents):
                for k in range(kt):
                    pe.wait_ge(squared, n + 1)
                    nc.tensor.matmul(core.ps[:, i], core.const("ones"), sq[:, n % 2], start=k == 0,
                                     stop=k == kt - 1).then_inc(square_used, 1)
                    n += 1
            pe.wait_ge(loaded, 16 * 15)
            pe.wait_ge(gates_out, 1)
            pe.wait_ge(normed, KQ)
            for h in range(HM):
                if h >= 2:
                    pe.wait_ge(q_out, h - 1)
                for k in range(KQ):
                    last = nc.tensor.matmul(core.ps[:, 2 + h % 2], wq[:, k, h * (NOPE + ROPE):h * (NOPE + ROPE) + NOPE],
                                            proj[:, CQ + k], start=k == 0, stop=k == KQ - 1)
                last.then_inc(q_ps, 1)
            for j in range(2):
                pe.wait_ge(q_out, HM - 1 + j)
                for half in range(2):
                    at = (2 * j + half) * (NOPE + ROPE) + NOPE
                    for k in range(KQ):
                        last = nc.tensor.matmul(core.ps[half * ROPE:(half + 1) * ROPE, 2 + j], wq[:, k, at:at + ROPE],
                                                proj[:, CQ + k], start=k == 0, stop=k == KQ - 1)
                last.then_inc(q_ps, 1)
            pe.wait_ge(normed, KQ + KKV)
            for h in range(HM):
                if h >= 2:
                    pe.wait_ge(kv_out, h - 1)
                for k in range(KKV):
                    last = nc.tensor.matmul(core.ps[:, 4 + h % 2], wkv[:, k, h * 2 * NOPE:h * 2 * NOPE + NOPE],
                                            proj[:, CKV + k], start=k == 0, stop=k == KKV - 1)
                last.then_inc(kv_ps, 1)
            for i, t in enumerate((qp[:, 0], qp[:, 1], proj[:, KR])):
                if i < 2:
                    pe.wait_ge(q_out, HM + i + 1)
                else:
                    pe.wait_ge(turned_used, 1)
                nc.tensor.matmul(core.ps[:, i % 2], table(core, "turn"), t, start=True, stop=True).then_inc(turned, 1)
            values = wkv.rearrange("p k (h m) -> p k h m", h=HM)
            for a in range(4):
                if a >= 2:
                    pe.wait_ge(v_out, a - 1)
                for k in range(KKV):
                    last = nc.tensor.matmul(core.ps[:, 6 + a % 2], proj[:, CKV + k, a * P:(a + 1) * P],
                                            values[:, k, :, NOPE:2 * NOPE], start=k == 0, stop=k == KKV - 1)
                last.then_inc(v_ps, 1)
            pe.wait_ge(q_out, HM + 2)
            pe.wait_ge(kv_out, HM)
            for t in range(2):
                pe.wait_ge(activated, t + 1)
                for i in (1, 2):
                    for lo in (0, 64):
                        last = nc.tensor.matmul(core.ps[lo:lo + 64, 2 * i + t], weights[lo:lo + 64, i, t],
                                                conv[lo:lo + 64, t], start=True, stop=True)
                last.then_inc(qk_ps, 1)
            for a in range(4):
                pe.wait_ge(v_out, 3 + a // 2)
                for t in range(2):
                    at = (a % 2) * 256 + t * P
                    last = nc.tensor.transpose(core.ps[:, 6 + a // 2, at:at + P], proj[:, XV + t, a * P:(a + 1) * P],
                                               core.const("ident"))
                if a % 2:
                    last.then_inc(mv_ps, 1)
            pe.wait_ge(rows_done, 1)
            pe.wait_ge(qk_out, 2)
            for a in range(4):
                last = nc.tensor.transpose(core.ps[:, 2, a * HM:(a + 1) * HM], F[:, a * P:(a + 1) * P],
                                           core.const("ident", HM)[:, 0:HM])
            last.then_inc(cols_ps, 1)
            for t in range(2):
                pe.wait_ge(pooled, t + 1)
                for lo in (0, 64):
                    last = nc.tensor.matmul(core.ps[lo:lo + 64, 4 + t], weights[lo:lo + 64, 0, t],
                                            proj[lo:lo + 64, XP + t], start=True, stop=True)
                last.then_inc(p_ps, 1)

        @block.vector
        def _(dve):
            for t in range(2):
                tap = lambda j: core.col("w_mconv", j * 2 + t)
                causal_conv(nc, dve, conv[:, t], proj[:, XQK + t], tap, TAPS).then_inc(convolved, 1)
            dve.wait_ge(gates_loaded, 48)
            dve.wait_ge(gates_ps, 1)
            nc.vector.tensor_scalar(li, core.ps[0:HM, 2], bias[:, 0:1], None, ALU.add)
            nc.vector.tensor_scalar(xf, core.ps[0:HM, 3], bias[:, 1:2], None, ALU.add).then_inc(gates_out, 1)
            n = 0
            for i, (first, kt, g, mean) in enumerate(latents):
                n += kt
                dve.wait_ge(square_used, n)
                nc.vector.tensor_scalar(rstd[:, i], core.ps[:, i], mean, RMS_EPS, ALU.mult, ALU.add).then_inc(floored, 1)
            for i, (first, kt, g, mean) in enumerate(latents):
                dve.wait_ge(rooted, i + 1)
                nc.vector.reciprocal(rstd[:, i], rstd[:, i])
                dve.drain()
                for k in range(kt):
                    nc.vector.scalar_tensor_tensor(proj[:, first + k], proj[:, first + k], core.col(g, k), rstd[:, i],
                                                   ALU.mult, ALU.mult).then_inc(normed, 1)
            nc.vector.memset(ones_row, 1.0)
            nc.vector.tensor_scalar(F, xf, 0.0, None, ALU.min)
            dve.wait_ge(soft_done, 1)
            dve.drain()
            nc.vector.tensor_tensor(xf, F, soft, ALU.subtract)
            dve.drain()
            nc.vector.tensor_tensor_scan(B, ones_row, xf, 0.0, ALU.mult, ALU.add)
            dve.drain()
            nc.vector.tensor_tensor(F, li, B, ALU.subtract)
            dve.drain()
            nc.vector.tensor_tensor_scan(M, F, F, 0.0, ALU.max, ALU.max)
            dve.drain()
            nc.vector.tensor_tensor(floor, B, M, ALU.add).then_inc(rows_done, 1)
            dve.wait_ge(loaded, 16 * 15)
            for t in range(2):
                x = proj[:, XP + t]
                src = x
                at = 0
                for step in range(2 * t + 2):
                    lo = 64 if step == 2 * t + 1 else 0
                    dst, shift = sums[:, at % 4], 1 << step
                    if lo:
                        nc.vector.tensor_copy(dst[0:64], src[0:64])
                    nc.vector.tensor_copy(dst[lo:P, 0:shift], src[lo:P, 0:shift])
                    nc.vector.tensor_tensor(dst[lo:P, shift:T], src[lo:P, shift:T], src[lo:P, 0:T - shift], ALU.add)
                    dve.drain()
                    src = dst
                    at += 1
                nc.vector.tensor_tensor(src, src, table(core, f"count{t}"), ALU.mult)
                dve.drain()
                nc.vector.tensor_tensor(x, src, x, ALU.subtract).then_inc(pooled, 1)
                dve.drain()
            for i, (t, turned_out) in enumerate(((qp[:, 0], qp[:, 0]), (qp[:, 1], qp[:, 1]), (proj[:, KR], kp))):
                dve.wait_ge(turned, i + 1)
                nc.vector.tensor_tensor(spare[:, 0], core.ps[:, i % 2], table(core, "sin"), ALU.mult).then_inc(turned_used, 1)
                nc.vector.tensor_tensor(spare[:, 1], t, table(core, "cos"), ALU.mult)
                dve.drain()
                nc.vector.tensor_tensor(turned_out, spare[:, 0], spare[:, 1], ALU.add)
                dve.drain()
            dve.wait_ge(cols_ps, 1)
            nc.vector.tensor_copy(core.first[:, 0:4 * HM], core.ps[:, 2, 0:4 * HM])
            for t in range(2):
                dve.wait_ge(p_ps, t + 1)
                nc.vector.tensor_scalar(out[:, HM + t], core.ps[:, 4 + t], core.col("s_pool", t), None, ALU.mult)


def attentions(core):
    nc = core.nc
    proj, out = core.slot(0, 16, T), core.slot(7, KD, T)
    v = core.slot(5, KD * T)[:, 2048:4096].rearrange("p (a n) -> p a n", a=4)
    qn, kn = core.slot(2, HM, T), core.slot(2, KD, T)[:, HM:2 * HM]
    qp, kp = core.slot(3, 2, T), core.slot(3, KD, T)[:, 2]
    prob, prob_t = core.slot(9, KD, T)[:, 4:6], core.slot(9, KD, T)[:, 6:8]
    small = core.mid[:]
    mq, mk = core.slot(8, KD, T)[:, 2:4], core.slot(8, KD, T)[:, 4:6]
    mv = core.slot(8, KD * T)[:, 6 * T:6 * T + 4 * 256].rearrange("p (a n) -> p a n", a=4)
    M, floor, den = core.m_rows[:, 5], core.m_rows[:, 6], core.m_rows[:, 2]
    peaks = core.slot(9, HM, T)
    weight, gram = core.slot(4, 2, T), core.slot(4, KD, T)[:, 2:4]
    sq, rstd = core.slot(4, KD, T)[:, 4:6], core.slot(4, KD, T)[:, 6:8]
    items = [(h, a) for h in range(HM) for a in range(4)]
    (s_ps, peak, risen, weighed, t_ps, t_out, o_ps, o_out, m_peak_ps, m_peaks, m_s_ps, m_differ, m_risen, m_weighed, m_used,
     m_den_abs, m_den_done, m_den_ps, m_centred_ps, m_centred, m_squared, m_var_ps, m_floored, m_rooted,
     m_opened) = core.semaphores(
        "s_ps", "peak", "risen", "weighed", "t_ps", "t_out", "o_ps", "o_out", "m_peak_ps", "m_peaks", "m_s_ps", "m_differ",
        "m_risen", "m_weighed", "m_used", "m_den_abs", "m_den_done", "m_den_ps", "m_centred_ps", "m_centred", "m_squared",
        "m_var_ps", "m_floored", "m_rooted", "m_opened")
    with nc.Block() as block:
        @block.sync
        def _(sp):
            core.clear_before(sp)

        @block.tensor
        def _(pe):
            def scores(n):
                h, a = items[n]
                lo, end = 64 * (h % 2), (a + 1) * P
                if n >= 2:
                    pe.wait_ge(risen, n - 1)
                bank = core.ps[:, n % 2, 0:end]
                nc.tensor.matmul(bank, qn[:, h, a * P:end], kn[:, h, 0:end], start=True, stop=False)
                nc.tensor.matmul(bank, qp[lo:lo + 64, h // 2, a * P:end], kp[lo:lo + 64, 0:end], start=False,
                                 stop=True).then_inc(s_ps, 1)

            def turn(n):
                h, a = items[n]
                pe.wait_ge(weighed, n + 1)
                for b in range(a + 1):
                    last = nc.tensor.transpose(core.ps[:, 2, b * P:(b + 1) * P], prob[:, n % 2, b * P:(b + 1) * P],
                                               core.const("ident"))
                last.then_inc(t_ps, 1)

            def values(n):
                h, a = items[n]
                pe.wait_ge(t_out, n + 1)
                if n >= 1:
                    pe.wait_ge(o_out, n)
                for b in range(a + 1):
                    last = nc.tensor.matmul(core.ps[:, 3, 0:P], v[:, b, h * NOPE:(h + 1) * NOPE],
                                            prob_t[:, n % 2, b * P:(b + 1) * P], start=b == 0, stop=b == a)
                last.then_inc(o_ps, 1)

            def m_scores(n):
                h, a = items[n]
                lo = 64 * (h % 2)
                nc.tensor.matmul(core.ps[:, 4, a * P:T], mk[lo:lo + 64, h // 2, a * P:(a + 1) * P],
                                 mq[lo:lo + 64, h // 2, a * P:T], start=True, stop=True).then_inc(m_s_ps, 1)

            def m_values(n):
                h, a = items[n]
                lo = 64 * (h % 2)
                pe.wait_ge(m_weighed, n + 1)
                g = gram[:, n % 2, a * P:T]
                nc.tensor.matmul(core.ps[lo:lo + 64, 5 + h // 2, a * P:T], mv[:, a, h * 64:(h + 1) * 64], g,
                                 start=a == 0, stop=a == 3, skip_group_check=True)
                nc.tensor.matmul(core.ps[0:HM, 7, a * P:T], core.const("pick8")[:, HG - 1 - h:HG - 1 - h + HM], g,
                                 start=n == 0, stop=n == len(items) - 1, skip_group_check=True).then_inc(m_used, 1)

            for h in range(HM):
                nc.tensor.matmul(core.ps[:, 2 + h], core.const("spread8", HM)[:, h * P:(h + 1) * P], M,
                                 start=True, stop=True).then_inc(m_peak_ps, 1)
            scores(0)
            pe.wait_ge(m_peaks, HM)
            m_scores(0)
            for n in range(len(items)):
                if n + 1 < len(items):
                    scores(n + 1)
                turn(n)
                m_values(n)
                if n + 1 < len(items):
                    m_scores(n + 1)
                values(n)
            pe.wait_ge(m_den_done, 1)
            for t in range(2):
                nc.tensor.matmul(core.ps[:, t], core.const("spread16", HM)[:, t * P:(t + 1) * P], den, start=True,
                                 stop=True).then_inc(m_den_ps, 1)
            pe.wait_ge(o_out, len(items))
            for t in range(2):
                pe.wait_ge(m_den_abs, 2 + t)
                nc.tensor.matmul(core.ps[:, 2 + t], core.const("head64"), out[:, 6 + t], start=True,
                                 stop=True).then_inc(m_centred_ps, 1)
            for t in range(2):
                pe.wait_ge(m_squared, t + 1)
                nc.tensor.matmul(core.ps[:, 4 + 3 * t], core.const("head64"), sq[:, t], start=True,
                                 stop=True).then_inc(m_var_ps, 1)

        @block.vector
        def _(dve):
            def row(n, i):
                return small[:, 3 * (n % 2) + i:3 * (n % 2) + i + 1]

            def highest(n):
                h, a = items[n]
                end = (a + 1) * P
                bank = core.ps[:, n % 2]
                dve.wait_ge(s_ps, n + 1)
                nc.vector.tensor_tensor(bank[:, a * P:end], bank[:, a * P:end], table(core, "later"), ALU.add)
                dve.drain()
                nc.vector.tensor_reduce(row(n, 0), bank[:, 0:end], AX_X, ALU.max, negate=True).then_inc(peak, 1)

            def scale(n):
                end = (items[n][1] + 1) * P
                dve.wait_ge(risen, n + 1)
                nc.vector.reciprocal(row(n, 2), row(n, 1))
                dve.drain()
                nc.vector.tensor_scalar(prob[:, n % 2, 0:end], prob[:, n % 2, 0:end], row(n, 2), None,
                                        ALU.mult).then_inc(weighed, 1)

            def m_exponents(n):
                h, a = items[n]
                nc.vector.tensor_scalar(weight[:, n % 2, a * P:T], peaks[:, h, a * P:T], core.first[:, a * HM + h:a * HM + h + 1],
                                        0.0, ALU.subtract, ALU.max).then_inc(m_differ, 1)

            def m_weigh(n):
                h, a = items[n]
                dve.wait_ge(m_risen, n + 1)
                w, g = weight[:, n % 2], gram[:, n % 2]
                nc.vector.tensor_tensor(w[:, a * P:(a + 1) * P], w[:, a * P:(a + 1) * P], core.const("upto"), ALU.mult)
                dve.drain()
                dve.wait_ge(m_s_ps, n + 1)
                if n >= 2:
                    dve.wait_ge(m_used, n - 1)
                nc.vector.tensor_tensor(g[:, a * P:T], core.ps[:, 4, a * P:T], w[:, a * P:T],
                                        ALU.mult).then_inc(m_weighed, 1)

            highest(0)
            dve.wait_ge(m_peaks, HM)
            m_exponents(0)
            for n in range(len(items)):
                scale(n)
                m_weigh(n)
                if n + 1 < len(items):
                    highest(n + 1)
                    m_exponents(n + 1)
            dve.wait_ge(m_den_abs, 1)
            nc.vector.tensor_tensor(den, den, floor, ALU.max)
            dve.drain()
            nc.vector.reciprocal(den, den).then_inc(m_den_done, 1)
            for t in range(2):
                dve.wait_ge(m_den_ps, t + 1)
                nc.vector.tensor_copy(rstd[:, t], core.ps[:, t])
                dve.drain()
                nc.vector.tensor_tensor(out[:, 6 + t], core.ps[:, 5 + t], rstd[:, t], ALU.mult).then_inc(m_den_abs, 1)
            for t in range(2):
                dve.wait_ge(m_centred_ps, t + 1)
                dve.drain()
                nc.vector.scalar_tensor_tensor(out[:, 6 + t], core.ps[:, 2 + t], -1.0 / 64, out[:, 6 + t], ALU.mult,
                                               ALU.add).then_inc(m_centred, 1)
            for t in range(2):
                dve.wait_ge(m_var_ps, t + 1)
                nc.vector.tensor_scalar(rstd[:, t], core.ps[:, 4 + 3 * t], 1.0 / 64, LN_EPS, ALU.mult,
                                        ALU.add).then_inc(m_floored, 1)
            for t in range(2):
                dve.wait_ge(m_rooted, t + 1)
                nc.vector.reciprocal(rstd[:, t], rstd[:, t])
                dve.drain()
                nc.vector.scalar_tensor_tensor(out[:, 6 + t], out[:, 6 + t], core.col("g_mh", t), rstd[:, t], ALU.mult,
                                               ALU.mult)
                dve.drain()
                dve.wait_ge(m_opened, t + 1)
                nc.vector.tensor_tensor(out[:, 6 + t], out[:, 6 + t], proj[:, XO + t], ALU.mult)

        @block.scalar
        def _(act):
            def rise(n):
                end = (items[n][1] + 1) * P
                top, total = (small[:, 3 * (n % 2) + i:3 * (n % 2) + i + 1] for i in range(2))
                act.wait_ge(peak, n + 1)
                nc.scalar.activation(prob[:, n % 2, 0:end], core.ps[:, n % 2, 0:end], ACT.Exp, bias=top,
                                     accum_out=total).then_inc(risen, 1)

            def m_rise(n):
                a = items[n][1]
                act.wait_ge(m_differ, n + 1)
                nc.scalar.activation(weight[:, n % 2, a * P:T], weight[:, n % 2, a * P:T], ACT.Exp,
                                     scale=-1.0).then_inc(m_risen, 1)

            for t in range(2):
                nc.scalar.activation(proj[:, XO + t], proj[:, XO + t], ACT.Sigmoid).then_inc(m_opened, 1)
            for h in range(HM):
                act.wait_ge(m_peak_ps, h + 1)
                nc.scalar.copy(peaks[:, h], core.ps[:, 2 + h]).then_inc(m_peaks, 1)
            rise(0)
            m_rise(0)
            for n, (h, a) in enumerate(items):
                end = (a + 1) * P
                act.wait_ge(t_ps, n + 1)
                nc.scalar.copy(prob_t[:, n % 2, 0:end], core.ps[:, 2, 0:end]).then_inc(t_out, 1)
                if n + 1 < len(items):
                    rise(n + 1)
                    m_rise(n + 1)
                act.wait_ge(o_ps, n + 1)
                nc.scalar.copy(out[:, h, a * P:end], core.ps[:, 3, 0:P]).then_inc(o_out, 1)
            act.wait_ge(m_used, len(items))
            nc.scalar.activation(den, core.ps[0:HM, 7], ACT.Abs).then_inc(m_den_abs, 1)
            for t in range(2):
                act.wait_ge(m_centred, t + 1)
                nc.scalar.activation(sq[:, t], out[:, 6 + t], ACT.Square).then_inc(m_squared, 1)
            for t in range(2):
                act.wait_ge(m_floored, t + 1)
                nc.scalar.activation(rstd[:, t], rstd[:, t], ACT.Sqrt).then_inc(m_rooted, 1)


def store_output(core, out):
    nc = core.nc
    rows = core.slot(0, 4, D)
    turned, copied, stored = core.semaphores("turned", "copied", "stored")
    with nc.Block() as block:
        @block.sync
        def _(sp):
            core.clear_before(sp)
            for a in range(4):
                sp.wait_ge(copied, 2 * (a + 1))
                sp.dma_start(out[0, a * P:(a + 1) * P, :], rows[:, a]).then_inc(stored, 16)
            sp.wait_ge(stored, 64)

        @block.tensor
        def _(pe):
            for a in range(4):
                for half in range(2):
                    n = 2 * a + half
                    if n >= 4:
                        pe.wait_ge(copied, n - 3)
                    for j in range(4):
                        last = nc.tensor.transpose(core.ps[:, n % 4, j * P:(j + 1) * P],
                                                   core.x[:, 4 * half + j, a * P:(a + 1) * P], core.const("ident"))
                    last.then_inc(turned, 1)

        @block.vector
        def _(dve):
            for n in range(8):
                dve.wait_ge(turned, n + 1)
                nc.vector.tensor_copy(rows[:, n // 2, (n % 2) * 512:(n % 2 + 1) * 512], core.ps[:, n % 4]).then_inc(copied, 1)


def network(nc, A, const, out, stop=None):
    with ExitStack() as ctx:
        core = Core(nc, ctx, const)
        core.lora_inner = core.sb("lora_inner", [P, 3, T])
        core.mid, core.first, core.ends = (core.sb(n, [P, KD * NC]) for n in ("mid", "first", "ends"))
        core.bonus = core.sb("bonus", [HR, T])
        core.gate_rows = core.slot(9, KD, T)[0:HG, 4:8]
        core.gate_cols, core.norm_cols, core.total = core.first, core.ends, core.mid
        core.norm_rows = core.lora_inner[0:HG]
        core.one_less_k_a = core.sb("one_less_k_a", [P, KD])

        def rows(ap, pattern, **sizes):
            return ap.rearrange(pattern, **sizes)

        def vec(name, layer=0):
            return A[name][layer:layer + 1].rearrange("o (r p) -> (o r) p", p=P)

        groups = [
            [("ada_b0", vec("ada_b", 0))] +
            [(f"ln_g{i}{j}", A["ln_g"][i, j:j + 1].rearrange("o (r p) -> (o r) p", p=P)) for i in range(2) for j in range(2)] +
            [(f"ln_b{i}{j}", A["ln_b"][i, j:j + 1].rearrange("o (r p) -> (o r) p", p=P)) for i in range(2) for j in range(2)] +
            [("c", vec("c"))],
            [("ada_b1", vec("ada_b", 1)), ("mu", A["rwkv_mu"].rearrange("o i (r p) -> (o i r) p", p=P))] +
            [(n, vec("rwkv_" + n)) for n in ("w0", "a0", "k_k", "k_a")],
            [("r_k", A["rwkv_r_k"].rearrange("o (r a) n -> (o r) (a n)", a=2))] +
            [(n, vec("rwkv_" + n)) for n in ("gn_g", "gn_b")] +
            [("conv", A["gdn_conv"].rearrange("o i (r p) -> (o i r) p", p=P)), ("norm_g", A["gdn_norm_g"])],
            [("ln0_g", A["ln0_g_2"].rearrange("(r p) -> r p", p=P)), ("ln0_b", A["ln0_b_2"].rearrange("(r p) -> r p", p=P))],
        ]
        at, n = CONST_AT["ident"]
        turn_rows(core, groups, after=early_loads(core, A), before=lambda sp, loaded: sp.dma_start(
            core.const_sb[:, at:at + n], const[:, at:at + n]).then_inc(loaded, 16))
        turn_x(core)
        modulation(core, 0, A["ada_w"], 4)
        one_less(core)
        rwkv_projections(core, A)
        rwkv_decays(core)
        rwkv_chunks(core)
        rwkv_output(core, A)
        
        feed_forward(core, 0, ("ln_g00", "ln_b00"), A["ffn_w_in"][0], A["ffn_w_out"][0],
                     ride=Ride(core, 1, A["ada_w"], 0, 384, 8, 2, 3.5))
        gdn_mixer(core, A)
        feed_forward(core, 1, ("ln_g10", "ln_b10"), A["ffn_w_in"][1], A["ffn_w_out"][1])
        layer_norm(core, "ln_g11", "ln_b11")

        layer_norm(core, "ln0_g", "ln0_b", summed=False)
        core.m_rows = core.slot(6, KD, T)[0:HM]
        core.clear_all()
        with nc.Fori(0, 2) as layer:
            core.n_cols = 0

            def of_layer(name, pattern="o (r p) -> (o r) p"):
                return A[name + "_2"][ds(layer, 1)].rearrange(pattern, p=P)

            turn_rows(core, [
                [(n, of_layer(n)) for n in ("g_qn", "g_kvn", "s_pool", "b_mconv", "g_mh", "ln1_g", "ln1_b", "ln2_g", "ln2_b")] +
                [("w_mconv", of_layer("w_mconv", "o i (r p) -> (o i r) p"))],
                [("w_fconv", of_layer("w_fconv", "o i (r p) -> (o i r) p")), ("b_fconv", of_layer("b_fconv"))],
            ])
            layer_projections(core, A, layer)
            heads_and_pool(core, A, layer)
            attentions(core)
            mixed = core.slot(7, KD, T)
            residual(core, None, 0, flat_rows(A["w_out_2"], layer), (mixed, core.rounded_tiles(0), core.rounded_tiles(7)), 8)
            feed_forward(core, None, ("ln1_g", "ln1_b"), flat_rows(A["w_up_2"], layer), flat_rows(A["w_down_2"], layer), gate_first=False,
                         conv=(core.col_at["w_fconv"], core.col_at["b_fconv"], 3))
            layer_norm(core, "ln2_g", "ln2_b")
            core.clear_all()
        store_output(core, out)


def flat_rows(w, layer):
    return w[ds(layer, 1)].rearrange("o k n -> (o k) n")


def one_less(core):
    nc = core.nc
    core.semaphores()
    with nc.Block() as block:
        @block.sync
        def _(sp):
            core.clear_before(sp)

        @block.vector
        def _(dve):
            nc.vector.tensor_scalar(core.one_less_k_a[:], core.col("k_a", 0, KD), -1.0, 1.0, ALU.mult, ALU.add)


_OUTS = [((1, T, D), "float32")]


def kernel(**inputs):
    import concourse.bacc as _bacc
    from concourse.bass_utils import run_bass_kernel_spmd as _run

    nc = _bacc.Bacc("TRN2", target_bir_lowering=False, num_devices=1)
    arrays, A = {}, {}
    for name, value in inputs.items():
        if name.split("_")[0] in ("diff", "swa"):
            continue
        a = np.ascontiguousarray(value)
        arrays[f"in_{name}_dram"] = a
        A[name] = nc.dram_tensor(f"in_{name}_dram", a.shape, mybir.dt.from_np(a.dtype), kind="ExternalInput").ap()
    arrays["const_dram"] = CONST
    const = nc.dram_tensor("const_dram", CONST.shape, F32, kind="ExternalInput").ap()
    shape, dtype = _OUTS[0]
    out = nc.dram_tensor("out_0_dram", shape, mybir.dt.from_np(np.dtype(dtype)), kind="ExternalOutput").ap()
    network(nc, A, const, out)
    r = _run(nc, [arrays], core_ids=[0])
    return r.results[0]["out_0_dram"]
```
